# Optimizing a Trainium2 kernel written in Bass

```python
import functools
import jax, jax.numpy as jnp
from jax import lax
import numpy as np

'''One inference step of a hybrid bidirectional mLSTM / retention diffusion backbone (DEPTH layers).

Each layer: adaLN-modulated RMSNorm -> one combined input projection whose columns are split between
an mLSTM head group (4 heads x 128) and a retention head group (4 heads x 128); each group runs a
forward and a backward chunkwise scan (separate gate / decay parameters per direction), the two
directions are summed, head-normalised and gated, concatenated over head groups and sent through one
output projection -> residual; then adaLN-modulated RMSNorm -> SwiGLU (even layers) or top-2-of-8
SwiGLU experts (odd layers) -> residual. Final RMSNorm.
Context tokens are modulated by c_ctx and scan only context tokens (from zero state); latent tokens are
modulated by SiLU(c) and every latent scan starts from the cached final context state of its direction.

Inputs:
  x_prompt        (BATCH, SEQ, D_MODEL)       context tokens of new requests
  x_sample        (DEC_BATCH, DEC_SEQ, D_MODEL) noisy latent tokens (grid, GRID_W columns)
  state_mlstm_C   (DEC_BATCH, DEPTH, 2, H_M, DH_M, DH_M)  cached final context mLSTM matrix memory (fwd, bwd)
  state_mlstm_n   (DEC_BATCH, DEPTH, 2, H_M, DH_M)        cached normaliser state
  state_mlstm_m   (DEC_BATCH, DEPTH, 2, H_M)              cached running-max stabiliser
  state_ret_S     (DEC_BATCH, DEPTH, 2, H_R, DH_R, DH_R)  cached final context retention state
  c               (DEC_BATCH, D_MODEL)        conditioning vectors
  c_ctx           (D_MODEL,)                  learned context conditioning vector
  ... weights
Output tuple:
  (y_prompt (BATCH, SEQ, D_MODEL), y_sample (DEC_BATCH, DEC_SEQ, D_MODEL),
   new_mlstm_C (BATCH, DEPTH, 2, H_M, DH_M, DH_M), new_mlstm_n (BATCH, DEPTH, 2, H_M, DH_M),
   new_mlstm_m (BATCH, DEPTH, 2, H_M), new_ret_S (BATCH, DEPTH, 2, H_R, DH_R, DH_R))
'''

D_MODEL = 1024
BATCH = 1
SEQ = 128
DEPTH = 2
DEC_BATCH = 1
DEC_SEQ = 128
PAST_LEN = 128

GRID_W = 64
H_M = 4
DH_M = 128
H_R = 4
DH_R = 128
W_M = H_M * DH_M
W_R = H_R * DH_R
N_GATES = 4 * H_M
D_IN = 4 * W_M + N_GATES + 4 * W_R
SPLITS = [W_M, 2 * W_M, 3 * W_M, 4 * W_M, 4 * W_M + N_GATES,
          4 * W_M + N_GATES + W_R, 4 * W_M + N_GATES + 2 * W_R, 4 * W_M + N_GATES + 3 * W_R]
CHUNK = 128
D_FF = 2816
N_EXPERTS = 8
TOP_K = 2
N_DENSE = (DEPTH + 1) // 2
N_MOE = DEPTH // 2
ROPE_BASE = 10000.0
EPS = 1e-6

kernel_name = 'hybrid_mlstm_retention_diffusion_step'

def rmsnorm(x, g):
    xf = x.astype(jnp.float32)
    y = xf * lax.rsqrt(jnp.mean(xf * xf, -1, keepdims=True) + EPS)
    return (y * g.astype(jnp.float32)).astype(x.dtype)

def head_rmsnorm(h, g):
    H, d = h.shape[1], h.shape[3]
    y = h * lax.rsqrt(jnp.mean(h * h, -1, keepdims=True) + EPS)
    return y * g.astype(jnp.float32).reshape(H, 1, d)

def flip(a):
    return jnp.flip(a, axis=2)

def to_chunks(a):
    B, H, T = a.shape[:3]
    a = a.reshape((B, H, T // CHUNK, CHUNK) + a.shape[3:])
    return jnp.moveaxis(a, 2, 0)

def from_chunks(a):
    N, B, H, L = a.shape[:4]
    return jnp.moveaxis(a, 0, 2).reshape((B, H, N * L) + a.shape[4:])

def rope_1d(x, pos):
    half = x.shape[-1] // 2
    freqs = ROPE_BASE ** (-jnp.arange(half, dtype=jnp.float32) / half)
    ang = pos.astype(jnp.float32)[:, None] * freqs
    cos, sin = jnp.cos(ang), jnp.sin(ang)
    x1, x2 = x[..., :half], x[..., half:]
    return jnp.concatenate([x1 * cos - x2 * sin, x1 * sin + x2 * cos], -1)

def rope_2d(x, row, col):
    d = x.shape[-1] // 2
    return jnp.concatenate([rope_1d(x[..., :d], row), rope_1d(x[..., d:], col)], -1)

def mlstm_scan(q, k, v, i_pre, f_log, C0, n0, m0):
    causal = jnp.tril(jnp.ones((CHUNK, CHUNK), dtype=bool))

    def step(carry, xs):
        C, n, m = carry
        qc, kc, vc, ic, fc = xs
        b = jnp.cumsum(fc, axis=-1)
        logD = jnp.where(causal, b[..., :, None] - b[..., None, :] + ic[..., None, :], -jnp.inf)
        m_inter = b + m[..., None]
        m_row = jnp.maximum(m_inter, jnp.max(logD, -1))
        s = jnp.einsum('bhid,bhjd->bhij', qc, kc) * jnp.exp(logD - m_row[..., None])
        w_inter = jnp.exp(m_inter - m_row)
        num = jnp.einsum('bhij,bhjd->bhid', s, vc) + w_inter[..., None] * jnp.einsum('bhid,bhde->bhie', qc, C)
        den = jnp.sum(s, -1) + w_inter * jnp.einsum('bhid,bhd->bhi', qc, n)
        h = num / jnp.maximum(jnp.abs(den), jnp.exp(-m_row))[..., None]
        b_end = b[..., -1]
        log_w = b_end[..., None] - b + ic
        m_new = jnp.maximum(b_end + m, jnp.max(log_w, -1))
        decay = jnp.exp(b_end + m - m_new)
        wk = jnp.exp(log_w - m_new[..., None])[..., None] * kc
        C_new = decay[..., None, None] * C + jnp.einsum('bhjd,bhje->bhde', wk, vc)
        n_new = decay[..., None] * n + jnp.sum(wk, -2)
        return (C_new, n_new, m_new), h

    xs = tuple(to_chunks(a) for a in (q, k, v, i_pre, f_log))
    (C, n, m), h = lax.scan(step, (C0, n0, m0), xs)
    return from_chunks(h), C, n, m

def retention_scan(q, k, v, log_gamma, S0):
    L = CHUNK
    pos = jnp.arange(L, dtype=jnp.float32)
    lg = log_gamma[:, None]
    rel = pos[:, None] - pos[None, :]
    decay_mat = jnp.where(rel >= 0, jnp.exp(lg[..., None] * jnp.maximum(rel, 0.0)), 0.0)
    decay_q = jnp.exp(lg * (pos + 1.0))
    decay_k = jnp.exp(lg * (L - 1.0 - pos))
    decay_L = jnp.exp(log_gamma * L)

    def step(S, xs):
        qc, kc, vc = xs
        s = jnp.einsum('bhid,bhjd->bhij', qc, kc) * decay_mat
        o = jnp.einsum('bhij,bhjd->bhid', s, vc) + decay_q[..., None] * jnp.einsum('bhid,bhde->bhie', qc, S)
        S_new = decay_L[:, None, None] * S + jnp.einsum('bhjd,bhje->bhde', kc * decay_k[..., None], vc)
        return S_new, o

    S, o = lax.scan(step, S0, tuple(to_chunks(a) for a in (q, k, v)))
    return from_chunks(o), S

def mixer(h, st, pos, w_in, b_gates, decay_logit, norm_m, norm_r, w_out):
    B, T, _ = h.shape
    f32 = jnp.float32
    p = jnp.einsum('btd,de->bte', h, w_in).astype(f32)
    qm, km, vm, om, gts, qr, kr, vr, gr = jnp.split(p, SPLITS, axis=-1)

    def heads(a, n):
        return a.reshape(B, T, n, -1).transpose(0, 2, 1, 3)

    qm, km, vm, om = (heads(a, H_M) for a in (qm, km, vm, om))
    qr, kr, vr, gr = (heads(a, H_R) for a in (qr, kr, vr, gr))
    km = km * DH_M ** -0.5
    if pos is not None:
        qr = rope_2d(qr, pos[0], pos[1])
        kr = rope_2d(kr, pos[0], pos[1])
    kr = kr * DH_R ** -0.5
    g = (gts + b_gates.astype(f32)).reshape(B, T, 4, H_M).transpose(2, 0, 3, 1)
    i_fw, i_bw = g[0], g[1]
    f_fw, f_bw = jax.nn.log_sigmoid(g[2]), jax.nn.log_sigmoid(g[3])
    C0, n0, m0, S0 = (a.astype(f32) for a in st)

    hf, Cf, nf, mf = mlstm_scan(qm, km, vm, i_fw, f_fw, C0[:, 0], n0[:, 0], m0[:, 0])
    hb, Cb, nb, mb = mlstm_scan(flip(qm), flip(km), flip(vm), flip(i_bw), flip(f_bw),
                                C0[:, 1], n0[:, 1], m0[:, 1])
    y_m = jax.nn.sigmoid(om) * head_rmsnorm(hf + flip(hb), norm_m)

    log_gamma = jax.nn.log_sigmoid(decay_logit.astype(f32))
    of, Sf = retention_scan(qr, kr, vr, log_gamma[0], S0[:, 0])
    ob, Sb = retention_scan(flip(qr), flip(kr), flip(vr), log_gamma[1], S0[:, 1])
    y_r = jax.nn.silu(gr) * head_rmsnorm(of + flip(ob), norm_r)

    y = jnp.concatenate([y_m, y_r], axis=1).transpose(0, 2, 1, 3).reshape(B, T, W_M + W_R).astype(h.dtype)
    out = jnp.einsum('btd,de->bte', y, w_out)
    new_st = (jnp.stack([Cf, Cb], 1), jnp.stack([nf, nb], 1), jnp.stack([mf, mb], 1), jnp.stack([Sf, Sb], 1))
    return out, new_st

def swiglu(h, wg, wu, wd):
    a = jnp.einsum('btd,df->btf', h, wg)
    b = jnp.einsum('btd,df->btf', h, wu)
    return jnp.einsum('btf,fd->btd', jax.nn.silu(a) * b, wd)

def moe_swiglu(h, w_router, wg, wu, wd):
    logits = jnp.einsum('btd,de->bte', h, w_router).astype(jnp.float32)
    top_v, top_i = lax.top_k(logits, TOP_K)
    w = jax.nn.softmax(top_v, axis=-1)
    gate = jnp.sum(jax.nn.one_hot(top_i, N_EXPERTS, dtype=jnp.float32) * w[..., None], axis=-2)
    gate = gate.astype(h.dtype)
    y = jnp.zeros_like(h)
    for e in range(N_EXPERTS):
        y = y + gate[..., e:e + 1] * swiglu(h, wg[e], wu[e], wd[e])
    return y

def block(x, mod, st, pos, g1, g2, w_in, b_gates, decay_logit, norm_m, norm_r, w_out, ffn):
    shift1, scale1, gate1, shift2, scale2, gate2 = jnp.split(mod[:, None, :].astype(x.dtype), 6, axis=-1)
    h = rmsnorm(x, g1) * (1.0 + scale1) + shift1
    y, new_st = mixer(h, st, pos, w_in, b_gates, decay_logit, norm_m, norm_r, w_out)
    x = x + gate1 * y
    h = rmsnorm(x, g2) * (1.0 + scale2) + shift2
    x = x + gate2 * ffn(h)
    return x, new_st

def setup_inputs(seed: int = 0) -> dict:
    key = jax.random.key(seed)
    ks = jax.random.split(key, 32)
    nrm = jax.random.normal
    f32 = jnp.float32
    D = D_MODEL
    gam = 1.0 - np.exp(np.linspace(np.log(1.0 / 32), np.log(1.0 / 512), H_R))
    logit = np.log(gam / (1.0 - gam)).astype(np.float32)
    f_bias = jnp.asarray(np.linspace(3.0, 6.0, H_M), dtype=f32)
    b_gates = jnp.concatenate([
        0.1 * nrm(ks[10], (DEPTH, 2 * H_M), f32),
        jnp.tile(f_bias, 2)[None, :] + 0.1 * nrm(ks[11], (DEPTH, 2 * H_M), f32)], axis=-1)
    return {
        'x_prompt': nrm(ks[0], (BATCH, SEQ, D), f32),
        'x_sample': nrm(ks[1], (DEC_BATCH, DEC_SEQ, D), f32),
        'state_mlstm_C': 0.3 * nrm(ks[2], (DEC_BATCH, DEPTH, 2, H_M, DH_M, DH_M), f32),
        'state_mlstm_n': 0.3 * nrm(ks[3], (DEC_BATCH, DEPTH, 2, H_M, DH_M), f32),
        'state_mlstm_m': 0.5 * nrm(ks[4], (DEC_BATCH, DEPTH, 2, H_M), f32),
        'state_ret_S': nrm(ks[5], (DEC_BATCH, DEPTH, 2, H_R, DH_R, DH_R), f32),
        'c': nrm(ks[6], (DEC_BATCH, D), f32),
        'c_ctx': nrm(ks[7], (D,), f32),
        'norm1_g': 1.0 + 0.02 * nrm(ks[8], (DEPTH, D), f32),
        'norm2_g': 1.0 + 0.02 * nrm(ks[9], (DEPTH, D), f32),
        'norm_f_g': 1.0 + 0.02 * nrm(ks[12], (D,), f32),
        'w_ada': 0.5 * D ** -0.5 * nrm(ks[13], (DEPTH, D, 6 * D), f32),
        'b_ada': 0.02 * nrm(ks[14], (DEPTH, 6 * D), f32),
        'w_in': D ** -0.5 * nrm(ks[15], (DEPTH, D, D_IN), f32),
        'b_gates': b_gates,
        'ret_decay_logit': jnp.asarray(logit)[None, None, :] + 0.05 * nrm(ks[16], (DEPTH, 2, H_R), f32),
        'mlstm_norm_g': 1.0 + 0.02 * nrm(ks[17], (DEPTH, W_M), f32),
        'ret_norm_g': 1.0 + 0.02 * nrm(ks[18], (DEPTH, W_R), f32),
        'w_out': (W_M + W_R) ** -0.5 * nrm(ks[19], (DEPTH, W_M + W_R, D), f32),
        'ffn_w_gate': D ** -0.5 * nrm(ks[20], (N_DENSE, D, D_FF), f32),
        'ffn_w_up': D ** -0.5 * nrm(ks[21], (N_DENSE, D, D_FF), f32),
        'ffn_w_down': D_FF ** -0.5 * nrm(ks[22], (N_DENSE, D_FF, D), f32),
        'moe_w_router': D ** -0.5 * nrm(ks[23], (N_MOE, D, N_EXPERTS), f32),
        'moe_w_gate': D ** -0.5 * nrm(ks[24], (N_MOE, N_EXPERTS, D, D_FF), f32),
        'moe_w_up': D ** -0.5 * nrm(ks[25], (N_MOE, N_EXPERTS, D, D_FF), f32),
        'moe_w_down': D_FF ** -0.5 * nrm(ks[26], (N_MOE, N_EXPERTS, D_FF, D), f32),
    }

def reference(x_prompt, x_sample, state_mlstm_C, state_mlstm_n, state_mlstm_m, state_ret_S, c, c_ctx,
              norm1_g, norm2_g, norm_f_g, w_ada, b_ada, w_in, b_gates, ret_decay_logit,
              mlstm_norm_g, ret_norm_g, w_out, ffn_w_gate, ffn_w_up, ffn_w_down,
              moe_w_router, moe_w_gate, moe_w_up, moe_w_down):
    f32 = jnp.float32
    B_ctx = x_prompt.shape[0]
    T_lat = x_sample.shape[1]
    rows = T_lat // GRID_W
    row = jnp.repeat(jnp.arange(rows), GRID_W)
    col = jnp.broadcast_to(jnp.arange(GRID_W)[None, :], (rows, GRID_W)).reshape(-1)
    pos = (row, col)
    zero_st = (jnp.zeros((B_ctx, 2, H_M, DH_M, DH_M), f32), jnp.zeros((B_ctx, 2, H_M, DH_M), f32),
               jnp.zeros((B_ctx, 2, H_M), f32), jnp.zeros((B_ctx, 2, H_R, DH_R, DH_R), f32))
    xp, xs = x_prompt, x_sample
    new_C, new_n, new_m, new_S = [], [], [], []
    for l in range(DEPTH):
        j = l // 2
        if l % 2 == 0:
            ffn = functools.partial(swiglu, wg=ffn_w_gate[j], wu=ffn_w_up[j], wd=ffn_w_down[j])
        else:
            ffn = functools.partial(moe_swiglu, w_router=moe_w_router[j], wg=moe_w_gate[j],
                                    wu=moe_w_up[j], wd=moe_w_down[j])
        lw = (norm1_g[l], norm2_g[l], w_in[l], b_gates[l], ret_decay_logit[l],
              mlstm_norm_g[l], ret_norm_g[l], w_out[l])
        mod_ctx = jnp.einsum('d,de->e', jax.nn.silu(c_ctx), w_ada[l])[None, :] + b_ada[l][None, :]
        mod_lat = jnp.einsum('bd,de->be', jax.nn.silu(c), w_ada[l]) + b_ada[l][None, :]
        xp, st_ctx = block(xp, mod_ctx, zero_st, None, *lw, ffn)
        new_C.append(st_ctx[0]); new_n.append(st_ctx[1]); new_m.append(st_ctx[2]); new_S.append(st_ctx[3])
        cache_l = (state_mlstm_C[:, l], state_mlstm_n[:, l], state_mlstm_m[:, l], state_ret_S[:, l])
        xs, _ = block(xs, mod_lat, cache_l, pos, *lw, ffn)
    y_prompt = rmsnorm(xp, norm_f_g)
    y_sample = rmsnorm(xs, norm_f_g)
    new_mlstm_C = jnp.stack(new_C, axis=1)
    new_mlstm_n = jnp.stack(new_n, axis=1)
    new_mlstm_m = jnp.stack(new_m, axis=1)
    new_ret_S = jnp.stack(new_S, axis=1)
    return (y_prompt, y_sample, new_mlstm_C, new_mlstm_n, new_mlstm_m, new_ret_S)


_drawn_inputs = setup_inputs


def setup_inputs(seed=0):
    import zlib

    import numpy as np

    out = dict(_drawn_inputs(seed))
    spreads = {}
    factors = {'state_mlstm_n': 2.782,
     'state_mlstm_m': 2.734,
     'norm2_g': 3.425,
     'norm_f_g': 2.886,
     'mlstm_norm_g': 8.0,
     'ret_norm_g': 6.152}
    for name, (base, spread) in spreads.items():
        noise = np.random.default_rng([zlib.crc32(name.encode()), seed]).standard_normal(out[name].shape)
        drawn = base * np.exp(spread * noise) if base else spread * noise
        out[name] = __import__('jax').numpy.asarray(drawn.astype(out[name].dtype))
    for name, factor in factors.items():
        out[name] = (out[name] * factor).astype(out[name].dtype)
    return out
```

```python
from contextlib import ExitStack

import numpy as np
import concourse.bass as bass
from concourse import mybir

ALU = mybir.AluOpType
ACT = mybir.ActivationFunctionType
F32 = mybir.dt.float32
F32R = mybir.dt.float32r
BF16 = mybir.dt.bfloat16
I32 = mybir.dt.int32
U32 = mybir.dt.uint32
AX_X = mybir.AxisListType.X

P = 128
S = 2
D = 1024
KT = D // P
DEPTH = 2
H = 4
WH = H * P
GATES = 4 * H
D_IN = 8 * WH + GATES
QM, KM, VM, OM, GT, QR, KR, VR, GR = (0, WH, 2 * WH, 3 * WH, 4 * WH, 4 * WH + GATES, 5 * WH + GATES,
                                      6 * WH + GATES, 7 * WH + GATES)
F = 2816
FT = F // P
NE = 8
EPS = 1e-6
GRID_W = 64
SCALE = float(P) ** -0.5
BLK = 512
HALF = 1024
RAW = 8
RAW_MOE = 11
HLS = 3
UNITS_FFN = 33
HALVES_FFN = 66
LAG = 2
BIG = 1.0e30
MAX_JOBS = 16
T_AFTER = [11, 19, 27, 35, 41, 47]
GATE_END = [3, 11, 19, 27, 35, 41]
UP_END = [7, 15, 23, 31, 39, 43]
PT_AFTER, GATHER_AFTER = 51, 57

C_ID, C_TRIF, C_TRIB, C_RELP, C_RELM, C_ONES, C_IOTA = (P * n for n in range(7))
C_COS = 7 * P
C_SIN = C_COS + 64
C_POS = C_SIN + 64
C_ALL = C_POS + 4


def shape_constants():
    i = np.arange(P, dtype=np.float64)
    row, col = i[:, None], i[None, :]
    t = np.zeros((P, C_ALL), np.float32)
    t[:, C_ID:C_ID + P] = row == col
    t[:, C_TRIF:C_TRIF + P] = row <= col
    t[:, C_TRIB:C_TRIB + P] = row >= col
    t[:, C_RELP:C_RELP + P] = np.maximum(col - row, 0)
    t[:, C_RELM:C_RELM + P] = np.maximum(row - col, 0)
    t[:, C_ONES:C_ONES + P] = 1
    t[:, C_IOTA:C_IOTA + P] = col
    half = P // 4
    freqs = (np.float32(10000.0) ** (-np.arange(half, dtype=np.float32) / np.float32(half))).astype(np.float32)
    for a, pos in enumerate((np.arange(P) // GRID_W, np.arange(P) % GRID_W)):
        ang = (pos.astype(np.float32)[:, None] * freqs).astype(np.float64)
        t[:, C_COS + a * half:C_COS + (a + 1) * half] = np.cos(ang)
        t[:, C_SIN + a * half:C_SIN + (a + 1) * half] = np.sin(ang)
    t[:, C_POS + 0] = i + 1
    t[:, C_POS + 1] = P - i
    t[:, C_POS + 2] = P - 1 - i
    t[:, C_POS + 3] = i
    return t


class Stages:

    def __init__(self, sem, first, layer, last):
        self.sem = sem
        self.value = {(n, None): k + 1 for k, n in enumerate(first)}
        for l in range(DEPTH):
            base = len(self.value)
            self.value |= {(n, l): base + k + 1 for k, n in enumerate(layer(l))}
        base = len(self.value)
        self.value |= {(n, None): base + k + 1 for k, n in enumerate(last)}
        self.at = 0

    def done(self, ins, name, l=None):
        self.at += 1
        assert self.value[(name, l)] == self.at, (name, l, self.at)
        ins.then_inc(self.sem, 1)

    def wait(self, eng, name, l=None):
        eng.wait_ge(self.sem, self.value[(name, l)])


def static_units():
    units = []
    for l in range(DEPTH):
        units += [("ada", l, b, h, [HALF, HALF]) for b in range(6 * D // BLK) for h in range(2)]
        units += [("gates", l, 0, 0, [KT * GATES])]
        units += [("in", l, b, h, [HALF, HALF]) for b in range(8) for h in range(2)]
        units += [("out", l, b, h, [HALF, HALF]) for b in range(D // BLK) for h in range(2)]
        if l == 0:
            units += [("ffn", l, u, 0, [HALF, HALF]) for u in range(UNITS_FFN)]
    return units


def bass_hybrid_backbone(nc, a, o):
    ctx = ExitStack()
    with ctx:
        base = 16512

        def at(name, offset, shape, dt=F32):
            return nc.alloc_sbuf_tensor_at(name, shape, dt, offset=base + offset)

        def sem(name):
            return ctx.enter_context(nc.semaphore(name))

        raw = [at(f"raw{n}", 8192 * n, [P, 2 * HALF]) for n in range(RAW)]
        top = 8192 * RAW
        hi = [at(f"hi{n}", top + 4096 * n, [P, HALF], F32R) for n in range(HLS)]
        top += 4096 * HLS
        lo = [at(f"lo{n}", top + 4096 * n, [P, HALF], F32R) for n in range(HLS)]
        top += 4096 * HLS
        region = top
        p = at("p", region, [P, S, D_IN])
        r = region + 4 * S * D_IN
        ET = at("ET", r, [P, 2, H, P])
        ysq = at("ysq", r, [P, 2 * H, P])
        ST = at("ST", r + 4096, [P, 2, H, P])
        upd = at("upd", r + 4096, [P, 2, BLK])
        QT = at("QT", r + 8192, [P, H, P])
        KTt = at("KTt", r + 10240, [P, H, P])
        VW = at("VW", r + 12288, [P, 2, H, P])
        rope1 = at("rope1", r + 12288, [P, 2 * H, 2, 32])
        rope2 = at("rope2", r + 14336, [P, 2 * H, 2, 32])
        AR = at("AR", r + 12288, [2 * H, 2, P])
        CM = at("CM", r + 16384, [P, 2, H, P])
        SM = at("SM", r + 20480, [P, 2, H, P])
        DS = at("DS", r + 24576, [P, H, P])
        TR = at("TR", r + 26624, [P, H, P])
        STC = at("STC", r + 28672, [P, 2, H, P])
        region_size = 4 * S * D_IN + 32768
        rowsA = at("rowsA", region, [96, P])
        rowsB = at("rowsB", region + 512, [80, P])
        hTh_d = at("hTh_d", region, [P, FT, S, P], F32R)
        hTl_d = at("hTl_d", region + 4 * FT * S * P, [P, FT, S, P], F32R)
        silu_d = at("silu_d", region + 8 * FT * S * P, [P, S, BLK])
        act_d = at("act_d", region + 8 * FT * S * P + 4096, [P, S, BLK])
        m = region
        hTh_m = at("hTh_m", m, [P, FT, 1, P], F32R)
        hTl_m = at("hTl_m", m + 4 * FT * P, [P, FT, 1, P], F32R)
        m += 8 * FT * P
        nath = at("nath", m, [P, S, D], F32R)
        natl = at("natl", m + 8192, [P, S, D], F32R)
        m += 16384
        yh = at("yh", m, [P, D], F32R)
        yl = at("yl", m + 4096, [P, D], F32R)
        silu_m = at("silu_m", m + 8192, [P, 1, BLK])
        act_m = at("act_m", m + 10240, [P, 1, BLK])
        m += 12288
        P1 = at("P1", m, [P, S, P])
        P2 = at("P2", m + 1024, [P, S, P])
        Pr = at("Pr", m + 2048, [P, S, P], F32R)
        PT = at("PT", m + 3072, [P, S, P], F32R)
        m += 4096
        slot8 = at("slot8", m, [P, 2 * HALF])
        jt = at("jt", m + 8192, [1, MAX_JOBS, NE])
        jtf = at("jtf", m + 8704, [1, MAX_JOBS + 1])
        assert m + 8192 + 1024 <= region + region_size
        gfin = at("gfin", region, [P, D])
        yfin = at("yfin", region + 4096, [P, S, D])
        top = region + region_size
        x = at("x", top, [P, S, D])
        top += 8192
        XTh = [at("XTh0", top, [P, KT, P], F32R), at("XTh1", top + 8192, [P, KT, P], F32R)]
        XTl = [at("XTl0", top + 4096, [P, KT, P], F32R), at("XTl1", top + 12288, [P, KT, P], F32R)]
        slot10 = at("slot10", top + 8192, [P, 2 * HALF])
        top += 16384
        N1 = at("N1", top, [P, S, D])
        N2 = at("N2", top + 8192, [P, S, KT, P])
        slot9 = at("slot9", top + 8192, [P, 2 * HALF])
        top += 16384
        raw_moe = raw + [slot8, slot9, slot10]
        assert len(raw_moe) == RAW_MOE
        small_at = [top]

        def small(name, shape, dt=F32):
            n = int(np.prod(shape[1:])) * (2 if dt == BF16 else 4)
            t = at(name, small_at[0], shape, dt)
            small_at[0] += -(-n // 32) * 32
            return t

        cst = small("cst", [P, C_ALL])
        identb = small("identb", [P, P], BF16)
        negm = small("negm", [P, 2, P], BF16)
        adarow = small("adarow", [4, 2, BLK])
        modc = [small(f"modc{l}", [P, 48, S]) for l in range(DEPTH)]
        colsA = small("colsA", [P, 96])
        colsB = small("colsB", [P, 80])
        sel4 = small("sel4", [4, 2])
        cT = small("cT", [P, KT, 4], F32R)
        csil = small("csil", [P, 16])
        scol = small("scol", [P, KT, S])
        bg = small("bg", [P, DEPTH, GATES])
        retl = small("retl", [P, DEPTH, 2 * H])
        rlg = small("rlg", [P, DEPTH, 2 * H])
        rtmp = small("rtmp", [P, DEPTH, 2 * H])
        dqk = small("dqk", [P, DEPTH, 4, H])
        m0b = small("m0b", [P, DEPTH, 2, H])
        m0r = small("m0r", [2 * H, DEPTH, 2])
        wr = small("wr", [P, KT, NE])
        gt = small("gt", [P, S, GATES])
        nab = small("nab", [P, S, 2 * H])
        lp = small("lp", [P, S, 2 * H])
        FL = small("FL", [P, 2, S, H])
        Bc = small("Bc", [P, 2, S, H])
        Ac = small("Ac", [P, 2, S, H])
        Mc = small("Mc", [P, 2, S, H])
        yy = N2
        mrow = small("mrow", [P, 2, S, H])
        em = small("em", [P, 2, S, H])
        wi = small("wi", [P, 2, H])
        dm = small("dm", [P, 2, H])
        MR = small("MR", [2 * H, 2, P])
        nMR = small("nMR", [2 * H, 2, P])
        den = small("den", [P, 2, H])
        dent = small("dent", [P, 2, H])
        rden = small("rden", [P, 2, S, H])
        wrd = small("wrd", [P, 2, H])
        wn = small("wn", [P, 2, H])
        ncol = small("ncol", [P, 2 * H])
        nrow = small("nrow", [2 * H, P])
        ss = small("ss", [P, S, 8])
        ln_v = small("ln_v", [P, S, 8])
        rs = small("rs", [P, S, 8])
        rs2 = small("rs2", [P, S, 8])
        lg = small("lg", [P, S, NE])
        mx = small("mx", [P, S, 8])
        mi = small("mi", [P, S, 8], U32)
        mif = small("mif", [P, S, 2])
        M1 = small("M1", [P, S, NE])
        M2 = small("M2", [P, S, NE])
        MK = small("MK", [P, S, NE])
        nb = small("nb", [P, NE])
        st_i = small("st_i", [P, NE])
        slots = small("slots", [P, S, NE])
        stmp = small("stmp", [P, S, NE])
        keys = small("keys", [P, 2, S])
        wts = small("wts", [P, 2, S])
        jti = small("jti", [1, MAX_JOBS + 1], I32)
        gs = small("gs", [P, 1])
        assert base + small_at[0] <= 229368, base + small_at[0]

        ident = cst[:, C_ID:C_ID + P]
        trif = cst[:, C_TRIF:C_TRIF + P]
        trib = cst[:, C_TRIB:C_TRIB + P]
        ones = cst[:, C_ONES:C_ONES + P]
        iota = cst[:, C_IOTA:C_IOTA + P]

        pb = ctx.enter_context(nc.psum_tensor("pb", [P, 8, BLK], F32))

        def bank(n):
            return pb[:, n, :]

        def tiles(n):
            return pb[:, n, :].rearrange("p (t c) -> p t c", c=P)

        raw_ld = [sem(f"raw_ld{n}") for n in range(RAW)]
        moe_ld = [sem(f"moe_ld{n}") for n in range(RAW_MOE)]
        hi_done, lo_done, w_used = sem("hi_done"), sem("lo_done"), sem("w_used")
        small_ld, state_ld, gfin_ld = sem("small_ld"), sem("state_ld"), sem("gfin_ld")
        ada_rows, ada_tr, ada_cols = (sem(n) for n in ("ada_rows", "ada_tr", "ada_cols"))
        in_evA, in_evD = sem("in_evA"), sem("in_evD")
        ffn_silu, ffn_prod = sem("ffn_silu"), sem("ffn_prod")
        ffn_tr, ffn_hTh, ffn_hTl = (sem(n) for n in ("ffn_tr", "ffn_hTh", "ffn_hTl"))
        job_silu, job_prod = sem("job_silu"), sem("job_prod")
        job_tr, job_hTh, job_hTl = (sem(n) for n in ("job_tr", "job_hTh", "job_hTl"))
        sel_ready, ptr_mm, pt_ready = sem("sel_ready"), sem("ptr_mm"), sem("pt_ready")
        sel_step, key_step = sem("sel_step"), sem("key_step")
        gath_mm, xh_ready, xl_ready = sem("gath_mm"), sem("xh_ready"), sem("xl_ready")
        yh_ready, yl_ready, scat_mm, acc_done = sem("yh_ready"), sem("yl_ready"), sem("scat_mm"), sem("acc_done")
        dve_chain, act_chain = sem("dve_chain"), sem("act_chain")
        st_out, m_out, n_out, y_out = sem("st_out"), sem("m_out"), sem("n_out"), sem("y_out")

        pe_st = Stages(sem("pe_stage"), ["cols"], lambda l: [
            "xt1", "bcum", "arow", "mcol",
            "qk0", "mb0", "pqk0", "num0", "cst", "nst", "nrow", "qkr0", "pr0", "o0", "rst",
            "qk1", "mb1", "pqk1", "num1", "qkr1", "pr1", "o1", "gb1", "yt", "xt2",
            *(["gb2"] if l == 0 else ["router", "nat", "rank", "gb2"])], [])
        act_st = Stages(sem("act_stage"), ["csil", "rlp", "rdec"], lambda l: [
            "sq1", "rs1", "xh1", "gate_e", "dse", "em", "wi", "sig",
            "kt0", "et0", "stc", "ktr0", "rstc",
            "kt1", "et1", "ktr1", "gb1", "hrs", "yh", "sq2", "rs2",
            *(["xh2", "gb2"] if l == 0 else ["nath", "we", "gb2"])], ["sqf", "rsf"])
        dve_st = Stages(sem("dve_stage"), ["prep", "cs", "rnab", "rarg"], lambda l: [
            "mod1", "v1", "xn1", "h1", "xl1", "gates", "fl", "ba", "mr", "mc", "rope",
            "qt0", "st0", "vw", "y0", "nc", "nr", "qtr0", "str0", "vwr", "yr0",
            "qt1", "st1", "y1", "qtr1", "str1", "yr1", "hv", "yn", "yl", "x1",
            "mod2", "v2", "xn2", "h2",
            *(["xl2", "x2"] if l == 0 else ["natl", "top", "masks", "route", "x2"])], ["vf", "yf"])

        units = static_units()
        n_static_halves = sum(len(u[-1]) for u in units)
        halves = []
        for n, u in enumerate(units):
            for k, size in enumerate(u[-1]):
                halves.append((n, k * HALF, size))
        halves_before = [sum(len(u[-1]) for u in units[:n]) for n in range(len(units) + 1)]

        def through(kind, l, b):
            return halves_before[1 + max(n for n, u in enumerate(units) if u[:3] == (kind, l, b))]

        ffn_first = halves_before[min(n for n, u in enumerate(units) if u[0] == "ffn")]

        def ffn_source(gate, up, down, u):
            if u < 22:
                j, part = (u // 4, u % 4) if u < 20 else (5, 2 * (u - 20))
                w, k0 = (gate, up)[part // 2], 4 * (part % 2)
                if j < 5:
                    return w.rearrange("(k p) n -> p k n", p=P)[:, k0:k0 + 4, j * BLK:(j + 1) * BLK]
                return w.rearrange("(k p) n -> p k n", p=P)[:, :, 5 * BLK:F]
            t = 2 * (u - 22)
            return down.rearrange("(t p) n -> p t n", p=P)[:, t:t + 2, :]

        def source(unit):
            kind, l, b, h, _ = unit
            if kind == "ada":
                return a["w_ada"][l].rearrange("(k p) n -> p k n", p=P)[:, 4 * h:4 * h + 4, b * BLK:(b + 1) * BLK]
            if kind == "gates":
                return a["w_in"][l].rearrange("(k p) n -> p k n", p=P)[:, :, GT:GT + GATES]
            if kind == "in":
                c = b * BLK + (GATES if b >= 4 else 0)
                return a["w_in"][l].rearrange("(k p) n -> p k n", p=P)[:, 4 * h:4 * h + 4, c:c + BLK]
            if kind == "out":
                return a["w_out"][l].rearrange("(k p) n -> p k n", p=P)[:, 4 * h:4 * h + 4, b * BLK:(b + 1) * BLK]
            return ffn_source(a["ffn_w_gate"][0], a["ffn_w_up"][0], a["ffn_w_down"][0], b)

        def unit_view(slot, size, cols):
            return slot[:, 0:size].rearrange("p (k n) -> p k n", n=cols)

        block = ctx.enter_context(nc.Block())

        @block.sync
        def _(sp):
            loads = [
                (cst[:, :], a["consts"]),
                (rowsA[:, :], a["b_ada"].rearrange("l (r p) -> (l r) p", p=P)),
                (rowsB[0:8, :], a["c_ctx"].rearrange("(r p) -> r p", p=P)),
                (rowsB[8:16, :], a["c"].rearrange("b (r p) -> (b r) p", p=P)),
                (rowsB[16:32, :], a["norm1_g"].rearrange("l (r p) -> (l r) p", p=P)),
                (rowsB[32:48, :], a["norm2_g"].rearrange("l (r p) -> (l r) p", p=P)),
                (rowsB[48:56, :], a["mlstm_norm_g"].rearrange("l (r p) -> (l r) p", p=P)),
                (rowsB[56:64, :], a["ret_norm_g"].rearrange("l (r p) -> (l r) p", p=P)),
                (rowsB[64:80, :], a["state_mlstm_n"].rearrange("b l d h p -> (b l d h) p")),
                (x[:, 0, :], a["x_prompt"][0]),
                (x[:, 1, :], a["x_sample"][0]),
                (bg[:, :, :], a["b_gates"].rearrange("(o l) g -> o l g", o=1).to_broadcast([P, DEPTH, GATES])),
                (retl[:, :, :], a["ret_decay_logit"].rearrange("(o l) d h -> o l (d h)", o=1)
                    .to_broadcast([P, DEPTH, 2 * H])),
                (m0b[:, :, :, :], a["state_mlstm_m"].to_broadcast([P, DEPTH, 2, H])),
                (wr[:, :, :], a["moe_w_router"][0].rearrange("(k p) e -> p k e", p=P)),
            ]
            for dst, src in loads:
                sp.dma_start(dst, src).then_inc(small_ld, 16)
            dve_st.wait(sp, "prep")
            for l in range(DEPTH):
                for d in range(2):
                    sp.dma_start(m0r[H:2 * H, l, d:d + 1], a["state_mlstm_m"][0, l, d].rearrange("(h o) -> h o", o=1))\
                        .then_inc(small_ld, 16)

            for n, unit in enumerate(units):
                if n >= RAW:
                    sp.wait_ge(lo_done, halves_before[n - RAW + 1])
                kind, l, b, h, sizes = unit
                cols = {"gates": GATES, "ffn": (BLK if b < 20 else F - 5 * BLK) if b < 22 else D}.get(kind, BLK)
                sp.dma_start(unit_view(raw[n % RAW], sum(sizes), cols), source(unit))\
                    .then_inc(raw_ld[n % RAW], 16)
                if kind == "gates":
                    if l > 0:
                        pe_st.wait(sp, "o1", l - 1)
                        dve_st.wait(sp, "x2", l - 1)
                    sp.dma_start(CM[:, :, :, :], a["state_mlstm_C"][0, l].rearrange("d h p e -> p d h e"))\
                        .then_inc(state_ld, 16)
                    sp.dma_start(SM[:, :, :, :], a["state_ret_S"][0, l].rearrange("d h p e -> p d h e"))\
                        .then_inc(state_ld, 16)

            def job(u, e):
                src = ffn_source(*(a[f"moe_w_{w}"][0][e] if isinstance(e, int) else
                                   a[f"moe_w_{w}"][0][bass.ds(e, 1)].rearrange("o r n -> (o r) n")
                                   for w in ("gate", "up", "down")), u)
                cols = (BLK if u < 20 else F - 5 * BLK) if u < 22 else D
                sp.dma_start(unit_view(raw_moe[u % RAW_MOE], 2 * HALF, cols), src)\
                    .then_inc(moe_ld[u % RAW_MOE], 16)

            for u in range(UNITS_FFN):
                if u < RAW:
                    last = max(n for n in range(len(units)) if n % RAW == u)
                    sp.wait_ge(lo_done, halves_before[last + 1])
                elif u < RAW_MOE:
                    if u == 8:
                        sp.wait_ge(st_out, 16 * 8)
                        dve_st.wait(sp, "x1", 1)
                    if u == 9:
                        act_st.wait(sp, "nath", 1)
                        dve_st.wait(sp, "natl", 1)
                        pe_st.wait(sp, "nat", 1)
                else:
                    sp.wait_ge(lo_done, n_static_halves + 2 * (u - RAW_MOE + 1))
                job(u, 0)
            dve_st.wait(sp, "route", 1)
            jobs = sp.value_load(jti[0:1, MAX_JOBS:MAX_JOBS + 1], min_val=NE, max_val=NE + 3)
            with sp.Fori(1, jobs) as i:
                e = sp.value_load(jti[0:1, bass.ds(i, 1)], min_val=0, max_val=NE - 1)
                for u in range(UNITS_FFN):
                    sp.wait_ge(lo_done, i * HALVES_FFN + (n_static_halves + 2 * (u - RAW_MOE + 1)))
                    job(u, e)
            pe_st.wait(sp, "gb2", 1)
            sp.dma_start(gfin[:, :], a["norm_f_g"].rearrange("(o n) -> o n", o=1).to_broadcast([P, D]))\
                .then_inc(gfin_ld, 16)
            dve_st.wait(sp, "yf")
            sp.dma_start(o["y_prompt"][0], yfin[:, 0, :]).then_inc(y_out, 16)
            sp.dma_start(o["y_sample"][0], yfin[:, 1, :]).then_inc(y_out, 16)
            sp.wait_ge(y_out, 32)
            sp.wait_ge(st_out, 16 * 8)
            sp.wait_ge(m_out, 16 * 4)
            sp.wait_ge(n_out, 16 * 2)

        @block.gpsimd
        def _(pool):
            for l in range(DEPTH):
                dve_st.wait(pool, "mc", l)
                pool.dma_start(o["new_m"][0, l, 0:1, :], mrow[P - 1:P, 0, 0, :]).then_inc(m_out, 16)
                pool.dma_start(o["new_m"][0, l, 1:2, :], mrow[0:1, 1, 0, :]).then_inc(m_out, 16)
                act_st.wait(pool, "stc", l)
                for d in range(2):
                    pool.dma_start(o["new_C"][0, l, d].rearrange("h p e -> p h e"), STC[:, d, :, :])\
                        .then_inc(st_out, 16)
                dve_st.wait(pool, "nr", l)
                pool.dma_start(o["new_n"][0, l].rearrange("d h p -> (d h) p"), nrow[:, :]).then_inc(n_out, 16)
                act_st.wait(pool, "rstc", l)
                for d in range(2):
                    pool.dma_start(o["new_S"][0, l, d].rearrange("h p e -> p h e"), STC[:, d, :, :])\
                        .then_inc(st_out, 16)

        @block.scalar
        def _(act):
            chain = [0]
            pos = [0]

            def link(ins):
                chain[0] += 1
                ins.then_inc(act_chain, 1)
                act.wait_ge(act_chain, chain[0])

            def copy(out, in_, scale=1.0):
                return nc.scalar.activation(out, in_, ACT.Copy, scale=scale)

            def split(n=1):
                for _ in range(n):
                    q = pos[0]
                    u, off, size = halves[q]
                    if off == 0:
                        act.wait_ge(raw_ld[u % RAW], 16 * (u // RAW + 1))
                    if q >= HLS:
                        act.wait_ge(w_used, q - HLS + 1)
                    copy(hi[q % HLS][:, 0:size], raw[u % RAW][:, off:off + size]).then_inc(hi_done, 1)
                    pos[0] += 1

            def rsqrt(src, n, name, l=None):
                link(nc.scalar.activation(ln_v[:, :, 0:n], src, ACT.Ln))
                act_st.done(nc.scalar.activation(rs[:, :, 0:n], ln_v[:, :, 0:n], ACT.Exp, scale=-0.5), name, l)

            def norm_sums(name, l=None):
                for s in range(S):
                    ins = nc.scalar.activation(N1[:, s, :], x[:, s, :], ACT.Square, accum_out=ss[:, s, 0:1])
                act_st.done(ins, name, l)

            def x_hi(k, l):
                dve_st.wait(act, f"h{k}", l)
                for s in range(S):
                    ins = copy(XTh[s][:, :, :], N2[:, s, :, :])
                act_st.done(ins, f"xh{k}", l)

            def gate_rows(name, l):
                pe_st.wait(act, name, l)
                for s in range(S):
                    for k in range(2):
                        ins = copy(N1[:, s, k * BLK:(k + 1) * BLK], bank(4 + 2 * s + k))
                act_st.done(ins, name, l)

            def ffn_act(split_half, ns, i, first, silu, hTh, sems):
                silu_sem, prod, tr, hTh_sem = sems

                def do_silu(j):
                    w = BLK if j < 5 else F - 5 * BLK
                    act.wait_ge(w_used, i * HALVES_FFN + (first + GATE_END[j] + 1))
                    for s in range(ns):
                        if not (isinstance(i, int) and j == 0):
                            act.wait_ge(prod, i * (6 * ns) + ns * j)
                        nc.scalar.activation(silu[:, s, 0:w], bank(2 * s)[:, 0:w], ACT.Silu)\
                            .then_inc(silu_sem, 1)

                def do_hT(j):
                    nt = 4 if j < 5 else 2
                    for s in range(ns):
                        act.wait_ge(tr, i * (6 * ns) + (ns * j + s + 1))
                        copy(hTh[:, 4 * j:4 * j + nt, s, :], tiles(4 + s)[:, 0:nt, :]).then_inc(hTh_sem, 1)

                for h in range(HALVES_FFN):
                    split_half(h)
                    for j in range(6):
                        if h == GATE_END[j] + LAG:
                            do_silu(j)
                    for j in range(6):
                        if h == T_AFTER[j] + LAG:
                            do_hT(j)

            pe_st.wait(act, "cols")
            act_st.done(nc.scalar.activation(csil[:, :], bank(5)[:, 0:16], ACT.Silu), "csil")
            dve_st.wait(act, "rnab")
            link(nc.scalar.activation(rtmp[:, :, :], rtmp[:, :, :], ACT.Exp))
            act_st.done(nc.scalar.activation(rtmp[:, :, :], rtmp[:, :, :], ACT.Ln, bias=1.0), "rlp")
            dve_st.wait(act, "rarg")
            act_st.done(nc.scalar.activation(dqk[:, :, :, :], dqk[:, :, :, :], ACT.Exp), "rdec")

            for l in range(DEPTH):
                def rows(b):
                    n = 12 * l + b
                    act.wait_ge(w_used, through("ada", l, b))
                    if n >= 2:
                        act.wait_ge(ada_tr, n - 1)
                    copy(adarow[:, b % 2, :], bank(b % 2)[0:4, :]).then_inc(ada_rows, 1)

                for b in range(12):
                    split(2)
                    if b:
                        rows(b - 1)
                    split(2)
                rows(11)
                if l:
                    dve_st.wait(act, "x2", l - 1)
                else:
                    act.wait_ge(small_ld, 16 * 15)
                norm_sums("sq1", l)
                dve_st.wait(act, "v1", l)
                rsqrt(ss[:, :, 0:1], 1, "rs1", l)
                x_hi(1, l)
                split(1)
                dve_st.wait(act, "gates", l)
                link(nc.scalar.activation(nab[:, :, :], nab[:, :, :], ACT.Exp))
                act_st.done(nc.scalar.activation(lp[:, :, :], nab[:, :, :], ACT.Ln, bias=1.0), "gate_e", l)

                def block_out(b):
                    act.wait_ge(w_used, through("in", l, b))
                    c = b * BLK + (GATES if b >= 4 else 0)
                    copy(p[:, 0, c:c + BLK], bank(b % 2 * 2)).then_inc(in_evA, 1)

                for b in range(8):
                    split(2)
                    if b:
                        block_out(b - 1)
                    split(2)
                block_out(7)
                for h in range(H):
                    nc.scalar.activation(DS[:, h, :], cst[:, C_RELP:C_RELP + P], ACT.Exp,
                                         scale=rlg[:, l, h:h + 1])
                    ins = nc.scalar.activation(TR[:, h, :], cst[:, C_RELM:C_RELM + P], ACT.Exp,
                                               scale=rlg[:, l, H + h:H + h + 1])
                act_st.done(ins, "dse", l)
                dve_st.wait(act, "mc", l)
                act_st.done(nc.scalar.activation(em[:, :, :, :], mrow[:, :, :, :], ACT.Exp, scale=-1.0), "em", l)
                act_st.done(nc.scalar.activation(wi[:, :, :], dm[:, :, :], ACT.Exp), "wi", l)
                act.wait_ge(in_evD, 8 * l + 8)
                act.wait_ge(in_evA, 8 * l + 8)
                nc.scalar.activation(p[:, :, OM:OM + WH], p[:, :, OM:OM + WH], ACT.Sigmoid)
                act_st.done(nc.scalar.activation(p[:, :, GR:GR + WH], p[:, :, GR:GR + WH], ACT.Silu), "sig", l)
                for s in range(S):
                    pe_st.wait(act, f"qk{s}", l)
                    act_st.done(copy(KTt[:, :, :], tiles(3)), f"kt{s}", l)
                    pe_st.wait(act, f"mb{s}", l)
                    if s:
                        dve_st.wait(act, "vw", l)
                    for d in range(2):
                        for h in range(H):
                            ins = nc.scalar.activation(ET[:, d, h, :], tiles(d)[:, h, :], ACT.Exp,
                                                       bias=Ac[:, d, s, h:h + 1])
                    act_st.done(ins, f"et{s}", l)
                    if s == 0:
                        pe_st.wait(act, "cst", l)
                        if l:
                            act.wait_ge(st_out, 16 * 4 * l)
                        for d in range(2):
                            ins = copy(STC[:, d, :, :], tiles(d))
                        act_st.done(ins, "stc", l)
                    pe_st.wait(act, f"qkr{s}", l)
                    act_st.done(copy(KTt[:, :, :], tiles(3)), f"ktr{s}", l)
                    if s == 0:
                        pe_st.wait(act, "rst", l)
                        act.wait_ge(st_out, 16 * (4 * l + 2))
                        for d in range(2):
                            ins = copy(STC[:, d, :, :], tiles(d))
                        act_st.done(ins, "rstc", l)
                gate_rows("gb1", l)
                dve_st.wait(act, "hv", l)
                rsqrt(ss[:, :, :], 8, "hrs", l)
                pe_st.wait(act, "yt", l)
                for s in range(S):
                    for t in range(KT):
                        g = 48 + 4 * l + t if t < H else 56 + 4 * l + t - H
                        ins = copy(XTh[s][:, t, :], tiles(2 * s + t // 4)[:, t % 4, :], colsB[:, g:g + 1])
                act_st.done(ins, "yh", l)
                split(8)
                dve_st.wait(act, "x1", l)
                norm_sums("sq2", l)
                dve_st.wait(act, "v2", l)
                rsqrt(ss[:, :, 0:1], 1, "rs2", l)
                if l == 0:
                    x_hi(2, l)
                    gate_rows("gb2", l)
                    ffn_act(lambda h: split(1), S, 0, ffn_first, silu_d, hTh_d,
                            (ffn_silu, ffn_prod, ffn_tr, ffn_hTh))

            pe_st.wait(act, "nat", 1)
            for s in range(S):
                for k in range(2):
                    ins = copy(nath[:, s, k * BLK:(k + 1) * BLK], bank(2 * s + k))
            act_st.done(ins, "nath", 1)
            dve_st.wait(act, "top", 1)
            act_st.done(nc.scalar.activation(wts[:, 1, :], wts[:, 0, :], ACT.Exp), "we", 1)

            def gather_hi(n):
                act.wait_ge(gath_mm, n + 1)
                for k in range(2):
                    copy(XTh[0][:, 4 * k:4 * k + 4, :], tiles(6 + k)).then_inc(xh_ready, 1)

            gather_hi(0)
            dve_st.wait(act, "route", 1)
            jobs = act.value_load(jti[0:1, MAX_JOBS:MAX_JOBS + 1], min_val=NE, max_val=NE + 3)
            with act.Fori(0, jobs) as i:
                def split_job(h):
                    u = h // 2
                    if h % 2 == 0:
                        act.wait_ge(moe_ld[u % RAW_MOE], i * (16 * 3) + 16 * (u // RAW_MOE + 1))
                    act.wait_ge(w_used, i * HALVES_FFN + (n_static_halves + h - HLS + 1))
                    copy(hi[(n_static_halves + h) % HLS][:, :],
                         raw_moe[u % RAW_MOE][:, h % 2 * HALF:(h % 2 + 1) * HALF]).then_inc(hi_done, 1)
                    if h == GATHER_AFTER + LAG:
                        gather_hi(i + 1)

                ffn_act(split_job, 1, i, n_static_halves, silu_m, hTh_m, (job_silu, job_prod, job_tr, job_hTh))
                act.wait_ge(w_used, i * HALVES_FFN + (n_static_halves + HALVES_FFN))
                act.wait_ge(pt_ready, i + 1)
                for c in range(2):
                    copy(yh[:, c * BLK:(c + 1) * BLK], bank(2 + c), gs[:, 0:1]).then_inc(yh_ready, 1)

            pe_st.wait(act, "gb2", 1)
            for s in range(S):
                for k in range(2):
                    ins = copy(N2[:, s, 4 * k:4 * k + 4, :], tiles(4 * (1 - s) + k))
            act_st.done(ins, "gb2", 1)
            dve_st.wait(act, "x2", 1)
            norm_sums("sqf")
            dve_st.wait(act, "vf")
            rsqrt(ss[:, :, 0:1], 1, "rsf")

        @block.vector
        def _(dve):
            chain = [0]
            pos = [0]
            v = nc.vector

            def link(ins):
                chain[0] += 1
                ins.then_inc(dve_chain, 1)
                dve.wait_ge(dve_chain, chain[0])

            def split(n=1):
                for _ in range(n):
                    q = pos[0]
                    u, off, size = halves[q]
                    dve.wait_ge(hi_done, q + 1)
                    v.tensor_tensor(lo[q % HLS][:, 0:size], raw[u % RAW][:, off:off + size],
                                    hi[q % HLS][:, 0:size].bitcast(F32), ALU.subtract).then_inc(lo_done, 1)
                    pos[0] += 1

            def refine(n):
                r_, t_, v_ = rs[:, :, 0:n], rs2[:, :, 0:n], ss[:, :, 0:n]
                link(v.tensor_tensor(t_, r_, r_, ALU.mult))
                link(v.tensor_tensor(t_, t_, v_, ALU.mult))
                link(v.tensor_scalar(t_, t_, -0.5, 1.5, ALU.mult, ALU.add))
                link(v.tensor_tensor(r_, r_, t_, ALU.mult))

            def negative_abs(out, z):
                return v.scalar_tensor_tensor(out=out, in0=z, scalar=-1.0, in1=z, op0=ALU.mult, op1=ALU.min)

            def log_sigmoid(out, z, softplus):
                return v.scalar_tensor_tensor(out=out, in0=z, scalar=0.0, in1=softplus, op0=ALU.min,
                                              op1=ALU.subtract)

            def mean(n, width, name, l=None):
                dve_st.done(v.tensor_scalar(ss[:, :, 0:n], ss[:, :, 0:n], 1.0 / width, EPS, ALU.mult, ALU.add),
                            name, l)

            def norm(k, l):
                g0 = (16 if k == 1 else 32) + 8 * l
                comp = 1 if k == 1 else 4
                dve_st.done(v.scalar_tensor_tensor(
                    out=scol[:, :, :], in0=modc[l][:, 8 * comp:8 * comp + 8, :], scalar=1.0,
                    in1=colsB[:, g0:g0 + 8].rearrange("p (t o) -> p t o", o=1).to_broadcast([P, KT, S]),
                    op0=ALU.add, op1=ALU.mult), f"mod{k}", l)
                act_st.wait(dve, f"sq{k}", l)
                mean(1, D, f"v{k}", l)
                act_st.wait(dve, f"rs{k}", l)
                refine(1)
                for s in range(S):
                    ins = v.tensor_scalar(N1[:, s, :], x[:, s, :], rs[:, s, 0:1], None, ALU.mult)
                dve_st.done(ins, f"xn{k}", l)
                pe_st.wait(dve, f"xt{k}", l)
                shift = 0 if k == 1 else 24
                for s in range(S):
                    for t in range(KT):
                        ins = v.tensor_scalar(N2[:, s, t, :], tiles(4 + 2 * s + t // 4)[:, t % 4, :],
                                              scol[:, t, s:s + 1], modc[l][:, shift + t, s:s + 1],
                                              ALU.mult, ALU.add)
                dve_st.done(ins, f"h{k}", l)
                if (k, l) != (2, 1):
                    act_st.wait(dve, f"xh{k}", l)
                    for s in range(S):
                        ins = v.tensor_tensor(XTl[s][:, :, :], N2[:, s, :, :], XTh[s][:, :, :].bitcast(F32),
                                              ALU.subtract)
                    dve_st.done(ins, f"xl{k}", l)

            def residual(banks, summed, name, l):
                for n, (s, c, bk) in enumerate(banks):
                    cols = slice(c * BLK, (c + 1) * BLK)
                    dve.wait_ge(w_used, summed(s, c))
                    link(v.tensor_tensor(upd[:, n % 2, :], bank(bk), N1[:, s, cols], ALU.mult))
                    ins = v.tensor_tensor(x[:, s, cols], x[:, s, cols], upd[:, n % 2, :], ALU.add)
                dve_st.done(ins, name, l)

            def ffn_dve(split_half, ns, i, first, silu, act_t, hTh, hTl, sems):
                silu_sem, prod, tr, hTh_sem, hTl_sem = sems

                def do_prod(j):
                    w = BLK if j < 5 else F - 5 * BLK
                    for s in range(ns):
                        dve.wait_ge(silu_sem, i * (6 * ns) + (ns * j + s + 1))
                        dve.wait_ge(w_used, i * HALVES_FFN + (first + UP_END[j] + 1))
                        if not (isinstance(i, int) and j == 0):
                            dve.wait_ge(tr, i * (6 * ns) + ns * j)
                        v.tensor_tensor(act_t[:, s, 0:w], bank(2 * s + 1)[:, 0:w], silu[:, s, 0:w], ALU.mult)\
                            .then_inc(prod, 1)

                def do_hT(j):
                    nt = 4 if j < 5 else 2
                    for s in range(ns):
                        dve.wait_ge(hTh_sem, i * (6 * ns) + (ns * j + s + 1))
                        v.tensor_tensor(hTl[:, 4 * j:4 * j + nt, s, :], tiles(4 + s)[:, 0:nt, :],
                                        hTh[:, 4 * j:4 * j + nt, s, :].bitcast(F32), ALU.subtract)\
                            .then_inc(hTl_sem, 1)

                for h in range(HALVES_FFN):
                    split_half(h)
                    for j in range(6):
                        if h == UP_END[j] + LAG:
                            do_prod(j)
                    for j in range(6):
                        if h == T_AFTER[j] + LAG:
                            do_hT(j)

            dve.wait_ge(small_ld, 16 * 15)
            v.tensor_copy(identb[:, :], ident)
            v.tensor_scalar(negm[:, 0, :], trif, 1.0, BIG, ALU.subtract, ALU.mult)
            v.tensor_scalar(negm[:, 1, :], trib, 1.0, BIG, ALU.subtract, ALU.mult)
            v.tensor_tensor(sel4[:, :], cst[0:4, C_ID:C_ID + 2], cst[0:4, C_ID + 2:C_ID + 4], ALU.add)
            dve_st.done(v.memset(m0r[:, :, :], 0.0), "prep")
            pe_st.wait(dve, "cols")
            v.tensor_copy(colsA[:, :], bank(4)[:, 0:96])
            act_st.wait(dve, "csil")
            v.tensor_copy(colsB[:, :], bank(5)[:, 0:80])
            csk = csil[:, :].rearrange("p (s k) -> p k s", s=2)
            link(v.tensor_copy(cT[:, :, 0:2], csk))
            dve_st.done(v.tensor_tensor(cT[:, :, 2:4], csk, cT[:, :, 0:2].bitcast(F32), ALU.subtract), "cs")
            dve_st.done(negative_abs(rtmp[:, :, :], retl[:, :, :]), "rnab")
            act_st.wait(dve, "rlp")
            link(log_sigmoid(rlg[:, :, :], retl[:, :, :], rtmp[:, :, :]))
            for d in range(4):
                ins = v.tensor_scalar(dqk[:, :, d, :], rlg[:, :, d % 2 * H:(d % 2 + 1) * H],
                                      cst[:, C_POS + d:C_POS + d + 1], None, ALU.mult)
            dve_st.done(ins, "rarg")

            for l in range(DEPTH):
                def cols(b):
                    dve.wait_ge(ada_tr, 12 * l + b + 1)
                    cb = colsA[:, 48 * l + 4 * b:48 * l + 4 * b + 4].rearrange("p (t o) -> p t o", o=1)
                    v.tensor_tensor(modc[l][:, 4 * b:4 * b + 4, :],
                                    bank(2 + b % 2)[:, 0:4 * S].rearrange("p (t s) -> p t s", s=S),
                                    cb.to_broadcast([P, 4, S]), ALU.add).then_inc(ada_cols, 1)

                for b in range(12):
                    split(2)
                    if b >= 2:
                        cols(b - 2)
                    split(2)
                cols(10)
                cols(11)
                dve.wait_ge(ada_cols, 12 * (l + 1))
                norm(1, l)

                split(1)
                dve.wait_ge(w_used, through("gates", l, 0))
                link(v.tensor_tensor(gt[:, :, :], bank(4)[:, 0:S * GATES].rearrange("p (s g) -> p s g", s=S),
                                     bg[:, l:l + 1, :].to_broadcast([P, S, GATES]), ALU.add))
                dve_st.done(negative_abs(nab[:, :, :], gt[:, :, 2 * H:4 * H]), "gates", l)

                def by_direction(t):
                    return t.rearrange("p s (d h) -> p d s h", d=2)

                def block_out(b):
                    dve.wait_ge(w_used, through("in", l, b))
                    c = b * BLK + (GATES if b >= 4 else 0)
                    v.tensor_copy(p[:, 1, c:c + BLK], bank(b % 2 * 2 + 1)).then_inc(in_evD, 1)

                for b in range(8):
                    split(2)
                    if b:
                        block_out(b - 1)
                    split(2)
                    if b == 0:
                        act_st.wait(dve, "gate_e", l)
                        for d in range(2):
                            ins = log_sigmoid(FL[:, d, :, :], gt[:, :, (2 + d) * H:(3 + d) * H],
                                              lp[:, :, d * H:(d + 1) * H])
                        dve_st.done(ins, "fl", l)
                    if b == 2:
                        pe_st.wait(dve, "bcum", l)
                        link(v.tensor_copy(Bc[:, :, :, :],
                                           bank(7)[:, 0:16].rearrange("p (d s h) -> p d s h", d=2, s=S)))
                        for d in range(2):
                            ins = v.tensor_tensor(Ac[:, d, :, :], gt[:, :, d * H:(d + 1) * H], Bc[:, d, :, :],
                                                  ALU.subtract)
                        dve_st.done(ins, "ba", l)
                    if b == 4:
                        pe_st.wait(dve, "arow", l)
                        dve.wait_ge(small_ld, 16 * 19)
                        link(v.tensor_copy(AR[:, :, :],
                                           bank(7)[0:2 * H, 0:2 * P].rearrange("p (d c) -> p d c", d=2)))
                        v.tensor_tensor_scan(MR[:, 0, :], AR[:, 0, :], AR[:, 0, :], m0r[:, l, 0:1],
                                             ALU.max, ALU.max)
                        link(v.tensor_tensor_scan(MR[:, 1, ::-1], AR[:, 1, ::-1], AR[:, 1, ::-1],
                                                  m0r[:, l, 1:2], ALU.max, ALU.max))
                        dve_st.done(v.tensor_scalar(nMR[:, :, :], MR[:, :, :], -1.0, None, ALU.mult), "mr", l)
                    if b == 6:
                        pe_st.wait(dve, "mcol", l)
                        if l:
                            dve.wait_ge(m_out, 32 * l)
                        link(v.tensor_copy(Mc[:, :, :, :],
                                           bank(7)[:, 0:16].rearrange("p (d s h) -> p d s h", d=2, s=S)))
                        v.tensor_tensor(dm[:, :, :], m0b[:, l, :, :], Mc[:, :, 1, :], ALU.subtract)
                        dve_st.done(v.tensor_tensor(mrow[:, :, :, :], Bc[:, :, :, :], Mc[:, :, :, :], ALU.add),
                                    "mc", l)
                block_out(7)
                dve.wait_ge(in_evD, 8 * l + 8)
                dve.wait_ge(in_evA, 8 * l + 8)

                qk = p[:, 1, QR:QR + 2 * WH].rearrange("p (h a f c) -> p h a f c", a=2, f=2, c=32)
                x1, x2 = qk[:, :, :, 0, :], qk[:, :, :, 1, :]

                def table(c0):
                    t = cst[:, c0:c0 + 64].rearrange("p (o a c) -> p o a c", o=1, a=2)
                    return t.to_broadcast([P, 2 * H, 2, 32])

                v.tensor_tensor(rope1[:, :, :, :], x2, table(C_SIN), ALU.mult)
                link(v.tensor_tensor(rope2[:, :, :, :], x1, table(C_SIN), ALU.mult))
                v.tensor_tensor(x1, x1, table(C_COS), ALU.mult)
                link(v.tensor_tensor(x2, x2, table(C_COS), ALU.mult))
                v.tensor_tensor(x1, x1, rope1[:, :, :, :], ALU.subtract)
                dve_st.done(v.tensor_tensor(x2, x2, rope2[:, :, :, :], ALU.add), "rope", l)
                dve_st.wait(dve, "rope", l)
                act_st.wait(dve, "dse", l)
                for t, c0 in ((DS, C_TRIF), (TR, C_TRIB)):
                    mask = cst[:, c0:c0 + P].rearrange("p (o c) -> p o c", o=1).to_broadcast([P, H, P])
                    ins = v.tensor_tensor(t[:, :, :], t[:, :, :], mask, ALU.mult)
                link(ins)
                link(v.tensor_tensor(DS[:, :, :], DS[:, :, :], TR[:, :, :], ALU.add))

                for s in range(S):
                    pe_st.wait(dve, f"qk{s}", l)
                    dve_st.done(v.tensor_copy(QT[:, :, :], tiles(2)), f"qt{s}", l)
                    act_st.wait(dve, f"et{s}", l)
                    pe_st.wait(dve, f"pqk{s}", l)
                    for d in range(2):
                        ins = v.scalar_tensor_tensor(out=ST[:, d, :, :], in0=tiles(4), scalar=SCALE,
                                                     in1=ET[:, d, :, :], op0=ALU.mult, op1=ALU.mult)
                    dve_st.done(ins, f"st{s}", l)
                    if s == 0:
                        for d, end in ((0, P - 1), (1, 0)):
                            v.tensor_scalar(wn[:, d, :], ET[:, d, :, end], SCALE, None, ALU.mult)
                            for h in range(H):
                                ins = v.tensor_scalar(VW[:, d, h, :], p[:, 0, VM + h * P:VM + (h + 1) * P],
                                                      ET[:, d, h, end:end + 1], SCALE, ALU.mult, ALU.mult)
                        dve_st.done(ins, "vw", l)
                    pe_st.wait(dve, f"num{s}", l)
                    act_st.wait(dve, "wi", l)

                    def small8(c0):
                        return bank(7)[:, c0:c0 + 8].rearrange("p (d h) -> p d h", d=2)

                    if s == 0:
                        link(v.tensor_copy(dent[:, :, :], small8(0)))
                    else:
                        link(v.tensor_tensor(dent[:, :, :], small8(8), wi[:, :, :], ALU.mult))
                        link(v.tensor_tensor(dent[:, :, :], small8(0), dent[:, :, :], ALU.add))
                    link(v.scalar_tensor_tensor(out=den[:, :, :], in0=dent[:, :, :], scalar=-1.0,
                                                in1=dent[:, :, :], op0=ALU.mult, op1=ALU.max))
                    link(v.tensor_tensor(den[:, :, :], den[:, :, :], em[:, :, s, :], ALU.max))
                    link(v.reciprocal(rden[:, :, s, :], den[:, :, :]))
                    terms = [(5, lambda h: rden[:, 0, s, h:h + 1]), (6, lambda h: rden[:, 1, s, h:h + 1])]
                    if s == 1:
                        link(v.tensor_tensor(wrd[:, :, :], wi[:, :, :], rden[:, :, 1, :], ALU.mult))
                        terms += [(2, lambda h: wrd[:, 0, h:h + 1]), (3, lambda h: wrd[:, 1, h:h + 1])]

                    def sum_terms(terms, h0, first):
                        for n, (bk, scalar) in enumerate(terms):
                            for h in range(H):
                                y = yy[:, s, h0 + h, :]
                                if n == 0 and first:
                                    ins = v.tensor_scalar(y, tiles(bk)[:, h, :], scalar(h), None, ALU.mult)
                                else:
                                    ins = v.scalar_tensor_tensor(out=y, in0=tiles(bk)[:, h, :], scalar=scalar(h),
                                                                 in1=y, op0=ALU.mult, op1=ALU.add)
                            if n + 1 < len(terms):
                                link(ins)
                        return ins

                    dve_st.done(sum_terms(terms, 0, True), f"y{s}", l)
                    if s == 0:
                        pe_st.wait(dve, "nst", l)
                        dve_st.done(v.tensor_copy(ncol[:, :], bank(7)[:, 0:8]), "nc", l)
                        pe_st.wait(dve, "nrow", l)
                        if l:
                            dve.wait_ge(n_out, 16 * l)
                        dve_st.done(v.tensor_copy(nrow[:, :], bank(4)[0:2 * H, 0:P]), "nr", l)
                    pe_st.wait(dve, f"qkr{s}", l)
                    dve_st.done(v.tensor_copy(QT[:, :, :], tiles(2)), f"qtr{s}", l)
                    pe_st.wait(dve, f"pr{s}", l)
                    dve_st.done(v.scalar_tensor_tensor(out=ST[:, 0, :, :], in0=tiles(4), scalar=SCALE,
                                                       in1=DS[:, :, :], op0=ALU.mult, op1=ALU.mult),
                                f"str{s}", l)
                    if s == 0:
                        pe_st.wait(dve, "cst", l)
                        act_st.wait(dve, "rdec")
                        for d in range(2):
                            for h in range(H):
                                ins = v.tensor_scalar(VW[:, d, h, :], p[:, 0, VR + h * P:VR + (h + 1) * P],
                                                      dqk[:, l, 2 + d, h:h + 1], SCALE, ALU.mult, ALU.mult)
                        dve_st.done(ins, "vwr", l)
                    pe_st.wait(dve, f"o{s}", l)
                    ins = v.tensor_copy(yy[:, s, H:2 * H, :], tiles(5))
                    if s == 1:
                        link(ins)
                        ins = sum_terms([(6, lambda h: dqk[:, l, 0, h:h + 1]), (0, lambda h: dqk[:, l, 1, h:h + 1])],
                                        H, False)
                    dve_st.done(ins, f"yr{s}", l)

                dve_st.wait(dve, "yr1", l)
                for s in range(S):
                    link(v.tensor_tensor(ysq[:, :, :], yy[:, s, :, :], yy[:, s, :, :], ALU.mult))
                    link(v.tensor_reduce(ss[:, s, :], ysq[:, :, :], AX_X, ALU.add))
                mean(8, P, "hv", l)
                act_st.wait(dve, "hrs", l)
                act_st.wait(dve, "sig", l)
                refine(8)
                for s in range(S):
                    for h in range(2 * H):
                        c = OM + h * P if h < H else GR + (h - H) * P
                        ins = v.scalar_tensor_tensor(out=yy[:, s, h, :], in0=yy[:, s, h, :],
                                                     scalar=rs[:, s, h:h + 1], in1=p[:, s, c:c + P],
                                                     op0=ALU.mult, op1=ALU.mult)
                dve_st.done(ins, "yn", l)
                pe_st.wait(dve, "yt", l)
                act_st.wait(dve, "yh", l)
                for s in range(S):
                    for t in range(KT):
                        g = 48 + 4 * l + t if t < H else 56 + 4 * l + t - H
                        ins = v.scalar_tensor_tensor(out=XTl[s][:, t, :], in0=tiles(2 * s + t // 4)[:, t % 4, :],
                                                     scalar=colsB[:, g:g + 1],
                                                     in1=XTh[s][:, t, :].bitcast(F32), op0=ALU.mult,
                                                     op1=ALU.subtract)
                dve_st.done(ins, "yl", l)
                split(8)
                act_st.wait(dve, "gb1", l)
                residual([(s, c, 2 * c + s) for c in range(2) for s in range(S)], 
                         lambda s, c: through("out", l, c), "x1", l)
                norm(2, l)
                if l == 0:
                    ffn_dve(lambda h: split(1), S, 0, ffn_first, silu_d, act_d, hTh_d, hTl_d,
                            (ffn_silu, ffn_prod, ffn_tr, ffn_hTh, ffn_hTl))
                    act_st.wait(dve, "gb2", l)
                    residual([(s, c, 2 * s + c) for s in range(S) for c in range(2)], 
                             lambda s, c: ffn_first + HALVES_FFN, "x2", l)

            v.memset(N1[:, :, :], 0.0)
            act_st.wait(dve, "nath", 1)
            for s in range(S):
                for k in range(2):
                    c = slice(k * BLK, (k + 1) * BLK)
                    ins = v.tensor_tensor(natl[:, s, c], bank(2 * s + k), nath[:, s, c].bitcast(F32), ALU.subtract)
            dve_st.done(ins, "natl", 1)
            pe_st.wait(dve, "router", 1)
            link(v.tensor_copy(lg[:, :, :], bank(4)[:, 0:S * NE].rearrange("p (s e) -> p s e", s=S)))
            for s in range(S):
                link(v.max(mx[:, s, :], lg[:, s, :]))
                link(v.max_index(mi[:, s, :], mx[:, s, :], lg[:, s, :]))
            v.tensor_copy(mif[:, :, :], mi[:, :, 0:2])
            ins = v.tensor_tensor(wts[:, 0, :], mx[:, :, 1], mx[:, :, 0], ALU.subtract)
            dve_st.done(ins, "top", 1)
            dve_st.wait(dve, "top", 1)
            for s in range(S):
                for t, k in ((M1, 0), (M2, 1)):
                    ins = v.tensor_scalar(t[:, s, :], cst[:, C_IOTA:C_IOTA + NE], mif[:, s, k:k + 1], None,
                                          ALU.is_equal)
            link(ins)
            dve_st.done(v.tensor_tensor(MK[:, :, :], M1[:, :, :], M2[:, :, :], ALU.add), "masks", 1)
            act_st.wait(dve, "we", 1)
            link(v.tensor_scalar(wts[:, 0, :], wts[:, 1, :], 1.0, None, ALU.add))
            link(v.reciprocal(wts[:, 0, :], wts[:, 0, :]))
            link(v.tensor_tensor(wts[:, 1, :], wts[:, 1, :], wts[:, 0, :], ALU.mult))
            dve.wait_ge(st_out, 16 * 8)
            pe_st.wait(dve, "rank", 1)
            link(v.tensor_scalar(nb[:, :], bank(5)[:, 16:24], float(P), 1.0, ALU.is_gt, ALU.add))
            link(v.tensor_tensor_scan(st_i[:, :], cst[:, C_ONES:C_ONES + NE], nb[:, :], 0.0, ALU.mult, ALU.add))
            link(v.tensor_copy(jtf[:, MAX_JOBS:MAX_JOBS + 1], st_i[0:1, NE - 1:NE]))
            link(v.tensor_tensor(st_i[:, :], st_i[:, :], nb[:, :], ALU.subtract))
            link(v.tensor_scalar(nb[:, :], st_i[:, :], float(P), -1.0, ALU.mult, ALU.add))
            for s in range(S):
                ins = v.tensor_tensor(slots[:, s, :], bank(5)[:, 8 * s:8 * s + 8], nb[:, :], ALU.add)
            link(ins)
            for k, t in enumerate((M1, M2)):
                link(v.tensor_tensor(stmp[:, :, :], t[:, :, :], slots[:, :, :], ALU.mult))
                link(v.tensor_reduce(keys[:, k, :], stmp[:, :, :], AX_X, ALU.add))
            starts = st_i[0:1, :].rearrange("p (o e) -> p o e", o=1).to_broadcast([1, MAX_JOBS, NE])
            number = cst[0:1, C_IOTA:C_IOTA + MAX_JOBS].rearrange("p (j o) -> p j o", o=1)
            link(v.tensor_tensor(jt[:, :, :], starts, number.to_broadcast([1, MAX_JOBS, NE]), ALU.is_le))
            link(v.tensor_reduce(jtf[:, 0:MAX_JOBS], jt[:, :, :], AX_X, ALU.add))
            link(v.tensor_scalar(jtf[:, 0:MAX_JOBS], jtf[:, 0:MAX_JOBS], 1.0, None, ALU.subtract))
            dve_st.done(v.tensor_copy(jti[:, :], jtf[:, :]), "route", 1)

            def select():
                for s in range(S):
                    v.tensor_scalar(P1[:, s, :], iota, keys[:, 0, s:s + 1], None, ALU.is_equal)
                    ins = v.tensor_scalar(P2[:, s, :], iota, keys[:, 1, s:s + 1], None, ALU.is_equal)
                ins.then_inc(sel_step, 1)

            def select_sum():
                v.tensor_tensor(Pr[:, :, :], P1[:, :, :], P2[:, :, :], ALU.add).then_inc(sel_ready, 1)
                v.tensor_scalar(keys[:, :, :], keys[:, :, :], float(P), None, ALU.subtract)\
                    .then_inc(key_step, 1)

            def gather_lo(n):
                dve.wait_ge(xh_ready, 2 * n + 2)
                for k in range(2):
                    v.tensor_tensor(XTl[0][:, 4 * k:4 * k + 4, :], tiles(6 + k),
                                    XTh[0][:, 4 * k:4 * k + 4, :].bitcast(F32), ALU.subtract)\
                        .then_inc(xl_ready, 1)

            select()
            dve.wait_ge(sel_step, 1)
            select_sum()
            gather_lo(0)
            dve_st.wait(dve, "route", 1)
            jobs = dve.value_load(jti[0:1, MAX_JOBS:MAX_JOBS + 1], min_val=NE, max_val=NE + 3)
            with dve.Fori(0, jobs) as i:
                def split_job(h):
                    u = h // 2
                    dve.wait_ge(hi_done, i * HALVES_FFN + (n_static_halves + h + 1))
                    q = (n_static_halves + h) % HLS
                    v.tensor_tensor(lo[q][:, :], raw_moe[u % RAW_MOE][:, h % 2 * HALF:(h % 2 + 1) * HALF],
                                    hi[q][:, :].bitcast(F32), ALU.subtract).then_inc(lo_done, 1)
                    if h == PT_AFTER + LAG:
                        dve.wait_ge(ptr_mm, i + 1)
                        v.tensor_copy(PT[:, :, :], bank(5)[:, 0:S * P].rearrange("p (s t) -> p s t", s=S))
                        v.tensor_copy(gs[:, :], bank(5)[:, S * P:S * P + 1]).then_inc(pt_ready, 1)
                        dve.wait_ge(key_step, i + 1)
                        select()
                        dve.wait_ge(sel_step, i + 2)
                        select_sum()
                    if h == GATHER_AFTER + LAG:
                        gather_lo(i + 1)

                ffn_dve(split_job, 1, i, n_static_halves, silu_m, act_m, hTh_m, hTl_m,
                        (job_silu, job_prod, job_tr, job_hTh, job_hTl))
                dve.wait_ge(yh_ready, i * 2 + 2)
                for c in range(2):
                    cols = slice(c * BLK, (c + 1) * BLK)
                    v.scalar_tensor_tensor(out=yl[:, cols], in0=bank(2 + c), scalar=gs[:, 0:1],
                                           in1=yh[:, cols].bitcast(F32), op0=ALU.mult, op1=ALU.subtract)\
                        .then_inc(yl_ready, 1)
                for g in range(4):
                    s, c = g // 2, g % 2
                    dve.wait_ge(scat_mm, i * 4 + (g + 1))
                    v.tensor_tensor(N1[:, s, c * BLK:(c + 1) * BLK], bank(6 + g % 2),
                                    N1[:, s, c * BLK:(c + 1) * BLK], ALU.add).then_inc(acc_done, 1)

            act_st.wait(dve, "gb2", 1)
            dve.wait_ge(acc_done, jobs * 4)
            link(v.tensor_tensor(N1[:, :, :], N1[:, :, :], N2[:, :, :, :].rearrange("p s t c -> p s (t c)"),
                                 ALU.mult))
            dve_st.done(v.tensor_tensor(x[:, :, :], x[:, :, :], N1[:, :, :], ALU.add), "x2", 1)
            act_st.wait(dve, "sqf")
            mean(1, D, "vf")
            act_st.wait(dve, "rsf")
            refine(1)
            dve.wait_ge(gfin_ld, 16)
            for s in range(S):
                ins = v.scalar_tensor_tensor(out=yfin[:, s, :], in0=x[:, s, :], scalar=rs[:, s, 0:1],
                                             in1=gfin[:, :], op0=ALU.mult, op1=ALU.mult)
            dve_st.done(ins, "yf")

        @block.tensor
        def _(pe):
            mm = nc.tensor.matmul
            pos = [0]

            def take():
                q = pos[0]
                pe.wait_ge(lo_done, q + 1)
                pos[0] += 1
                return q % HLS

            def product(out, xh, xl, q, cols, start, stop):
                mm(out, xh, hi[q][:, cols], start=start, stop=False)
                mm(out, xh, lo[q][:, cols], start=False, stop=False)
                return mm(out, xl, hi[q][:, cols], start=False, stop=stop)

            def turn(out, in_, n=P):
                return nc.tensor.transpose(out, in_, cst[0:n, C_ID:C_ID + n])

            def gate_rows(name, l, comp, banks):
                for s in range(S):
                    for t in range(KT):
                        ins = mm(tiles(banks[2 * s + t // 4])[:, t % 4, :],
                                 modc[l][:, 8 * comp + t, s:s + 1].to_broadcast([P, P]), ident,
                                 start=True, stop=True)
                pe_st.done(ins, name, l)

            def norm_turns(k, l):
                dve_st.wait(pe, f"xn{k}", l)
                for s in range(S):
                    for t in range(KT):
                        ins = turn(tiles(4 + 2 * s + t // 4)[:, t % 4, :], N1[:, s, t * P:(t + 1) * P])
                pe_st.done(ins, f"xt{k}", l)

            def ffn_pe(take_half, ns, i, xt, act_t, hTh, hTl, down_banks, sems, extra):
                silu_sem, prod, tr, hTl_sem = sems

                def turns(j):
                    nt = 4 if j < 5 else 2
                    for s in range(ns):
                        pe.wait_ge(prod, i * (6 * ns) + (ns * j + s + 1))
                        if not (isinstance(i, int) and j == 0):
                            pe.wait_ge(hTl_sem, i * (6 * ns) + ns * j)
                        for t in range(nt):
                            ins = turn(tiles(4 + s)[:, t, :], act_t[:, s, t * P:(t + 1) * P])
                        ins.then_inc(tr, 1)

                for h in range(HALVES_FFN):
                    if h < 44:
                        j = h // 8 if h < 40 else 5
                        r, per, w = (h % 8, 4, BLK) if h < 40 else (h - 40, 2, F - 5 * BLK)
                        is_up, part = r // per, r % per
                        kts = KT // per
                        if part == 0 and not (isinstance(i, int) and j == 0):
                            pe.wait_ge(prod if is_up else silu_sem, i * (6 * ns) + ns * j)
                        q = take_half(h)
                        for s in range(ns):
                            out = bank(2 * s + is_up)[:, 0:w]
                            for k in range(kts):
                                kt = part * kts + k
                                ins = product(out, xt[s][0][:, kt, :], xt[s][1][:, kt, :], q,
                                              slice(k * w, (k + 1) * w), kt == 0, kt == KT - 1)
                        release(ins)
                    else:
                        t = h - 44
                        if t == 0:
                            extra("down")
                        if t % 4 == 0:
                            pe.wait_ge(hTl_sem, i * (6 * ns) + ns * (t // 4 + 1))
                        q = take_half(h)
                        for s in range(ns):
                            for c in range(2):
                                ins = product(bank(down_banks[2 * s + c]), hTh[:, t, s, :], hTl[:, t, s, :], q,
                                              slice(c * BLK, (c + 1) * BLK), t == 0, t == FT - 1)
                        release(ins)
                    for j in range(6):
                        if h == T_AFTER[j]:
                            turns(j)
                    extra(h)

            def release(ins):
                ins.then_inc(w_used, 1)

            pe.wait_ge(small_ld, 16 * 15)
            turn(bank(4)[:, 0:96], rowsA[:, :], 96)
            pe_st.done(turn(bank(5)[:, 0:80], rowsB[:, :], 80), "cols")
            dve_st.wait(pe, "cs")

            for l in range(DEPTH):
                if l:
                    dve_st.wait(pe, "x2", l - 1)

                def ada_turns(b):
                    n = 12 * l + b
                    pe.wait_ge(ada_rows, n + 1)
                    if n >= 2:
                        pe.wait_ge(ada_cols, n - 1)
                    for t in range(4):
                        ins = mm(bank(2 + b % 2)[:, S * t:S * t + S], adarow[:, b % 2, t * P:(t + 1) * P],
                                 sel4[:, :], start=True, stop=True)
                    ins.then_inc(ada_tr, 1)

                for b in range(12):
                    n = 12 * l + b
                    if n >= 2:
                        pe.wait_ge(ada_rows, n - 1)
                    for k in range(4):
                        q = take()
                        for t in range(2):
                            c = slice(t * BLK, (t + 1) * BLK)
                            kt = 2 * k + t
                            mm(bank(b % 2)[0:4, :], cT[:, kt, :], hi[q][:, c], start=(kt == 0), stop=False)
                            ins = mm(bank(b % 2)[0:4, :], cT[:, kt, :], lo[q][:, c], start=False, stop=(kt == KT - 1))
                        release(ins)
                    if b:
                        ada_turns(b - 1)
                ada_turns(11)

                norm_turns(1, l)
                dve_st.wait(pe, "xl1", l)
                q = take()
                for s in range(S):
                    for kt in range(KT):
                        ins = product(bank(4)[:, s * GATES:(s + 1) * GATES], XTh[s][:, kt, :], XTl[s][:, kt, :], q,
                                      slice(kt * GATES, (kt + 1) * GATES), kt == 0, kt == KT - 1)
                release(ins)
                for b in range(8):
                    n = 8 * l + b
                    if n >= 2:
                        pe.wait_ge(in_evA, n - 1)
                        pe.wait_ge(in_evD, n - 1)
                    if b < 2:
                        pe.wait_ge(ada_cols, 12 * (l + 1))
                    for k in range(4):
                        q = take()
                        for s in range(S):
                            for t in range(2):
                                kt = 2 * k + t
                                ins = product(bank(b % 2 * 2 + s), XTh[s][:, kt, :], XTl[s][:, kt, :], q,
                                              slice(t * BLK, (t + 1) * BLK), kt == 0, kt == KT - 1)
                        release(ins)
                    if b == 1:
                        dve_st.wait(pe, "fl", l)
                        for d, tri in enumerate((trif, trib)):
                            ins = mm(bank(7)[:, 8 * d:8 * d + 8], tri, FL[:, d, :, :], start=True, stop=True)
                        pe_st.done(ins, "bcum", l)
                    if b == 3:
                        dve_st.wait(pe, "ba", l)
                        for d in range(2):
                            ins = turn(bank(7)[0:2 * H, d * P:(d + 1) * P],
                                       Ac[:, d, :, :].rearrange("p s h -> p (s h)"))
                        pe_st.done(ins, "arow", l)
                    if b == 5:
                        dve_st.wait(pe, "mr", l)
                        for d in range(2):
                            ins = turn(bank(7)[:, 8 * d:8 * d + 8], MR[:, d, :], 2 * H)
                        pe_st.done(ins, "mcol", l)

                pe.wait_ge(in_evA, 8 * l + 8)
                pe.wait_ge(in_evD, 8 * l + 8)
                pe.wait_ge(state_ld, 32 * (l + 1))

                def head(s, c0, h):
                    return p[:, s, c0 + h * P:c0 + (h + 1) * P]

                def turn_qk(s, qc, kc, name):
                    for bk, c0 in ((2, qc), (3, kc)):
                        for h in range(H):
                            ins = turn(tiles(bk)[:, h, :], head(s, c0, h))
                    pe_st.done(ins, name, l)

                def scores(name):
                    for h in range(H):
                        ins = mm(tiles(4)[:, h, :], KTt[:, h, :], QT[:, h, :], start=True, stop=True)
                    pe_st.done(ins, name, l)

                for s in range(S):
                    if s:
                        dve_st.wait(pe, "qtr0", l)
                    turn_qk(s, QM, KM, f"qk{s}")
                    dve_st.wait(pe, "mc", l)
                    if s:
                        act_st.wait(pe, "rstc", l)
                    for d in range(2):
                        mm(bank(d), identb[:, :],
                           negm[:, d:d + 1, :].to_broadcast([P, H, P]), start=True, stop=True)
                        for h in range(H):
                            r = s * H + h
                            ins = mm(tiles(d)[:, h, :], cst[0:2 * H, C_ID + r:C_ID + r + 1].to_broadcast([2 * H, P]),
                                     nMR[:, d, :], start=False, stop=True, skip_group_check=True)
                    pe_st.done(ins, f"mb{s}", l)
                    act_st.wait(pe, f"kt{s}", l)
                    dve_st.wait(pe, f"qt{s}", l)
                    scores(f"pqk{s}")
                    dve_st.wait(pe, f"st{s}", l)
                    for d in range(2):
                        for h in range(H):
                            mm(tiles(5 + d)[:, h, :], ST[:, d, h, :], head(s, VM, h), start=True, stop=True)
                    for d in range(2):
                        for h in range(H):
                            ins = mm(bank(7)[:, 4 * d + h:4 * d + h + 1], ST[:, d, h, :], cst[:, C_ONES:C_ONES + 1],
                                     start=True, stop=True)
                    if s == 1:
                        for d in range(2):
                            for h in range(H):
                                g = 64 + 8 * l + 4 * d + h
                                mm(tiles(2 + d)[:, h, :], QT[:, h, :], CM[:, d, h, :], start=True, stop=True)
                                ins = mm(bank(7)[:, 8 + 4 * d + h:9 + 4 * d + h], QT[:, h, :], colsB[:, g:g + 1],
                                         start=True, stop=True)
                    pe_st.done(ins, f"num{s}", l)
                    if s == 0:
                        dve_st.wait(pe, "vw", l)
                        act_st.wait(pe, "et0", l)
                        for d in range(2):
                            for h in range(H):
                                ins = mm(tiles(d)[:, h, :], head(0, KM, h), VW[:, d, h, :], start=True, stop=True)
                        pe_st.done(ins, "cst", l)
                        dve_st.wait(pe, "y0", l)
                        for d in range(2):
                            for h in range(H):
                                ins = mm(bank(7)[:, 4 * d + h:4 * d + h + 1], head(0, KM, h), wn[:, d, h:h + 1],
                                         start=True, stop=True)
                        pe_st.done(ins, "nst", l)
                        dve_st.wait(pe, "nc", l)
                        pe_st.done(turn(bank(4)[0:2 * H, 0:P], ncol[:, :]), "nrow", l)
                    else:
                        dve_st.wait(pe, "y1", l)
                        dve_st.wait(pe, "rope", l)
                    turn_qk(s, QR, KR, f"qkr{s}")
                    act_st.wait(pe, f"ktr{s}", l)
                    dve_st.wait(pe, f"qtr{s}", l)
                    scores(f"pr{s}")
                    dve_st.wait(pe, f"str{s}", l)
                    for h in range(H):
                        ins = mm(tiles(5)[:, h, :], ST[:, 0, h, :], head(s, VR, h), start=True, stop=True)
                    if s == 1:
                        for d, bk in ((0, 6), (1, 0)):
                            for h in range(H):
                                ins = mm(tiles(bk)[:, h, :], QT[:, h, :], SM[:, d, h, :], start=True, stop=True)
                    pe_st.done(ins, f"o{s}", l)
                    if s == 0:
                        act_st.wait(pe, "stc", l)
                        dve_st.wait(pe, "vwr", l)
                        for d in range(2):
                            for h in range(H):
                                ins = mm(tiles(d)[:, h, :], head(0, KR, h), VW[:, d, h, :], start=True, stop=True)
                        pe_st.done(ins, "rst", l)

                dve_st.wait(pe, "yr1", l)
                gate_rows("gb1", l, 2, (4, 5, 6, 7))
                dve_st.wait(pe, "yn", l)
                for s in range(S):
                    for t in range(KT):
                        ins = turn(tiles(2 * s + t // 4)[:, t % 4, :], yy[:, s, t, :])
                pe_st.done(ins, "yt", l)
                dve_st.wait(pe, "yl", l)
                for b in range(2):
                    for k in range(4):
                        q = take()
                        for s in range(S):
                            for t in range(2):
                                kt = 2 * k + t
                                ins = product(bank(2 * b + s), XTh[s][:, kt, :], XTl[s][:, kt, :], q,
                                              slice(t * BLK, (t + 1) * BLK), kt == 0, kt == KT - 1)
                        release(ins)
                norm_turns(2, l)
                if l == 0:
                    dve_st.wait(pe, "h2", l)
                    gate_rows("gb2", l, 5, (4, 5, 6, 7))
                    dve_st.wait(pe, "xl2", l)
                    act_st.wait(pe, "gb2", l)

                    def dense_extra(h):
                        if h == "down":
                            pe.wait_ge(ffn_prod, 12)

                    ffn_pe(lambda h: take(), S, 0, list(zip(XTh, XTl)), act_d, hTh_d, hTl_d, (0, 1, 2, 3),
                           (ffn_silu, ffn_prod, ffn_tr, ffn_hTl), dense_extra)

            dve_st.wait(pe, "h2", 1)
            for s in range(S):
                for kt in range(KT):
                    ins = mm(bank(4)[:, NE * s:NE * s + NE], N2[:, s, kt, :], wr[:, kt, :],
                             start=(kt == 0), stop=(kt == KT - 1))
            pe_st.done(ins, "router", 1)
            for s in range(S):
                for t in range(KT):
                    ins = turn(tiles(2 * s + t // 4)[:, t % 4, :], N2[:, s, t, :])
            pe_st.done(ins, "nat", 1)
            dve_st.wait(pe, "masks", 1)
            mm(bank(5)[:, 0:8], trif, MK[:, 0, :], start=True, stop=True)
            mm(bank(5)[:, 8:16], trif, MK[:, 1, :], start=True, stop=False)
            mm(bank(5)[:, 8:16], ones, MK[:, 0, :], start=False, stop=True)
            mm(bank(5)[:, 16:24], ones, MK[:, 0, :], start=True, stop=False)
            pe_st.done(mm(bank(5)[:, 16:24], ones, MK[:, 1, :], start=False, stop=True), "rank", 1)

            def gather(n):
                pe.wait_ge(sel_ready, n + 1)
                for t in range(KT):
                    out = tiles(6 + t // 4)[:, t % 4, :]
                    for s in range(S):
                        mm(out, nath[:, s, t * P:(t + 1) * P], Pr[:, s, :], start=(s == 0), stop=False)
                        ins = mm(out, natl[:, s, t * P:(t + 1) * P], Pr[:, s, :], start=False, stop=(s == S - 1))
                ins.then_inc(gath_mm, 1)

            dve_st.wait(pe, "natl", 1)
            gather(0)
            dve_st.wait(pe, "route", 1)
            jobs = pe.value_load(jti[0:1, MAX_JOBS:MAX_JOBS + 1], min_val=NE, max_val=NE + 3)
            with pe.Fori(0, jobs) as i:
                def take_job(h):
                    pe.wait_ge(lo_done, i * HALVES_FFN + (n_static_halves + h + 1))
                    return (n_static_halves + h) % HLS

                def job_extra(h):
                    if h == "down":
                        pe.wait_ge(yl_ready, i * 2)
                    if h == PT_AFTER:
                        pe.wait_ge(sel_ready, i + 1)
                        for s in range(S):
                            out = bank(5)[:, s * P:(s + 1) * P]
                            mm(out, P1[:, s, :], ident, start=True, stop=False)
                            mm(out, P2[:, s, :], ident, start=False, stop=True)
                        out = bank(5)[:, S * P:S * P + 1]
                        for n, (sel, k, s) in enumerate(((P1, 0, 0), (P1, 0, 1), (P2, 1, 0), (P2, 1, 1))):
                            ins = mm(out, sel[:, s, :], wts[:, k, s:s + 1], start=(n == 0), stop=(n == 3))
                        ins.then_inc(ptr_mm, 1)
                    if h == GATHER_AFTER:
                        pe.wait_ge(acc_done, i * 4)
                        gather(i + 1)

                pe.wait_ge(xl_ready, i * 2 + 2)
                ffn_pe(take_job, 1, i, [(XTh[0], XTl[0])], act_m, hTh_m, hTl_m, (2, 3),
                       (job_silu, job_prod, job_tr, job_hTl), job_extra)
                pe.wait_ge(yl_ready, i * 2 + 2)
                pe.wait_ge(xl_ready, i * 2 + 4)
                for g in range(4):
                    s, c = g // 2, g % 2
                    if g >= 2:
                        pe.wait_ge(acc_done, i * 4 + (g - 1))
                    cols = slice(c * BLK, (c + 1) * BLK)
                    mm(bank(6 + g % 2), PT[:, s, :], yh[:, cols], start=True, stop=False)
                    mm(bank(6 + g % 2), PT[:, s, :], yl[:, cols], start=False, stop=True).then_inc(scat_mm, 1)

            gate_rows("gb2", 1, 5, (4, 5, 0, 1))


_INS = ["x_prompt", "x_sample", "state_mlstm_C", "state_mlstm_n", "state_mlstm_m", "state_ret_S", "c", "c_ctx",
        "norm1_g", "norm2_g", "norm_f_g", "w_ada", "b_ada", "w_in", "b_gates", "ret_decay_logit",
        "mlstm_norm_g", "ret_norm_g", "w_out", "ffn_w_gate", "ffn_w_up", "ffn_w_down",
        "moe_w_router", "moe_w_gate", "moe_w_up", "moe_w_down"]
_OUTS = {"y_prompt": (1, P, D), "y_sample": (1, P, D), "new_C": (1, DEPTH, 2, H, P, P),
         "new_n": (1, DEPTH, 2, H, P), "new_m": (1, DEPTH, 2, H), "new_S": (1, DEPTH, 2, H, P, P)}


def kernel(**inputs):
    import concourse.bacc as bacc
    from concourse.bass_utils import run_bass_kernel_spmd

    nc = bacc.Bacc("TRN2", target_bir_lowering=False, num_devices=1)
    arrays = {name: np.ascontiguousarray(inputs[name]) for name in _INS}
    arrays["consts"] = shape_constants()
    a = {n: nc.dram_tensor(n, v.shape, mybir.dt.from_np(v.dtype), kind="ExternalInput").ap()
         for n, v in arrays.items()}
    o = {n: nc.dram_tensor(n, shape, F32, kind="ExternalOutput").ap() for n, shape in _OUTS.items()}
    bass_hybrid_backbone(nc, a, o)
    got = run_bass_kernel_spmd(nc, [arrays], core_ids=[0]).results[0]
    return tuple(got[n] for n in _OUTS)
```

```python
from contextlib import ExitStack

import numpy as np
import concourse.bass as bass
from concourse import mybir

ALU = mybir.AluOpType
ACT = mybir.ActivationFunctionType
F32 = mybir.dt.float32
F32R = mybir.dt.float32r
BF16 = mybir.dt.bfloat16
I32 = mybir.dt.int32
U32 = mybir.dt.uint32
AX_X = mybir.AxisListType.X

P = 128
S = 2
D = 1024
KT = D // P
DEPTH = 2
H = 4
WH = H * P
GATES = 4 * H
D_IN = 8 * WH + GATES
QM, KM, VM, OM, GT, QR, KR, VR, GR = (0, WH, 2 * WH, 3 * WH, 4 * WH, 4 * WH + GATES, 5 * WH + GATES,
                                      6 * WH + GATES, 7 * WH + GATES)
F = 2816
FT = F // P
NE = 8
EPS = 1e-6
GRID_W = 64
SCALE = float(P) ** -0.5
BLK = 512
HALF = 1024
RAW = 8
HLS = 3
HLS_MOE = 6
UNITS_FFN = 33
HALVES_FFN = 66
BIG = 1.0e30
MAX_JOBS = 16
PACE_DENSE = 2, [11, 19, 27, 35, 41, 47]
PACE_JOB = 4, [13, 21, 29, 37, 45, 51]
GATE_END = [3, 11, 19, 27, 35, 41]
UP_END = [7, 15, 23, 31, 39, 43]
PT_AFTER, GATHER_AFTER = 48, 55
Y_AT, SCATTER_AFTER = 3, (8, 12)

C_ID, C_TRIF, C_TRIB, C_RELP, C_RELM, C_ONES, C_IOTA = (P * n for n in range(7))
C_COS = 7 * P
C_SIN = C_COS + 64
C_POS = C_SIN + 64
C_ALL = C_POS + 4


def shape_constants():
    i = np.arange(P, dtype=np.float64)
    row, col = i[:, None], i[None, :]
    t = np.zeros((P, C_ALL), np.float32)
    t[:, C_ID:C_ID + P] = row == col
    t[:, C_TRIF:C_TRIF + P] = row <= col
    t[:, C_TRIB:C_TRIB + P] = row >= col
    t[:, C_RELP:C_RELP + P] = np.maximum(col - row, 0)
    t[:, C_RELM:C_RELM + P] = np.maximum(row - col, 0)
    t[:, C_ONES:C_ONES + P] = 1
    t[:, C_IOTA:C_IOTA + P] = col
    half = P // 4
    freqs = (np.float32(10000.0) ** (-np.arange(half, dtype=np.float32) / np.float32(half))).astype(np.float32)
    for a, pos in enumerate((np.arange(P) // GRID_W, np.arange(P) % GRID_W)):
        ang = (pos.astype(np.float32)[:, None] * freqs).astype(np.float64)
        t[:, C_COS + a * half:C_COS + (a + 1) * half] = np.cos(ang)
        t[:, C_SIN + a * half:C_SIN + (a + 1) * half] = np.sin(ang)
    t[:, C_POS + 0] = i + 1
    t[:, C_POS + 1] = P - i
    t[:, C_POS + 2] = P - 1 - i
    t[:, C_POS + 3] = i
    return t


class Stages:

    def __init__(self, sem, first, layer, last):
        self.sem = sem
        self.value = {(n, None): k + 1 for k, n in enumerate(first)}
        for l in range(DEPTH):
            base = len(self.value)
            self.value |= {(n, l): base + k + 1 for k, n in enumerate(layer(l))}
        base = len(self.value)
        self.value |= {(n, None): base + k + 1 for k, n in enumerate(last)}
        self.at = 0

    def done(self, ins, name, l=None):
        self.at += 1
        assert self.value[(name, l)] == self.at, (name, l, self.at)
        ins.then_inc(self.sem, 1)

    def wait(self, eng, name, l=None):
        eng.wait_ge(self.sem, self.value[(name, l)])


RAW_MOE_SLOT = [k for n in (8, 7, 6, 6, 6) for k in range(n)]


def last_user(slots, n):
    return next(m for m in range(n - 1, n - 1 - len(slots), -1) if slots[m % len(slots)] == slots[n])


ADA_NB = 4
ADA_W = S * ADA_NB
ADA_FILL = {("first", 0): 32,
            ("mb0", 0): 2, ("pqk0", 0): 5, ("num0", 0): 3, ("cst", 0): 3, ("qkr0", 0): 2, ("pr0", 0): 2,
            ("o0", 0): 1, ("rst", 0): 2, ("mb1", 0): 2, ("pqk1", 0): 5, ("qkr1", 0): 1, ("pr1", 0): 1, ("o1", 0): 3,
            ("gb1", 0): 10, ("yt", 0): 10, ("x1", 0): 12,
            ("xt2", 0): 4, ("gb2", 0): 4, ("ffn12", 0): 8, ("x2", 0): 16,
            ("xt1", 1): 8,
            ("mb0", 1): 2, ("pqk0", 1): 4, ("num0", 1): 3, ("cst", 1): 2, ("qkr0", 1): 1, ("pr0", 1): 1,
            ("rst", 1): 2, ("mb1", 1): 1, ("pqk1", 1): 4, ("qkr1", 1): 1, ("o1", 1): 3,
            ("gb1", 1): 10, ("yt", 1): 10, ("x1", 1): 12}
ADA_BEFORE_OUT = ["mb0", "pqk0", "num0", "cst", "qkr0", "pr0", "o0", "rst", "mb1", "pqk1", "num1", "qkr1", "pr1",
                  "o1", "gb1", "yt"]


def static_units():
    left = [("ada", l, b, h, []) for l in range(DEPTH) for b in range(6 * D // BLK) for h in range(2)]
    units = []

    def ada(l, *steps):
        tiles = sum(ADA_FILL.get((step, l), 0) for step in steps)
        assert tiles % 4 == 0
        units.extend(left.pop(0) for _ in range(tiles // 4))

    ada(0, "first")
    for l in range(DEPTH):
        ada(l, "xt1")
        units += [("gates", l, 0, 0, [KT * GATES])]
        units += [("in", l, b, h, [HALF, HALF]) for b in range(8) for h in range(2)]
        ada(l, *ADA_BEFORE_OUT)
        units += [("out", l, b, h, [HALF, HALF]) for b in range(D // BLK) for h in range(2)]
        ada(l, "x1", "xt2", "gb2")
        if l == 0:
            for u in range(UNITS_FFN):
                units += [("ffn", l, u, 0, [HALF, HALF])]
                ada(l, f"ffn{u}")
            ada(l, "x2")
    assert not left
    return units


def bass_hybrid_backbone(nc, a, o):
    ctx = ExitStack()
    with ctx:
        base = 16512

        def at(name, offset, shape, dt=F32):
            return nc.alloc_sbuf_tensor_at(name, shape, dt, offset=base + offset)

        def sem(name):
            return ctx.enter_context(nc.semaphore(name))

        raw = [at(f"raw{n}", 8192 * n, [P, 2 * HALF]) for n in range(RAW)]
        top = 8192 * RAW
        hi = [at(f"hi{n}", top + 4096 * n, [P, HALF], F32R) for n in range(HLS)]
        top += 4096 * HLS
        lo = [at(f"lo{n}", top + 4096 * n, [P, HALF], F32R) for n in range(HLS)]
        top += 4096 * HLS
        region = top
        p = at("p", region, [P, S, D_IN])
        r = region + 4 * S * D_IN
        ET = at("ET", r, [P, 2, H, P])
        ysq = at("ysq", r, [P, 2 * H, P])
        ST = at("ST", r + 4096, [P, 2, H, P])
        upd = at("upd", r + 4096, [P, 2, BLK])
        QT = at("QT", r + 8192, [P, H, P])
        KTt = at("KTt", r + 10240, [P, H, P])
        VW = at("VW", r + 12288, [P, 2, H, P])
        rope1 = at("rope1", r + 12288, [P, 2 * H, 2, 32])
        rope2 = at("rope2", r + 14336, [P, 2 * H, 2, 32])
        AR = at("AR", r + 12288, [2 * H, 2, P])
        CM = at("CM", r + 16384, [P, 2, H, P])
        SM = at("SM", r + 20480, [P, 2, H, P])
        DS = at("DS", r + 24576, [P, H, P])
        TR = at("TR", r + 26624, [P, H, P])
        STC = at("STC", r + 28672, [P, 2, H, P])
        region_size = 4 * S * D_IN + 32768
        rowsA = at("rowsA", region, [96, P])
        rowsB = at("rowsB", region + 512, [80, P])
        hTh_d = at("hTh_d", region, [P, FT, S, P], F32R)
        hTl_d = at("hTl_d", region + 4 * FT * S * P, [P, FT, S, P], F32R)
        silu_d = at("silu_d", region + 8 * FT * S * P, [P, S, BLK])
        act_d = at("act_d", region + 8 * FT * S * P + 4096, [P, S, BLK])
        m = region
        hTh_m = at("hTh_m", m, [P, FT, 1, P], F32R)
        hTl_m = at("hTl_m", m + 4 * FT * P, [P, FT, 1, P], F32R)
        m += 8 * FT * P
        nath = at("nath", m, [P, S, D], F32R)
        natl = at("natl", m + 8192, [P, S, D], F32R)
        m += 16384
        yh = at("yh", m, [P, D], F32R)
        yl = at("yl", m + 4096, [P, D], F32R)
        silu_m = at("silu_m", m + 8192, [P, 1, BLK])
        act_m = at("act_m", m + 10240, [P, 1, BLK])
        m += 12288
        P1 = at("P1", m, [P, S, P])
        P2 = at("P2", m + 1024, [P, S, P])
        Pr = at("Pr", m + 2048, [P, S, P], F32R)
        PT = at("PT", m + 3072, [P, S, P], F32R)
        m += 4096
        hi3, lo3 = at("hi3", m, [P, HALF], F32R), at("lo3", m + 4096, [P, HALF], F32R)
        jt = at("jt", m + 8192, [1, MAX_JOBS, NE])
        jtf = at("jtf", m + 8704, [1, MAX_JOBS + 1])
        assert m + 8192 + 1024 <= region + region_size
        gfin = at("gfin", region, [P, D])
        yfin = at("yfin", region + 4096, [P, S, D])
        top = region + region_size
        x = at("x", top, [P, S, D])
        top += 8192
        XTh = [at("XTh0", top, [P, KT, P], F32R), at("XTh1", top + 8192, [P, KT, P], F32R)]
        XTl = [at("XTl0", top + 4096, [P, KT, P], F32R), at("XTl1", top + 12288, [P, KT, P], F32R)]
        hi4, lo4 = at("hi4", top + 8192, [P, HALF], F32R), at("lo4", top + 12288, [P, HALF], F32R)
        top += 16384
        N1 = at("N1", top, [P, S, D])
        N2 = at("N2", top + 8192, [P, S, KT, P])
        hi5, lo5 = at("hi5", top + 8192, [P, HALF], F32R), at("lo5", top + 12288, [P, HALF], F32R)
        top += 16384
        hi += [hi3, hi4, hi5]
        lo += [lo3, lo4, lo5]
        assert len(hi) == HLS_MOE and HALVES_FFN % HLS_MOE == 0 and len(RAW_MOE_SLOT) == UNITS_FFN
        small_at = [top]

        def small(name, shape, dt=F32):
            n = int(np.prod(shape[1:])) * (2 if dt == BF16 else 4)
            t = at(name, small_at[0], shape, dt)
            small_at[0] += -(-n // 32) * 32
            return t

        cst = small("cst", [P, C_ALL])
        identb = small("identb", [P, P], BF16)
        negm = small("negm", [P, 2, P], BF16)
        modc = [small(f"modc{l}", [P, 48, S]) for l in range(DEPTH)]
        colsA = small("colsA", [P, 96])
        colsB = small("colsB", [P, 80])
        csil = small("csil", [P, 16])
        cond = small("cond", [P, KT, 2 * ADA_W - S])
        adarow = small("adarow", [ADA_W, BLK])
        scol = small("scol", [P, KT, S])
        bg = small("bg", [P, DEPTH, GATES])
        retl = small("retl", [P, DEPTH, 2 * H])
        rlg = small("rlg", [P, DEPTH, 2 * H])
        rtmp = small("rtmp", [P, DEPTH, 2 * H])
        dqk = small("dqk", [P, DEPTH, 4, H])
        m0b = small("m0b", [P, DEPTH, 2, H])
        m0r = small("m0r", [2 * H, DEPTH, 2])
        wr = small("wr", [P, KT, NE])
        gt = small("gt", [P, S, GATES])
        nab = small("nab", [P, S, 2 * H])
        lp = small("lp", [P, S, 2 * H])
        FL = small("FL", [P, 2, S, H])
        Bc = small("Bc", [P, 2, S, H])
        Ac = small("Ac", [P, 2, S, H])
        Mc = small("Mc", [P, 2, S, H])
        yy = N2
        mrow = small("mrow", [P, 2, S, H])
        em = small("em", [P, 2, S, H])
        wi = small("wi", [P, 2, H])
        dm = small("dm", [P, 2, H])
        MR = small("MR", [2 * H, 2, P])
        nMR = small("nMR", [2 * H, 2, P])
        den = small("den", [P, 2, H])
        dent = small("dent", [P, 2, H])
        rden = small("rden", [P, 2, S, H])
        wrd = small("wrd", [P, 2, H])
        wn = small("wn", [P, 2, H])
        ncol = small("ncol", [P, 2 * H])
        nrow = small("nrow", [2 * H, P])
        ss = small("ss", [P, S, 8])
        ln_v = small("ln_v", [P, S, 8])
        rs = small("rs", [P, S, 8])
        rs2 = small("rs2", [P, S, 8])
        lg = small("lg", [P, S, NE])
        mx = small("mx", [P, S, 8])
        mi = small("mi", [P, S, 8], U32)
        mif = small("mif", [P, S, 2])
        M1 = small("M1", [P, S, NE])
        M2 = small("M2", [P, S, NE])
        MK = small("MK", [P, S, NE])
        nb = small("nb", [P, NE])
        st_i = small("st_i", [P, NE])
        slots = small("slots", [P, S, NE])
        stmp = small("stmp", [P, S, NE])
        keys = small("keys", [P, 2, S])
        wts = small("wts", [P, 2, S])
        jti = small("jti", [1, MAX_JOBS + 1], I32)
        gs = small("gs", [P, 1])
        assert base + small_at[0] <= 229368, base + small_at[0]

        ident = cst[:, C_ID:C_ID + P]
        trif = cst[:, C_TRIF:C_TRIF + P]
        trib = cst[:, C_TRIB:C_TRIB + P]
        ones = cst[:, C_ONES:C_ONES + P]
        iota = cst[:, C_IOTA:C_IOTA + P]

        pb = ctx.enter_context(nc.psum_tensor("pb", [P, 8, BLK], F32))

        def bank(n):
            return pb[:, n, :]

        def tiles(n):
            return pb[:, n, :].rearrange("p (t c) -> p t c", c=P)

        raw_ld = [sem(f"raw_ld{n}") for n in range(RAW)]
        moe_ld = [sem(f"moe_ld{n}") for n in range(RAW)]
        hi_done, lo_done, w_used = sem("hi_done"), sem("lo_done"), sem("w_used")
        small_ld, state_ld, gfin_ld = sem("small_ld"), sem("state_ld"), sem("gfin_ld")
        ada_sum, ada_rows, ada_turned, ada_cols = (sem(f"ada_{n}") for n in ("sum", "rows", "turned", "cols"))
        in_evA, in_evD = sem("in_evA"), sem("in_evD")
        ffn_silu, ffn_prod = sem("ffn_silu"), sem("ffn_prod")
        ffn_tr, ffn_hTh, ffn_hTl = (sem(n) for n in ("ffn_tr", "ffn_hTh", "ffn_hTl"))
        job_silu, job_prod = sem("job_silu"), sem("job_prod")
        job_tr, job_hTh, job_hTl = (sem(n) for n in ("job_tr", "job_hTh", "job_hTl"))
        sel_ready, ptr_mm, pt_ready = sem("sel_ready"), sem("ptr_mm"), sem("pt_ready")
        sel_step, key_step = sem("sel_step"), sem("key_step")
        gath_mm, xh_ready, xl_ready = sem("gath_mm"), sem("xh_ready"), sem("xl_ready")
        yh_ready, yl_ready, scat_mm, acc_done = sem("yh_ready"), sem("yl_ready"), sem("scat_mm"), sem("acc_done")
        dve_chain, act_chain = sem("dve_chain"), sem("act_chain")
        st_out, m_out, n_out, y_out = sem("st_out"), sem("m_out"), sem("n_out"), sem("y_out")

        pe_st = Stages(sem("pe_stage"), ["cols"], lambda l: [
            "xt1", "bcum", "arow", "mcol",
            "qk0", "mb0", "pqk0", "num0", "cst", "nst", "nrow", "qkr0", "pr0", "o0", "rst",
            "qk1", "mb1", "pqk1", "num1", "qkr1", "pr1", "o1", "gb1a", "gb1", "yt", "xt2",
            *(["gb2a", "gb2"] if l == 0 else ["router", "nat", "rank", "gb2a", "gb2"])], [])
        act_st = Stages(sem("act_stage"), ["csil", "rlp", "rdec"], lambda l: [
            "sq1", "rs1", "xh1", "gate_e", "dse", "em", "wi", "sig",
            "kt0", "et0", "stc", "ktr0", "rstc",
            "kt1", "et1", "ktr1", "gb1a", "gb1", "hrs", "yh", "sq2", "rs2",
            *(["xh2", "gb2a", "gb2"] if l == 0 else ["nath", "we", "gb2a", "gb2"])], ["sqf", "rsf"])
        dve_st = Stages(sem("dve_stage"), ["prep", "cond", "rnab", "rarg"], lambda l: [
            "v1", "xn1", "mod1", "h1", "xl1", "gates", "fl", "ba", "mr", "mc", "rope",
            "qt0", "st0", "vw", "y0", "nc", "nr", "qtr0", "str0", "vwr", "yr0",
            "qt1", "st1", "y1", "qtr1", "str1", "yr1", "hv", "yn", "yl", "x1",
            "v2", "xn2", "mod2", "h2",
            *(["xl2", "x2"] if l == 0 else ["natl", "top", "masks", "route", "x2"])], ["vf", "yf"])

        units = static_units()
        n_static_halves = sum(len(u[-1]) for u in units)
        halves = []
        for n, u in enumerate(units):
            for k, size in enumerate(u[-1]):
                halves.append((n, k * HALF, size))
        halves_before = [sum(len(u[-1]) for u in units[:n]) for n in range(len(units) + 1)]

        def through(kind, l, b):
            return halves_before[1 + max(n for n, u in enumerate(units) if u[:3] == (kind, l, b))]

        ffn_first = halves_before[min(n for n, u in enumerate(units) if u[0] == "ffn")]

        def ffn_source(gate, up, down, u):
            if u < 22:
                j, part = (u // 4, u % 4) if u < 20 else (5, 2 * (u - 20))
                w, k0 = (gate, up)[part // 2], 4 * (part % 2)
                if j < 5:
                    return w.rearrange("(k p) n -> p k n", p=P)[:, k0:k0 + 4, j * BLK:(j + 1) * BLK]
                return w.rearrange("(k p) n -> p k n", p=P)[:, :, 5 * BLK:F]
            t = 2 * (u - 22)
            return down.rearrange("(t p) n -> p t n", p=P)[:, t:t + 2, :]

        def source(unit):
            kind, l, b, h, _ = unit
            if kind == "ada":
                return a["w_ada"][l].rearrange("(k p) n -> p k n", p=P)[:, 4 * h:4 * h + 4, b * BLK:(b + 1) * BLK]
            if kind == "gates":
                return a["w_in"][l].rearrange("(k p) n -> p k n", p=P)[:, :, GT:GT + GATES]
            if kind == "in":
                c = b * BLK + (GATES if b >= 4 else 0)
                return a["w_in"][l].rearrange("(k p) n -> p k n", p=P)[:, 4 * h:4 * h + 4, c:c + BLK]
            if kind == "out":
                return a["w_out"][l].rearrange("(k p) n -> p k n", p=P)[:, 4 * h:4 * h + 4, b * BLK:(b + 1) * BLK]
            return ffn_source(a["ffn_w_gate"][0], a["ffn_w_up"][0], a["ffn_w_down"][0], b)

        def unit_view(slot, size, cols):
            return slot[:, 0:size].rearrange("p (k n) -> p k n", n=cols)

        block = ctx.enter_context(nc.Block())

        @block.sync
        def _(sp):
            loads = [
                (cst[:, :], a["consts"]),
                (rowsA[:, :], a["b_ada"].rearrange("l (r p) -> (l r) p", p=P)),
                (rowsB[0:8, :], a["c_ctx"].rearrange("(r p) -> r p", p=P)),
                (rowsB[8:16, :], a["c"].rearrange("b (r p) -> (b r) p", p=P)),
                (rowsB[16:32, :], a["norm1_g"].rearrange("l (r p) -> (l r) p", p=P)),
                (rowsB[32:48, :], a["norm2_g"].rearrange("l (r p) -> (l r) p", p=P)),
                (rowsB[48:56, :], a["mlstm_norm_g"].rearrange("l (r p) -> (l r) p", p=P)),
                (rowsB[56:64, :], a["ret_norm_g"].rearrange("l (r p) -> (l r) p", p=P)),
                (rowsB[64:80, :], a["state_mlstm_n"].rearrange("b l d h p -> (b l d h) p")),
                (x[:, 0, :], a["x_prompt"][0]),
                (x[:, 1, :], a["x_sample"][0]),
                (bg[:, :, :], a["b_gates"].rearrange("(o l) g -> o l g", o=1).to_broadcast([P, DEPTH, GATES])),
                (retl[:, :, :], a["ret_decay_logit"].rearrange("(o l) d h -> o l (d h)", o=1)
                    .to_broadcast([P, DEPTH, 2 * H])),
                (m0b[:, :, :, :], a["state_mlstm_m"].to_broadcast([P, DEPTH, 2, H])),
                (wr[:, :, :], a["moe_w_router"][0].rearrange("(k p) e -> p k e", p=P)),
            ]
            for dst, src in loads:
                sp.dma_start(dst, src).then_inc(small_ld, 16)
            dve_st.wait(sp, "prep")
            for l in range(DEPTH):
                for d in range(2):
                    sp.dma_start(m0r[H:2 * H, l, d:d + 1], a["state_mlstm_m"][0, l, d].rearrange("(h o) -> h o", o=1))\
                        .then_inc(small_ld, 16)

            def wait_used(n):
                if units[n][0] == "ada":
                    sp.wait_ge(ada_sum, sum(u[0] == "ada" for u in units[:n + 1]))
                else:
                    sp.wait_ge(lo_done, halves_before[n + 1])

            for n, unit in enumerate(units):
                if n >= RAW:
                    wait_used(n - RAW)
                kind, l, b, h, sizes = unit
                cols = {"gates": GATES, "ffn": (BLK if b < 20 else F - 5 * BLK) if b < 22 else D}.get(kind, BLK)
                sp.dma_start(unit_view(raw[n % RAW], sum(sizes) or 2 * HALF, cols), source(unit))\
                    .then_inc(raw_ld[n % RAW], 16)
                if kind == "gates":
                    if l > 0:
                        pe_st.wait(sp, "o1", l - 1)
                        dve_st.wait(sp, "x2", l - 1)
                    sp.dma_start(CM[:, :, :, :], a["state_mlstm_C"][0, l].rearrange("d h p e -> p d h e"))\
                        .then_inc(state_ld, 16)
                    sp.dma_start(SM[:, :, :, :], a["state_ret_S"][0, l].rearrange("d h p e -> p d h e"))\
                        .then_inc(state_ld, 16)

            def job(u, e):
                src = ffn_source(*(a[f"moe_w_{w}"][0][e] if isinstance(e, int) else
                                   a[f"moe_w_{w}"][0][bass.ds(e, 1)].rearrange("o r n -> (o r) n")
                                   for w in ("gate", "up", "down")), u)
                cols = (BLK if u < 20 else F - 5 * BLK) if u < 22 else D
                slot = RAW_MOE_SLOT[u]
                sp.dma_start(unit_view(raw[slot], 2 * HALF, cols), src).then_inc(moe_ld[slot], 16)

            for u in range(UNITS_FFN):
                if u < RAW:
                    wait_used(max(n for n in range(len(units)) if n % RAW == u))
                else:
                    sp.wait_ge(lo_done, n_static_halves + 2 * (last_user(RAW_MOE_SLOT, u) + 1))
                job(u, 0)
            dve_st.wait(sp, "route", 1)
            jobs = sp.value_load(jti[0:1, MAX_JOBS:MAX_JOBS + 1], min_val=NE, max_val=NE + 3)
            with sp.Fori(1, jobs) as i:
                e = sp.value_load(jti[0:1, bass.ds(i, 1)], min_val=0, max_val=NE - 1)
                for u in range(UNITS_FFN):
                    sp.wait_ge(lo_done, i * HALVES_FFN + (n_static_halves + 2 * (last_user(RAW_MOE_SLOT, u) + 1)))
                    job(u, e)
            pe_st.wait(sp, "gb2", 1)
            sp.dma_start(gfin[:, :], a["norm_f_g"].rearrange("(o n) -> o n", o=1).to_broadcast([P, D]))\
                .then_inc(gfin_ld, 16)
            dve_st.wait(sp, "yf")
            sp.dma_start(o["y_prompt"][0], yfin[:, 0, :]).then_inc(y_out, 16)
            sp.dma_start(o["y_sample"][0], yfin[:, 1, :]).then_inc(y_out, 16)
            sp.wait_ge(y_out, 32)
            sp.wait_ge(st_out, 16 * 8)
            sp.wait_ge(m_out, 16 * 4)
            sp.wait_ge(n_out, 16 * 2)

        @block.gpsimd
        def _(pool):
            for l in range(DEPTH):
                dve_st.wait(pool, "mc", l)
                pool.dma_start(o["new_m"][0, l, 0:1, :], mrow[P - 1:P, 0, 0, :]).then_inc(m_out, 16)
                pool.dma_start(o["new_m"][0, l, 1:2, :], mrow[0:1, 1, 0, :]).then_inc(m_out, 16)
                act_st.wait(pool, "stc", l)
                for d in range(2):
                    pool.dma_start(o["new_C"][0, l, d].rearrange("h p e -> p h e"), STC[:, d, :, :])\
                        .then_inc(st_out, 16)
                dve_st.wait(pool, "nr", l)
                pool.dma_start(o["new_n"][0, l].rearrange("d h p -> (d h) p"), nrow[:, :]).then_inc(n_out, 16)
                act_st.wait(pool, "rstc", l)
                for d in range(2):
                    pool.dma_start(o["new_S"][0, l, d].rearrange("h p e -> p h e"), STC[:, d, :, :])\
                        .then_inc(st_out, 16)

        @block.scalar
        def _(act):
            chain = [0]
            pos = [0]

            def link(ins):
                chain[0] += 1
                ins.then_inc(act_chain, 1)
                act.wait_ge(act_chain, chain[0])

            def copy(out, in_, scale=1.0):
                return nc.scalar.activation(out, in_, ACT.Copy, scale=scale)

            def split(n=1):
                for _ in range(n):
                    q = pos[0]
                    u, off, size = halves[q]
                    if off == 0:
                        act.wait_ge(raw_ld[u % RAW], 16 * (u // RAW + 1))
                    if q >= HLS:
                        act.wait_ge(w_used, q - HLS + 1)
                    copy(hi[q % HLS][:, 0:size], raw[u % RAW][:, off:off + size]).then_inc(hi_done, 1)
                    pos[0] += 1

            def rsqrt(src, n, name, l=None):
                link(nc.scalar.activation(ln_v[:, :, 0:n], src, ACT.Ln))
                act_st.done(nc.scalar.activation(rs[:, :, 0:n], ln_v[:, :, 0:n], ACT.Exp, scale=-0.5), name, l)

            def norm_sums(name, l=None):
                for s in range(S):
                    ins = nc.scalar.activation(N1[:, s, :], x[:, s, :], ACT.Square, accum_out=ss[:, s, 0:1])
                act_st.done(ins, name, l)

            def x_hi(k, l):
                dve_st.wait(act, f"h{k}", l)
                for s in range(S):
                    ins = copy(XTh[s][:, :, :], N2[:, s, :, :])
                act_st.done(ins, f"xh{k}", l)

            def n1_tiles(s, k):
                return N1[:, s, k * BLK:(k + 1) * BLK].rearrange("p (t c) -> p t c", c=P)

            def gate_rows(name, l, dst=n1_tiles):
                for s, step in enumerate((name + "a", name)):
                    pe_st.wait(act, step, l)
                    for k in range(2):
                        ins = copy(dst(s, k), tiles(4 + k))
                    act_st.done(ins, step, l)

            def ffn_act(split_half, pace, ns, i, first, silu, hTh, sems):
                silu_sem, prod, tr, hTh_sem = sems
                lag, t_after = pace

                def do_silu(j):
                    w = BLK if j < 5 else F - 5 * BLK
                    act.wait_ge(w_used, i * HALVES_FFN + (first + GATE_END[j] + 1))
                    for s in range(ns):
                        if not (isinstance(i, int) and j == 0):
                            act.wait_ge(prod, i * (6 * ns) + ns * j)
                        nc.scalar.activation(silu[:, s, 0:w], bank(2 * s)[:, 0:w], ACT.Silu)\
                            .then_inc(silu_sem, 1)

                def do_hT(j):
                    nt = 4 if j < 5 else 2
                    for s in range(ns):
                        act.wait_ge(tr, i * (6 * ns) + (ns * j + s + 1))
                        copy(hTh[:, 4 * j:4 * j + nt, s, :], tiles(4 + s)[:, 0:nt, :]).then_inc(hTh_sem, 1)

                for h in range(HALVES_FFN):
                    split_half(h)
                    for j in range(6):
                        if h == GATE_END[j] + lag:
                            do_silu(j)
                    for j in range(6):
                        if h == t_after[j] + lag:
                            do_hT(j)

            pe_st.wait(act, "cols")
            act_st.done(nc.scalar.activation(csil[:, :], bank(5)[:, 0:16], ACT.Silu), "csil")
            dve_st.wait(act, "rnab")
            link(nc.scalar.activation(rtmp[:, :, :], rtmp[:, :, :], ACT.Exp))
            act_st.done(nc.scalar.activation(rtmp[:, :, :], rtmp[:, :, :], ACT.Ln, bias=1.0), "rlp")
            dve_st.wait(act, "rarg")
            act_st.done(nc.scalar.activation(dqk[:, :, :, :], dqk[:, :, :, :], ACT.Exp), "rdec")

            def ada_rows_out(batch):
                act.wait_ge(ada_sum, 2 * ADA_NB * (batch + 1))
                if batch:
                    act.wait_ge(ada_turned, batch)
                copy(adarow[:, :], bank(7)[0:ADA_W, :]).then_inc(ada_rows, 1)

            for l in range(DEPTH):
                if l:
                    dve_st.wait(act, "x2", l - 1)
                else:
                    act.wait_ge(small_ld, 16 * 15)
                norm_sums("sq1", l)
                dve_st.wait(act, "v1", l)
                rsqrt(ss[:, :, 0:1], 1, "rs1", l)
                ada_rows_out(3 * l)
                x_hi(1, l)
                split(1)
                dve_st.wait(act, "gates", l)
                link(nc.scalar.activation(nab[:, :, :], nab[:, :, :], ACT.Exp))
                act_st.done(nc.scalar.activation(lp[:, :, :], nab[:, :, :], ACT.Ln, bias=1.0), "gate_e", l)

                def block_out(b):
                    act.wait_ge(w_used, through("in", l, b))
                    c = b * BLK + (GATES if b >= 4 else 0)
                    copy(p[:, 0, c:c + BLK], bank(b % 2 * 2)).then_inc(in_evA, 1)

                for b in range(8):
                    split(2)
                    if b:
                        block_out(b - 1)
                    split(2)
                block_out(7)
                for h in range(H):
                    nc.scalar.activation(DS[:, h, :], cst[:, C_RELP:C_RELP + P], ACT.Exp,
                                         scale=rlg[:, l, h:h + 1])
                    ins = nc.scalar.activation(TR[:, h, :], cst[:, C_RELM:C_RELM + P], ACT.Exp,
                                               scale=rlg[:, l, H + h:H + h + 1])
                act_st.done(ins, "dse", l)
                dve_st.wait(act, "mc", l)
                act_st.done(nc.scalar.activation(em[:, :, :, :], mrow[:, :, :, :], ACT.Exp, scale=-1.0), "em", l)
                act_st.done(nc.scalar.activation(wi[:, :, :], dm[:, :, :], ACT.Exp), "wi", l)
                act.wait_ge(in_evD, 8 * l + 8)
                act.wait_ge(in_evA, 8 * l + 8)
                nc.scalar.activation(p[:, :, OM:OM + WH], p[:, :, OM:OM + WH], ACT.Sigmoid)
                act_st.done(nc.scalar.activation(p[:, :, GR:GR + WH], p[:, :, GR:GR + WH], ACT.Silu), "sig", l)
                for s in range(S):
                    pe_st.wait(act, f"qk{s}", l)
                    act_st.done(copy(KTt[:, :, :], tiles(3)), f"kt{s}", l)
                    pe_st.wait(act, f"mb{s}", l)
                    if s:
                        dve_st.wait(act, "vw", l)
                    for d in range(2):
                        for h in range(H):
                            ins = nc.scalar.activation(ET[:, d, h, :], tiles(d)[:, h, :], ACT.Exp,
                                                       bias=Ac[:, d, s, h:h + 1])
                    act_st.done(ins, f"et{s}", l)
                    if s == 0:
                        pe_st.wait(act, "cst", l)
                        if l:
                            act.wait_ge(st_out, 16 * 4 * l)
                        for d in range(2):
                            ins = copy(STC[:, d, :, :], tiles(d))
                        act_st.done(ins, "stc", l)
                    pe_st.wait(act, f"qkr{s}", l)
                    act_st.done(copy(KTt[:, :, :], tiles(3)), f"ktr{s}", l)
                    if s == 0:
                        pe_st.wait(act, "rst", l)
                        act.wait_ge(st_out, 16 * (4 * l + 2))
                        for d in range(2):
                            ins = copy(STC[:, d, :, :], tiles(d))
                        act_st.done(ins, "rstc", l)
                ada_rows_out(3 * l + 1)
                gate_rows("gb1", l)
                dve_st.wait(act, "hv", l)
                rsqrt(ss[:, :, :], 8, "hrs", l)
                pe_st.wait(act, "yt", l)
                for s in range(S):
                    for t in range(KT):
                        g = 48 + 4 * l + t if t < H else 56 + 4 * l + t - H
                        ins = copy(XTh[s][:, t, :], tiles(2 * s + t // 4)[:, t % 4, :], colsB[:, g:g + 1])
                act_st.done(ins, "yh", l)
                split(8)
                dve_st.wait(act, "x1", l)
                norm_sums("sq2", l)
                dve_st.wait(act, "v2", l)
                rsqrt(ss[:, :, 0:1], 1, "rs2", l)
                ada_rows_out(3 * l + 2)
                if l == 0:
                    x_hi(2, l)
                    gate_rows("gb2", l)
                    ffn_act(lambda h: split(1), PACE_DENSE, S, 0, ffn_first, silu_d, hTh_d,
                            (ffn_silu, ffn_prod, ffn_tr, ffn_hTh))

            pe_st.wait(act, "nat", 1)
            for s in range(S):
                for k in range(2):
                    ins = copy(nath[:, s, k * BLK:(k + 1) * BLK], bank(2 * s + k))
            act_st.done(ins, "nath", 1)
            dve_st.wait(act, "top", 1)
            act_st.done(nc.scalar.activation(wts[:, 1, :], wts[:, 0, :], ACT.Exp), "we", 1)

            def gather_hi(n):
                act.wait_ge(gath_mm, n + 1)
                for k in range(2):
                    copy(XTh[0][:, 4 * k:4 * k + 4, :], tiles(6 + k)).then_inc(xh_ready, 1)

            def y_hi(n):
                act.wait_ge(w_used, n * HALVES_FFN + n_static_halves)
                act.wait_ge(pt_ready, n)
                for c in range(2):
                    copy(yh[:, c * BLK:(c + 1) * BLK], bank(2 + c), gs[:, 0:1]).then_inc(yh_ready, 1)

            gather_hi(0)
            dve_st.wait(act, "route", 1)
            jobs = act.value_load(jti[0:1, MAX_JOBS:MAX_JOBS + 1], min_val=NE, max_val=NE + 3)
            with act.Fori(0, jobs) as i:
                def split_job(h):
                    u = h // 2
                    if h % 2 == 0:
                        slot = RAW_MOE_SLOT[u]
                        act.wait_ge(moe_ld[slot], i * (16 * RAW_MOE_SLOT.count(slot))
                                    + 16 * RAW_MOE_SLOT[:u + 1].count(slot))
                    act.wait_ge(w_used, i * HALVES_FFN + (n_static_halves + h - HLS_MOE + 1))
                    copy(hi[h % HLS_MOE][:, :],
                         raw[RAW_MOE_SLOT[u]][:, h % 2 * HALF:(h % 2 + 1) * HALF]).then_inc(hi_done, 1)
                    if h == Y_AT:
                        y_hi(i)
                    if h == GATHER_AFTER + PACE_JOB[0]:
                        gather_hi(i + 1)

                ffn_act(split_job, PACE_JOB, 1, i, n_static_halves, silu_m, hTh_m, (job_silu, job_prod, job_tr, job_hTh))
            y_hi(jobs)

            gate_rows("gb2", 1, lambda s, k: N2[:, s, 4 * k:4 * k + 4, :])
            dve_st.wait(act, "x2", 1)
            norm_sums("sqf")
            dve_st.wait(act, "vf")
            rsqrt(ss[:, :, 0:1], 1, "rsf")

        @block.vector
        def _(dve):
            chain = [0]
            pos = [0]
            v = nc.vector

            def link(ins):
                chain[0] += 1
                ins.then_inc(dve_chain, 1)
                dve.wait_ge(dve_chain, chain[0])

            def split(n=1):
                for _ in range(n):
                    q = pos[0]
                    u, off, size = halves[q]
                    dve.wait_ge(hi_done, q + 1)
                    v.tensor_tensor(lo[q % HLS][:, 0:size], raw[u % RAW][:, off:off + size],
                                    hi[q % HLS][:, 0:size].bitcast(F32), ALU.subtract).then_inc(lo_done, 1)
                    pos[0] += 1

            def refine(n):
                r_, t_, v_ = rs[:, :, 0:n], rs2[:, :, 0:n], ss[:, :, 0:n]
                link(v.tensor_tensor(t_, r_, r_, ALU.mult))
                link(v.tensor_tensor(t_, t_, v_, ALU.mult))
                link(v.tensor_scalar(t_, t_, -0.5, 1.5, ALU.mult, ALU.add))
                link(v.tensor_tensor(r_, r_, t_, ALU.mult))

            def negative_abs(out, z):
                return v.scalar_tensor_tensor(out=out, in0=z, scalar=-1.0, in1=z, op0=ALU.mult, op1=ALU.min)

            def log_sigmoid(out, z, softplus):
                return v.scalar_tensor_tensor(out=out, in0=z, scalar=0.0, in1=softplus, op0=ALU.min,
                                              op1=ALU.subtract)

            def mean(n, width, name, l=None):
                dve_st.done(v.tensor_scalar(ss[:, :, 0:n], ss[:, :, 0:n], 1.0 / width, EPS, ALU.mult, ALU.add),
                            name, l)

            def modulation(batch):
                dve.wait_ge(ada_turned, batch + 1)
                l, b = batch // 3, batch % 3 * ADA_NB
                bias = colsA[:, 48 * l + 4 * b:48 * l + 4 * (b + ADA_NB)]
                v.tensor_tensor(
                    modc[l][:, 4 * b:4 * (b + ADA_NB), :].rearrange("p (b t) s -> p b t s", t=4),
                    bank(7)[:, 0:4 * ADA_W].rearrange("p (t b s) -> p b t s", t=4, s=S),
                    bias.rearrange("p (b t o) -> p b t o", t=4, o=1).to_broadcast([P, ADA_NB, 4, S]), ALU.add)\
                    .then_inc(ada_cols, 1)

            def norm(k, l):
                act_st.wait(dve, f"sq{k}", l)
                mean(1, D, f"v{k}", l)
                act_st.wait(dve, f"rs{k}", l)
                refine(1)
                for s in range(S):
                    ins = v.tensor_scalar(N1[:, s, :], x[:, s, :], rs[:, s, 0:1], None, ALU.mult)
                dve_st.done(ins, f"xn{k}", l)
                batch = 3 * l + (0 if k == 1 else 2)
                modulation(batch)
                dve.wait_ge(ada_cols, batch + 1)
                g0 = (16 if k == 1 else 32) + 8 * l
                comp = 1 if k == 1 else 4
                dve_st.done(v.scalar_tensor_tensor(
                    out=scol[:, :, :], in0=modc[l][:, 8 * comp:8 * comp + 8, :], scalar=1.0,
                    in1=colsB[:, g0:g0 + 8].rearrange("p (t o) -> p t o", o=1).to_broadcast([P, KT, S]),
                    op0=ALU.add, op1=ALU.mult), f"mod{k}", l)
                dve_st.wait(dve, f"mod{k}", l)
                pe_st.wait(dve, f"xt{k}", l)
                shift = 0 if k == 1 else 24
                for s in range(S):
                    for t in range(KT):
                        ins = v.tensor_scalar(N2[:, s, t, :], tiles(2 * s + t // 4)[:, t % 4, :],
                                              scol[:, t, s:s + 1], modc[l][:, shift + t, s:s + 1],
                                              ALU.mult, ALU.add)
                dve_st.done(ins, f"h{k}", l)
                if (k, l) != (2, 1):
                    act_st.wait(dve, f"xh{k}", l)
                    for s in range(S):
                        ins = v.tensor_tensor(XTl[s][:, :, :], N2[:, s, :, :], XTh[s][:, :, :].bitcast(F32),
                                              ALU.subtract)
                    dve_st.done(ins, f"xl{k}", l)

            def residual(banks, summed, name, l):
                for n, (s, c, bk) in enumerate(banks):
                    cols = slice(c * BLK, (c + 1) * BLK)
                    dve.wait_ge(w_used, summed(s, c))
                    link(v.tensor_tensor(upd[:, n % 2, :], bank(bk), N1[:, s, cols], ALU.mult))
                    ins = v.tensor_tensor(x[:, s, cols], x[:, s, cols], upd[:, n % 2, :], ALU.add)
                dve_st.done(ins, name, l)

            def ffn_dve(split_half, pace, ns, i, first, silu, act_t, hTh, hTl, sems):
                silu_sem, prod, tr, hTh_sem, hTl_sem = sems
                lag, t_after = pace

                def do_prod(j):
                    w = BLK if j < 5 else F - 5 * BLK
                    for s in range(ns):
                        dve.wait_ge(silu_sem, i * (6 * ns) + (ns * j + s + 1))
                        dve.wait_ge(w_used, i * HALVES_FFN + (first + UP_END[j] + 1))
                        if not (isinstance(i, int) and j == 0):
                            dve.wait_ge(tr, i * (6 * ns) + ns * j)
                        v.tensor_tensor(act_t[:, s, 0:w], bank(2 * s + 1)[:, 0:w], silu[:, s, 0:w], ALU.mult)\
                            .then_inc(prod, 1)

                def do_hT(j):
                    nt = 4 if j < 5 else 2
                    for s in range(ns):
                        dve.wait_ge(hTh_sem, i * (6 * ns) + (ns * j + s + 1))
                        v.tensor_tensor(hTl[:, 4 * j:4 * j + nt, s, :], tiles(4 + s)[:, 0:nt, :],
                                        hTh[:, 4 * j:4 * j + nt, s, :].bitcast(F32), ALU.subtract)\
                            .then_inc(hTl_sem, 1)

                for h in range(HALVES_FFN):
                    split_half(h)
                    for j in range(6):
                        if h == UP_END[j] + lag:
                            do_prod(j)
                    for j in range(6):
                        if h == t_after[j] + lag:
                            do_hT(j)

            dve.wait_ge(small_ld, 16 * 15)
            v.tensor_copy(identb[:, :], ident)
            v.tensor_scalar(negm[:, 0, :], trif, 1.0, BIG, ALU.subtract, ALU.mult)
            v.tensor_scalar(negm[:, 1, :], trib, 1.0, BIG, ALU.subtract, ALU.mult)
            dve_st.done(v.memset(m0r[:, :, :], 0.0), "prep")
            pe_st.wait(dve, "cols")
            v.tensor_copy(colsA[:, :], bank(4)[:, 0:96])
            act_st.wait(dve, "csil")
            v.tensor_copy(colsB[:, :], bank(5)[:, 0:80])
            link(v.memset(cond[:, :, :], 0.0))
            dve_st.done(v.tensor_copy(cond[:, :, ADA_W - S:ADA_W], csil[:, :].rearrange("p (s k) -> p k s", s=S)),
                        "cond")
            dve_st.done(negative_abs(rtmp[:, :, :], retl[:, :, :]), "rnab")
            act_st.wait(dve, "rlp")
            link(log_sigmoid(rlg[:, :, :], retl[:, :, :], rtmp[:, :, :]))
            for d in range(4):
                ins = v.tensor_scalar(dqk[:, :, d, :], rlg[:, :, d % 2 * H:(d % 2 + 1) * H],
                                      cst[:, C_POS + d:C_POS + d + 1], None, ALU.mult)
            dve_st.done(ins, "rarg")

            for l in range(DEPTH):
                norm(1, l)

                split(1)
                dve.wait_ge(w_used, through("gates", l, 0))
                link(v.tensor_tensor(gt[:, :, :], bank(4)[:, 0:S * GATES].rearrange("p (s g) -> p s g", s=S),
                                     bg[:, l:l + 1, :].to_broadcast([P, S, GATES]), ALU.add))
                dve_st.done(negative_abs(nab[:, :, :], gt[:, :, 2 * H:4 * H]), "gates", l)

                def by_direction(t):
                    return t.rearrange("p s (d h) -> p d s h", d=2)

                def block_out(b):
                    dve.wait_ge(w_used, through("in", l, b))
                    c = b * BLK + (GATES if b >= 4 else 0)
                    v.tensor_copy(p[:, 1, c:c + BLK], bank(b % 2 * 2 + 1)).then_inc(in_evD, 1)

                for b in range(8):
                    split(2)
                    if b:
                        block_out(b - 1)
                    split(2)
                    if b == 0:
                        act_st.wait(dve, "gate_e", l)
                        for d in range(2):
                            ins = log_sigmoid(FL[:, d, :, :], gt[:, :, (2 + d) * H:(3 + d) * H],
                                              lp[:, :, d * H:(d + 1) * H])
                        dve_st.done(ins, "fl", l)
                    if b == 2:
                        pe_st.wait(dve, "bcum", l)
                        link(v.tensor_copy(Bc[:, :, :, :],
                                           bank(5)[:, 0:16].rearrange("p (d s h) -> p d s h", d=2, s=S)))
                        for d in range(2):
                            ins = v.tensor_tensor(Ac[:, d, :, :], gt[:, :, d * H:(d + 1) * H], Bc[:, d, :, :],
                                                  ALU.subtract)
                        dve_st.done(ins, "ba", l)
                    if b == 4:
                        pe_st.wait(dve, "arow", l)
                        dve.wait_ge(small_ld, 16 * 19)
                        link(v.tensor_copy(AR[:, :, :],
                                           bank(5)[0:2 * H, 0:2 * P].rearrange("p (d c) -> p d c", d=2)))
                        v.tensor_tensor_scan(MR[:, 0, :], AR[:, 0, :], AR[:, 0, :], m0r[:, l, 0:1],
                                             ALU.max, ALU.max)
                        link(v.tensor_tensor_scan(MR[:, 1, ::-1], AR[:, 1, ::-1], AR[:, 1, ::-1],
                                                  m0r[:, l, 1:2], ALU.max, ALU.max))
                        dve_st.done(v.tensor_scalar(nMR[:, :, :], MR[:, :, :], -1.0, None, ALU.mult), "mr", l)
                    if b == 6:
                        pe_st.wait(dve, "mcol", l)
                        if l:
                            dve.wait_ge(m_out, 32 * l)
                        link(v.tensor_copy(Mc[:, :, :, :],
                                           bank(5)[:, 0:16].rearrange("p (d s h) -> p d s h", d=2, s=S)))
                        v.tensor_tensor(dm[:, :, :], m0b[:, l, :, :], Mc[:, :, 1, :], ALU.subtract)
                        dve_st.done(v.tensor_tensor(mrow[:, :, :, :], Bc[:, :, :, :], Mc[:, :, :, :], ALU.add),
                                    "mc", l)
                block_out(7)
                dve.wait_ge(in_evD, 8 * l + 8)
                dve.wait_ge(in_evA, 8 * l + 8)

                qk = p[:, 1, QR:QR + 2 * WH].rearrange("p (h a f c) -> p h a f c", a=2, f=2, c=32)
                x1, x2 = qk[:, :, :, 0, :], qk[:, :, :, 1, :]

                def table(c0):
                    t = cst[:, c0:c0 + 64].rearrange("p (o a c) -> p o a c", o=1, a=2)
                    return t.to_broadcast([P, 2 * H, 2, 32])

                v.tensor_tensor(rope1[:, :, :, :], x2, table(C_SIN), ALU.mult)
                link(v.tensor_tensor(rope2[:, :, :, :], x1, table(C_SIN), ALU.mult))
                v.tensor_tensor(x1, x1, table(C_COS), ALU.mult)
                link(v.tensor_tensor(x2, x2, table(C_COS), ALU.mult))
                v.tensor_tensor(x1, x1, rope1[:, :, :, :], ALU.subtract)
                dve_st.done(v.tensor_tensor(x2, x2, rope2[:, :, :, :], ALU.add), "rope", l)
                dve_st.wait(dve, "rope", l)
                act_st.wait(dve, "dse", l)
                for t, c0 in ((DS, C_TRIF), (TR, C_TRIB)):
                    mask = cst[:, c0:c0 + P].rearrange("p (o c) -> p o c", o=1).to_broadcast([P, H, P])
                    ins = v.tensor_tensor(t[:, :, :], t[:, :, :], mask, ALU.mult)
                link(ins)
                link(v.tensor_tensor(DS[:, :, :], DS[:, :, :], TR[:, :, :], ALU.add))

                for s in range(S):
                    pe_st.wait(dve, f"qk{s}", l)
                    dve_st.done(v.tensor_copy(QT[:, :, :], tiles(2)), f"qt{s}", l)
                    act_st.wait(dve, f"et{s}", l)
                    pe_st.wait(dve, f"pqk{s}", l)
                    for d in range(2):
                        ins = v.scalar_tensor_tensor(out=ST[:, d, :, :], in0=tiles(4), scalar=SCALE,
                                                     in1=ET[:, d, :, :], op0=ALU.mult, op1=ALU.mult)
                    dve_st.done(ins, f"st{s}", l)
                    if s == 0:
                        for d, end in ((0, P - 1), (1, 0)):
                            v.tensor_scalar(wn[:, d, :], ET[:, d, :, end], SCALE, None, ALU.mult)
                            for h in range(H):
                                ins = v.tensor_scalar(VW[:, d, h, :], p[:, 0, VM + h * P:VM + (h + 1) * P],
                                                      ET[:, d, h, end:end + 1], SCALE, ALU.mult, ALU.mult)
                        dve_st.done(ins, "vw", l)
                    pe_st.wait(dve, f"num{s}", l)
                    act_st.wait(dve, "wi", l)

                    def small8(c0):
                        return bank(4)[:, c0:c0 + 8].rearrange("p (d h) -> p d h", d=2)

                    if s == 0:
                        link(v.tensor_copy(dent[:, :, :], small8(0)))
                    else:
                        link(v.tensor_tensor(dent[:, :, :], small8(8), wi[:, :, :], ALU.mult))
                        link(v.tensor_tensor(dent[:, :, :], small8(0), dent[:, :, :], ALU.add))
                    link(v.scalar_tensor_tensor(out=den[:, :, :], in0=dent[:, :, :], scalar=-1.0,
                                                in1=dent[:, :, :], op0=ALU.mult, op1=ALU.max))
                    link(v.tensor_tensor(den[:, :, :], den[:, :, :], em[:, :, s, :], ALU.max))
                    link(v.reciprocal(rden[:, :, s, :], den[:, :, :]))
                    terms = [(5, lambda h: rden[:, 0, s, h:h + 1]), (6, lambda h: rden[:, 1, s, h:h + 1])]
                    if s == 1:
                        link(v.tensor_tensor(wrd[:, :, :], wi[:, :, :], rden[:, :, 1, :], ALU.mult))
                        terms += [(2, lambda h: wrd[:, 0, h:h + 1]), (3, lambda h: wrd[:, 1, h:h + 1])]

                    def sum_terms(terms, h0, first):
                        for n, (bk, scalar) in enumerate(terms):
                            for h in range(H):
                                y = yy[:, s, h0 + h, :]
                                if n == 0 and first:
                                    ins = v.tensor_scalar(y, tiles(bk)[:, h, :], scalar(h), None, ALU.mult)
                                else:
                                    ins = v.scalar_tensor_tensor(out=y, in0=tiles(bk)[:, h, :], scalar=scalar(h),
                                                                 in1=y, op0=ALU.mult, op1=ALU.add)
                            if n + 1 < len(terms):
                                link(ins)
                        return ins

                    dve_st.done(sum_terms(terms, 0, True), f"y{s}", l)
                    if s == 0:
                        pe_st.wait(dve, "nst", l)
                        dve_st.done(v.tensor_copy(ncol[:, :], bank(4)[:, 0:8]), "nc", l)
                        pe_st.wait(dve, "nrow", l)
                        if l:
                            dve.wait_ge(n_out, 16 * l)
                        dve_st.done(v.tensor_copy(nrow[:, :], bank(4)[0:2 * H, 0:P]), "nr", l)
                    pe_st.wait(dve, f"qkr{s}", l)
                    dve_st.done(v.tensor_copy(QT[:, :, :], tiles(2)), f"qtr{s}", l)
                    pe_st.wait(dve, f"pr{s}", l)
                    dve_st.done(v.scalar_tensor_tensor(out=ST[:, 0, :, :], in0=tiles(4), scalar=SCALE,
                                                       in1=DS[:, :, :], op0=ALU.mult, op1=ALU.mult),
                                f"str{s}", l)
                    if s == 0:
                        pe_st.wait(dve, "cst", l)
                        act_st.wait(dve, "rdec")
                        for d in range(2):
                            for h in range(H):
                                ins = v.tensor_scalar(VW[:, d, h, :], p[:, 0, VR + h * P:VR + (h + 1) * P],
                                                      dqk[:, l, 2 + d, h:h + 1], SCALE, ALU.mult, ALU.mult)
                        dve_st.done(ins, "vwr", l)
                    pe_st.wait(dve, f"o{s}", l)
                    ins = v.tensor_copy(yy[:, s, H:2 * H, :], tiles(5))
                    if s == 1:
                        link(ins)
                        ins = sum_terms([(6, lambda h: dqk[:, l, 0, h:h + 1]), (0, lambda h: dqk[:, l, 1, h:h + 1])],
                                        H, False)
                    dve_st.done(ins, f"yr{s}", l)

                modulation(3 * l + 1)
                dve_st.wait(dve, "yr1", l)
                for s in range(S):
                    link(v.tensor_tensor(ysq[:, :, :], yy[:, s, :, :], yy[:, s, :, :], ALU.mult))
                    link(v.tensor_reduce(ss[:, s, :], ysq[:, :, :], AX_X, ALU.add))
                mean(8, P, "hv", l)
                act_st.wait(dve, "hrs", l)
                act_st.wait(dve, "sig", l)
                refine(8)
                for s in range(S):
                    for h in range(2 * H):
                        c = OM + h * P if h < H else GR + (h - H) * P
                        ins = v.scalar_tensor_tensor(out=yy[:, s, h, :], in0=yy[:, s, h, :],
                                                     scalar=rs[:, s, h:h + 1], in1=p[:, s, c:c + P],
                                                     op0=ALU.mult, op1=ALU.mult)
                dve_st.done(ins, "yn", l)
                pe_st.wait(dve, "yt", l)
                act_st.wait(dve, "yh", l)
                for s in range(S):
                    for t in range(KT):
                        g = 48 + 4 * l + t if t < H else 56 + 4 * l + t - H
                        ins = v.scalar_tensor_tensor(out=XTl[s][:, t, :], in0=tiles(2 * s + t // 4)[:, t % 4, :],
                                                     scalar=colsB[:, g:g + 1],
                                                     in1=XTh[s][:, t, :].bitcast(F32), op0=ALU.mult,
                                                     op1=ALU.subtract)
                dve_st.done(ins, "yl", l)
                split(8)
                act_st.wait(dve, "gb1", l)
                residual([(s, c, 2 * c + s) for c in range(2) for s in range(S)], 
                         lambda s, c: through("out", l, c), "x1", l)
                norm(2, l)
                if l == 0:
                    ffn_dve(lambda h: split(1), PACE_DENSE, S, 0, ffn_first, silu_d, act_d, hTh_d, hTl_d,
                            (ffn_silu, ffn_prod, ffn_tr, ffn_hTh, ffn_hTl))
                    act_st.wait(dve, "gb2", l)
                    residual([(s, c, 2 * s + c) for s in range(S) for c in range(2)], 
                             lambda s, c: ffn_first + HALVES_FFN, "x2", l)

            v.memset(N1[:, :, :], 0.0)
            act_st.wait(dve, "nath", 1)
            for s in range(S):
                for k in range(2):
                    c = slice(k * BLK, (k + 1) * BLK)
                    ins = v.tensor_tensor(natl[:, s, c], bank(2 * s + k), nath[:, s, c].bitcast(F32), ALU.subtract)
            dve_st.done(ins, "natl", 1)
            pe_st.wait(dve, "router", 1)
            link(v.tensor_copy(lg[:, :, :], bank(4)[:, 0:S * NE].rearrange("p (s e) -> p s e", s=S)))
            for s in range(S):
                link(v.max(mx[:, s, :], lg[:, s, :]))
                link(v.max_index(mi[:, s, :], mx[:, s, :], lg[:, s, :]))
            v.tensor_copy(mif[:, :, :], mi[:, :, 0:2])
            ins = v.tensor_tensor(wts[:, 0, :], mx[:, :, 1], mx[:, :, 0], ALU.subtract)
            dve_st.done(ins, "top", 1)
            dve_st.wait(dve, "top", 1)
            for s in range(S):
                for t, k in ((M1, 0), (M2, 1)):
                    ins = v.tensor_scalar(t[:, s, :], cst[:, C_IOTA:C_IOTA + NE], mif[:, s, k:k + 1], None,
                                          ALU.is_equal)
            link(ins)
            dve_st.done(v.tensor_tensor(MK[:, :, :], M1[:, :, :], M2[:, :, :], ALU.add), "masks", 1)
            act_st.wait(dve, "we", 1)
            link(v.tensor_scalar(wts[:, 0, :], wts[:, 1, :], 1.0, None, ALU.add))
            link(v.reciprocal(wts[:, 0, :], wts[:, 0, :]))
            link(v.tensor_tensor(wts[:, 1, :], wts[:, 1, :], wts[:, 0, :], ALU.mult))
            dve.wait_ge(st_out, 16 * 8)
            v.memset(PT[:, :, :].bitcast(F32), 0.0)
            v.memset(gs[:, :], 0.0)
            pe_st.wait(dve, "rank", 1)
            link(v.tensor_scalar(nb[:, :], bank(5)[:, 16:24], float(P), 1.0, ALU.is_gt, ALU.add))
            link(v.tensor_tensor_scan(st_i[:, :], cst[:, C_ONES:C_ONES + NE], nb[:, :], 0.0, ALU.mult, ALU.add))
            link(v.tensor_copy(jtf[:, MAX_JOBS:MAX_JOBS + 1], st_i[0:1, NE - 1:NE]))
            link(v.tensor_tensor(st_i[:, :], st_i[:, :], nb[:, :], ALU.subtract))
            link(v.tensor_scalar(nb[:, :], st_i[:, :], float(P), -1.0, ALU.mult, ALU.add))
            for s in range(S):
                ins = v.tensor_tensor(slots[:, s, :], bank(5)[:, 8 * s:8 * s + 8], nb[:, :], ALU.add)
            link(ins)
            for k, t in enumerate((M1, M2)):
                link(v.tensor_tensor(stmp[:, :, :], t[:, :, :], slots[:, :, :], ALU.mult))
                link(v.tensor_reduce(keys[:, k, :], stmp[:, :, :], AX_X, ALU.add))
            starts = st_i[0:1, :].rearrange("p (o e) -> p o e", o=1).to_broadcast([1, MAX_JOBS, NE])
            number = cst[0:1, C_IOTA:C_IOTA + MAX_JOBS].rearrange("p (j o) -> p j o", o=1)
            link(v.tensor_tensor(jt[:, :, :], starts, number.to_broadcast([1, MAX_JOBS, NE]), ALU.is_le))
            link(v.tensor_reduce(jtf[:, 0:MAX_JOBS], jt[:, :, :], AX_X, ALU.add))
            link(v.tensor_scalar(jtf[:, 0:MAX_JOBS], jtf[:, 0:MAX_JOBS], 1.0, None, ALU.subtract))
            dve_st.done(v.tensor_copy(jti[:, :], jtf[:, :]), "route", 1)

            def select():
                for s in range(S):
                    v.tensor_scalar(P1[:, s, :], iota, keys[:, 0, s:s + 1], None, ALU.is_equal)
                    ins = v.tensor_scalar(P2[:, s, :], iota, keys[:, 1, s:s + 1], None, ALU.is_equal)
                ins.then_inc(sel_step, 1)

            def select_sum():
                v.tensor_tensor(Pr[:, :, :], P1[:, :, :], P2[:, :, :], ALU.add).then_inc(sel_ready, 1)
                v.tensor_scalar(keys[:, :, :], keys[:, :, :], float(P), None, ALU.subtract)\
                    .then_inc(key_step, 1)

            def gather_lo(n):
                dve.wait_ge(xh_ready, 2 * n + 2)
                for k in range(2):
                    v.tensor_tensor(XTl[0][:, 4 * k:4 * k + 4, :], tiles(6 + k),
                                    XTh[0][:, 4 * k:4 * k + 4, :].bitcast(F32), ALU.subtract)\
                        .then_inc(xl_ready, 1)

            def y_lo(n):
                dve.wait_ge(yh_ready, n * 2 + 2)
                for c in range(2):
                    cols = slice(c * BLK, (c + 1) * BLK)
                    v.scalar_tensor_tensor(out=yl[:, cols], in0=bank(2 + c), scalar=gs[:, 0:1],
                                           in1=yh[:, cols].bitcast(F32), op0=ALU.mult, op1=ALU.subtract)\
                        .then_inc(yl_ready, 1)

            def accumulate(n, s):
                for c in range(2):
                    dve.wait_ge(scat_mm, n * 4 + (2 * s + c + 1))
                    v.tensor_tensor(N1[:, s, c * BLK:(c + 1) * BLK], bank(6 + c),
                                    N1[:, s, c * BLK:(c + 1) * BLK], ALU.add).then_inc(acc_done, 1)

            select()
            dve.wait_ge(sel_step, 1)
            select_sum()
            gather_lo(0)
            dve_st.wait(dve, "route", 1)
            jobs = dve.value_load(jti[0:1, MAX_JOBS:MAX_JOBS + 1], min_val=NE, max_val=NE + 3)
            with dve.Fori(0, jobs) as i:
                def split_job(h):
                    u = h // 2
                    dve.wait_ge(hi_done, i * HALVES_FFN + (n_static_halves + h + 1))
                    q = h % HLS_MOE
                    v.tensor_tensor(lo[q][:, :], raw[RAW_MOE_SLOT[u]][:, h % 2 * HALF:(h % 2 + 1) * HALF],
                                    hi[q][:, :].bitcast(F32), ALU.subtract).then_inc(lo_done, 1)
                    if h == Y_AT + 1:
                        y_lo(i)
                    for part in range(2):
                        if h == SCATTER_AFTER[part] + PACE_JOB[0]:
                            accumulate(i, part)
                    if h == PT_AFTER + PACE_JOB[0]:
                        dve.wait_ge(ptr_mm, i + 1)
                        v.tensor_copy(PT[:, :, :], bank(5)[:, 0:S * P].rearrange("p (s t) -> p s t", s=S))
                        v.tensor_copy(gs[:, :], bank(5)[:, S * P:S * P + 1]).then_inc(pt_ready, 1)
                        dve.wait_ge(key_step, i + 1)
                        select()
                        dve.wait_ge(sel_step, i + 2)
                        select_sum()
                    if h == GATHER_AFTER + PACE_JOB[0]:
                        gather_lo(i + 1)

                ffn_dve(split_job, PACE_JOB, 1, i, n_static_halves, silu_m, act_m, hTh_m, hTl_m,
                        (job_silu, job_prod, job_tr, job_hTh, job_hTl))
            y_lo(jobs)
            accumulate(jobs, 0)
            accumulate(jobs, 1)

            act_st.wait(dve, "gb2", 1)
            dve.wait_ge(acc_done, jobs * 4 + 4)
            link(v.tensor_tensor(N1[:, :, :], N1[:, :, :], N2[:, :, :, :].rearrange("p s t c -> p s (t c)"),
                                 ALU.mult))
            dve_st.done(v.tensor_tensor(x[:, :, :], x[:, :, :], N1[:, :, :], ALU.add), "x2", 1)
            act_st.wait(dve, "sqf")
            mean(1, D, "vf")
            act_st.wait(dve, "rsf")
            refine(1)
            dve.wait_ge(gfin_ld, 16)
            for s in range(S):
                ins = v.scalar_tensor_tensor(out=yfin[:, s, :], in0=x[:, s, :], scalar=rs[:, s, 0:1],
                                             in1=gfin[:, :], op0=ALU.mult, op1=ALU.mult)
            dve_st.done(ins, "yf")

        @block.tensor
        def _(pe):
            mm = nc.tensor.matmul
            pos = [0]

            def take():
                q = pos[0]
                pe.wait_ge(lo_done, q + 1)
                pos[0] += 1
                return q % HLS

            def product(out, xh, xl, q, cols, start, stop):
                mm(out, xh, hi[q][:, cols], start=start, stop=False)
                mm(out, xh, lo[q][:, cols], start=False, stop=False)
                return mm(out, xl, hi[q][:, cols], start=False, stop=stop)

            def turn(out, in_, n=P):
                return nc.tensor.transpose(out, in_, cst[0:n, C_ID:C_ID + n])

            def gate_rows(name, l, comp):
                for s, step in enumerate((name + "a", name)):
                    if s:
                        act_st.wait(pe, name + "a", l)
                    for t in range(KT):
                        ins = mm(tiles(4 + t // 4)[:, t % 4, :],
                                 modc[l][:, 8 * comp + t, s:s + 1].to_broadcast([P, P]), ident,
                                 start=True, stop=True)
                    pe_st.done(ins, step, l)

            def norm_turns(k, l):
                dve_st.wait(pe, f"xn{k}", l)
                for s in range(S):
                    for t in range(KT):
                        ins = turn(tiles(2 * s + t // 4)[:, t % 4, :], N1[:, s, t * P:(t + 1) * P])
                pe_st.done(ins, f"xt{k}", l)

            def ffn_pe(take_half, pace, ns, i, xt, act_t, hTh, hTl, down_banks, sems, extra):
                silu_sem, prod, tr, hTl_sem = sems
                t_after = pace[1]

                def turns(j):
                    nt = 4 if j < 5 else 2
                    for s in range(ns):
                        pe.wait_ge(prod, i * (6 * ns) + (ns * j + s + 1))
                        if not (isinstance(i, int) and j == 0):
                            pe.wait_ge(hTl_sem, i * (6 * ns) + ns * j)
                        for t in range(nt):
                            ins = turn(tiles(4 + s)[:, t, :], act_t[:, s, t * P:(t + 1) * P])
                        ins.then_inc(tr, 1)

                for h in range(HALVES_FFN):
                    if h < 44:
                        j = h // 8 if h < 40 else 5
                        r, per, w = (h % 8, 4, BLK) if h < 40 else (h - 40, 2, F - 5 * BLK)
                        is_up, part = r // per, r % per
                        kts = KT // per
                        if part == 0 and not (isinstance(i, int) and j == 0):
                            pe.wait_ge(prod if is_up else silu_sem, i * (6 * ns) + ns * j)
                        q = take_half(h)
                        for s in range(ns):
                            out = bank(2 * s + is_up)[:, 0:w]
                            for k in range(kts):
                                kt = part * kts + k
                                ins = product(out, xt[s][0][:, kt, :], xt[s][1][:, kt, :], q,
                                              slice(k * w, (k + 1) * w), kt == 0, kt == KT - 1)
                        release(ins)
                    else:
                        t = h - 44
                        if t == 0:
                            extra("down")
                        if t % 4 == 0:
                            pe.wait_ge(hTl_sem, i * (6 * ns) + ns * (t // 4 + 1))
                        q = take_half(h)
                        for s in range(ns):
                            for c in range(2):
                                ins = product(bank(down_banks[2 * s + c]), hTh[:, t, s, :], hTl[:, t, s, :], q,
                                              slice(c * BLK, (c + 1) * BLK), t == 0, t == FT - 1)
                        release(ins)
                    for j in range(6):
                        if h == t_after[j]:
                            turns(j)
                    extra(h)

            def release(ins):
                ins.then_inc(w_used, 1)

            pe.wait_ge(small_ld, 16 * 15)
            turn(bank(4)[:, 0:96], rowsA[:, :], 96)
            pe_st.done(turn(bank(5)[:, 0:80], rowsB[:, :], 80), "cols")
            dve_st.wait(pe, "cond")
            ada_at = [0]
            ada_unit = [n for n, u in enumerate(units) if u[0] == "ada"]

            def fill(step, l):
                for _ in range(ADA_FILL.get((step, l), 0)):
                    k, kt = divmod(ada_at[0], KT)
                    batch, j = divmod(k, ADA_NB)
                    u = ada_unit[2 * k + kt // 4]
                    if batch and j == kt == 0:
                        pe.wait_ge(ada_cols, batch)
                    if kt % 4 == 0:
                        pe.wait_ge(raw_ld[u % RAW], 16 * (u // RAW + 1))
                    c0 = ADA_W - S - S * j
                    ins = mm(bank(7)[0:ADA_W, :], cond[:, kt, c0:c0 + ADA_W],
                             raw[u % RAW][:, kt % 4 * BLK:(kt % 4 + 1) * BLK],
                             start=(j == kt == 0), stop=(j == ADA_NB - 1 and kt == KT - 1))
                    if kt % 4 == 3:
                        ins.then_inc(ada_sum, 1)
                    ada_at[0] += 1

            def ada_turns(batch):
                pe.wait_ge(ada_rows, batch + 1)
                for t in range(4):
                    ins = turn(bank(7)[:, t * ADA_W:(t + 1) * ADA_W], adarow[:, t * P:(t + 1) * P], ADA_W)
                ins.then_inc(ada_turned, 1)

            fill("first", 0)
            for l in range(DEPTH):
                if l:
                    dve_st.wait(pe, "x2", l - 1)
                norm_turns(1, l)
                ada_turns(3 * l)
                fill("xt1", l)
                dve_st.wait(pe, "xl1", l)
                q = take()
                for s in range(S):
                    for kt in range(KT):
                        ins = product(bank(4)[:, s * GATES:(s + 1) * GATES], XTh[s][:, kt, :], XTl[s][:, kt, :], q,
                                      slice(kt * GATES, (kt + 1) * GATES), kt == 0, kt == KT - 1)
                release(ins)
                for b in range(8):
                    n = 8 * l + b
                    if n >= 2:
                        pe.wait_ge(in_evA, n - 1)
                        pe.wait_ge(in_evD, n - 1)
                    for k in range(4):
                        q = take()
                        for s in range(S):
                            for t in range(2):
                                kt = 2 * k + t
                                ins = product(bank(b % 2 * 2 + s), XTh[s][:, kt, :], XTl[s][:, kt, :], q,
                                              slice(t * BLK, (t + 1) * BLK), kt == 0, kt == KT - 1)
                        release(ins)
                    if b == 1:
                        dve_st.wait(pe, "fl", l)
                        for d, tri in enumerate((trif, trib)):
                            ins = mm(bank(5)[:, 8 * d:8 * d + 8], tri, FL[:, d, :, :], start=True, stop=True)
                        pe_st.done(ins, "bcum", l)
                    if b == 3:
                        dve_st.wait(pe, "ba", l)
                        for d in range(2):
                            ins = turn(bank(5)[0:2 * H, d * P:(d + 1) * P],
                                       Ac[:, d, :, :].rearrange("p s h -> p (s h)"))
                        pe_st.done(ins, "arow", l)
                    if b == 5:
                        dve_st.wait(pe, "mr", l)
                        for d in range(2):
                            ins = turn(bank(5)[:, 8 * d:8 * d + 8], MR[:, d, :], 2 * H)
                        pe_st.done(ins, "mcol", l)

                pe.wait_ge(in_evA, 8 * l + 8)
                pe.wait_ge(in_evD, 8 * l + 8)
                pe.wait_ge(state_ld, 32 * (l + 1))

                def head(s, c0, h):
                    return p[:, s, c0 + h * P:c0 + (h + 1) * P]

                def turn_qk(s, qc, kc, name):
                    for bk, c0 in ((2, qc), (3, kc)):
                        for h in range(H):
                            ins = turn(tiles(bk)[:, h, :], head(s, c0, h))
                    pe_st.done(ins, name, l)
                    fill(name, l)

                def scores(name):
                    for h in range(H):
                        ins = mm(tiles(4)[:, h, :], KTt[:, h, :], QT[:, h, :], start=True, stop=True)
                    pe_st.done(ins, name, l)
                    fill(name, l)

                for s in range(S):
                    if s:
                        dve_st.wait(pe, "qtr0", l)
                    turn_qk(s, QM, KM, f"qk{s}")
                    dve_st.wait(pe, "mc", l)
                    if s:
                        act_st.wait(pe, "rstc", l)
                    for d in range(2):
                        mm(bank(d), identb[:, :],
                           negm[:, d:d + 1, :].to_broadcast([P, H, P]), start=True, stop=True)
                        for h in range(H):
                            r = s * H + h
                            ins = mm(tiles(d)[:, h, :], cst[0:2 * H, C_ID + r:C_ID + r + 1].to_broadcast([2 * H, P]),
                                     nMR[:, d, :], start=False, stop=True, skip_group_check=True)
                    pe_st.done(ins, f"mb{s}", l)
                    fill(f"mb{s}", l)
                    act_st.wait(pe, f"kt{s}", l)
                    dve_st.wait(pe, f"qt{s}", l)
                    scores(f"pqk{s}")
                    dve_st.wait(pe, f"st{s}", l)
                    for d in range(2):
                        for h in range(H):
                            mm(tiles(5 + d)[:, h, :], ST[:, d, h, :], head(s, VM, h), start=True, stop=True)
                    for d in range(2):
                        for h in range(H):
                            ins = mm(bank(4)[:, 4 * d + h:4 * d + h + 1], ST[:, d, h, :], cst[:, C_ONES:C_ONES + 1],
                                     start=True, stop=True)
                    if s == 1:
                        for d in range(2):
                            for h in range(H):
                                g = 64 + 8 * l + 4 * d + h
                                mm(tiles(2 + d)[:, h, :], QT[:, h, :], CM[:, d, h, :], start=True, stop=True)
                                ins = mm(bank(4)[:, 8 + 4 * d + h:9 + 4 * d + h], QT[:, h, :], colsB[:, g:g + 1],
                                         start=True, stop=True)
                    pe_st.done(ins, f"num{s}", l)
                    fill(f"num{s}", l)
                    if s == 0:
                        dve_st.wait(pe, "vw", l)
                        act_st.wait(pe, "et0", l)
                        for d in range(2):
                            for h in range(H):
                                ins = mm(tiles(d)[:, h, :], head(0, KM, h), VW[:, d, h, :], start=True, stop=True)
                        pe_st.done(ins, "cst", l)
                        fill("cst", l)
                        dve_st.wait(pe, "y0", l)
                        for d in range(2):
                            for h in range(H):
                                ins = mm(bank(4)[:, 4 * d + h:4 * d + h + 1], head(0, KM, h), wn[:, d, h:h + 1],
                                         start=True, stop=True)
                        pe_st.done(ins, "nst", l)
                        dve_st.wait(pe, "nc", l)
                        pe_st.done(turn(bank(4)[0:2 * H, 0:P], ncol[:, :]), "nrow", l)
                    else:
                        dve_st.wait(pe, "y1", l)
                        dve_st.wait(pe, "rope", l)
                    turn_qk(s, QR, KR, f"qkr{s}")
                    act_st.wait(pe, f"ktr{s}", l)
                    dve_st.wait(pe, f"qtr{s}", l)
                    scores(f"pr{s}")
                    dve_st.wait(pe, f"str{s}", l)
                    for h in range(H):
                        ins = mm(tiles(5)[:, h, :], ST[:, 0, h, :], head(s, VR, h), start=True, stop=True)
                    if s == 1:
                        for d, bk in ((0, 6), (1, 0)):
                            for h in range(H):
                                ins = mm(tiles(bk)[:, h, :], QT[:, h, :], SM[:, d, h, :], start=True, stop=True)
                    pe_st.done(ins, f"o{s}", l)
                    fill(f"o{s}", l)
                    if s == 0:
                        act_st.wait(pe, "stc", l)
                        dve_st.wait(pe, "vwr", l)
                        for d in range(2):
                            for h in range(H):
                                ins = mm(tiles(d)[:, h, :], head(0, KR, h), VW[:, d, h, :], start=True, stop=True)
                        pe_st.done(ins, "rst", l)
                        fill("rst", l)

                ada_turns(3 * l + 1)
                dve_st.wait(pe, "yr1", l)
                pe.wait_ge(ada_cols, 3 * l + 2)
                gate_rows("gb1", l, 2)
                fill("gb1", l)
                dve_st.wait(pe, "yn", l)
                for s in range(S):
                    for t in range(KT):
                        ins = turn(tiles(2 * s + t // 4)[:, t % 4, :], yy[:, s, t, :])
                pe_st.done(ins, "yt", l)
                fill("yt", l)
                dve_st.wait(pe, "yl", l)
                for b in range(2):
                    for k in range(4):
                        q = take()
                        for s in range(S):
                            for t in range(2):
                                kt = 2 * k + t
                                ins = product(bank(2 * b + s), XTh[s][:, kt, :], XTl[s][:, kt, :], q,
                                              slice(t * BLK, (t + 1) * BLK), kt == 0, kt == KT - 1)
                        release(ins)
                fill("x1", l)
                norm_turns(2, l)
                ada_turns(3 * l + 2)
                fill("xt2", l)
                if l == 0:
                    pe.wait_ge(ada_cols, 3 * l + 3)
                    gate_rows("gb2", l, 5)
                    fill("gb2", l)
                    dve_st.wait(pe, "xl2", l)
                    act_st.wait(pe, "gb2", l)

                    def dense_extra(h):
                        if h == "down":
                            pe.wait_ge(ffn_prod, 12)
                        elif h % 2:
                            fill(f"ffn{h // 2}", l)

                    ffn_pe(lambda h: take(), PACE_DENSE, S, 0, list(zip(XTh, XTl)), act_d, hTh_d, hTl_d, (0, 1, 2, 3),
                           (ffn_silu, ffn_prod, ffn_tr, ffn_hTl), dense_extra)
                    fill("x2", l)

            dve_st.wait(pe, "h2", 1)
            for s in range(S):
                for kt in range(KT):
                    ins = mm(bank(4)[:, NE * s:NE * s + NE], N2[:, s, kt, :], wr[:, kt, :],
                             start=(kt == 0), stop=(kt == KT - 1))
            pe_st.done(ins, "router", 1)
            for s in range(S):
                for t in range(KT):
                    ins = turn(tiles(2 * s + t // 4)[:, t % 4, :], N2[:, s, t, :])
            pe_st.done(ins, "nat", 1)
            dve_st.wait(pe, "masks", 1)
            mm(bank(5)[:, 0:8], trif, MK[:, 0, :], start=True, stop=True)
            mm(bank(5)[:, 8:16], trif, MK[:, 1, :], start=True, stop=False)
            mm(bank(5)[:, 8:16], ones, MK[:, 0, :], start=False, stop=True)
            mm(bank(5)[:, 16:24], ones, MK[:, 0, :], start=True, stop=False)
            pe_st.done(mm(bank(5)[:, 16:24], ones, MK[:, 1, :], start=False, stop=True), "rank", 1)

            def gather(n):
                pe.wait_ge(sel_ready, n + 1)
                for t in range(KT):
                    out = tiles(6 + t // 4)[:, t % 4, :]
                    for s in range(S):
                        mm(out, nath[:, s, t * P:(t + 1) * P], Pr[:, s, :], start=(s == 0), stop=False)
                        ins = mm(out, natl[:, s, t * P:(t + 1) * P], Pr[:, s, :], start=False, stop=(s == S - 1))
                ins.then_inc(gath_mm, 1)

            def scatter(n, s):
                pe.wait_ge(yl_ready, n * 2 + 2)
                for c in range(2):
                    if s:
                        pe.wait_ge(acc_done, n * 4 + (c + 1))
                    cols = slice(c * BLK, (c + 1) * BLK)
                    mm(bank(6 + c), PT[:, s, :], yh[:, cols], start=True, stop=False)
                    mm(bank(6 + c), PT[:, s, :], yl[:, cols], start=False, stop=True).then_inc(scat_mm, 1)

            dve_st.wait(pe, "natl", 1)
            gather(0)
            dve_st.wait(pe, "route", 1)
            jobs = pe.value_load(jti[0:1, MAX_JOBS:MAX_JOBS + 1], min_val=NE, max_val=NE + 3)
            with pe.Fori(0, jobs) as i:
                def take_job(h):
                    pe.wait_ge(lo_done, i * HALVES_FFN + (n_static_halves + h + 1))
                    return h % HLS_MOE

                def job_extra(h):
                    for part in range(2):
                        if h == SCATTER_AFTER[part]:
                            scatter(i, part)
                    if h == PT_AFTER:
                        pe.wait_ge(sel_ready, i + 1)
                        for s in range(S):
                            out = bank(5)[:, s * P:(s + 1) * P]
                            mm(out, P1[:, s, :], ident, start=True, stop=False)
                            mm(out, P2[:, s, :], ident, start=False, stop=True)
                        out = bank(5)[:, S * P:S * P + 1]
                        for n, (sel, k, s) in enumerate(((P1, 0, 0), (P1, 0, 1), (P2, 1, 0), (P2, 1, 1))):
                            ins = mm(out, sel[:, s, :], wts[:, k, s:s + 1], start=(n == 0), stop=(n == 3))
                        ins.then_inc(ptr_mm, 1)
                    if h == GATHER_AFTER:
                        pe.wait_ge(acc_done, i * 4 + 4)
                        gather(i + 1)

                pe.wait_ge(xl_ready, i * 2 + 2)
                ffn_pe(take_job, PACE_JOB, 1, i, [(XTh[0], XTl[0])], act_m, hTh_m, hTl_m, (2, 3),
                       (job_silu, job_prod, job_tr, job_hTl), job_extra)
            scatter(jobs, 0)
            scatter(jobs, 1)

            gate_rows("gb2", 1, 5)


_INS = ["x_prompt", "x_sample", "state_mlstm_C", "state_mlstm_n", "state_mlstm_m", "state_ret_S", "c", "c_ctx",
        "norm1_g", "norm2_g", "norm_f_g", "w_ada", "b_ada", "w_in", "b_gates", "ret_decay_logit",
        "mlstm_norm_g", "ret_norm_g", "w_out", "ffn_w_gate", "ffn_w_up", "ffn_w_down",
        "moe_w_router", "moe_w_gate", "moe_w_up", "moe_w_down"]
_OUTS = {"y_prompt": (1, P, D), "y_sample": (1, P, D), "new_C": (1, DEPTH, 2, H, P, P),
         "new_n": (1, DEPTH, 2, H, P), "new_m": (1, DEPTH, 2, H), "new_S": (1, DEPTH, 2, H, P, P)}


def kernel(**inputs):
    import concourse.bacc as bacc
    from concourse.bass_utils import run_bass_kernel_spmd

    nc = bacc.Bacc("TRN2", target_bir_lowering=False, num_devices=1)
    arrays = {name: np.ascontiguousarray(inputs[name]) for name in _INS}
    arrays["consts"] = shape_constants()
    a = {n: nc.dram_tensor(n, v.shape, mybir.dt.from_np(v.dtype), kind="ExternalInput").ap()
         for n, v in arrays.items()}
    o = {n: nc.dram_tensor(n, shape, F32, kind="ExternalOutput").ap() for n, shape in _OUTS.items()}
    bass_hybrid_backbone(nc, a, o)
    got = run_bass_kernel_spmd(nc, [arrays], core_ids=[0]).results[0]
    return tuple(got[n] for n in _OUTS)
```

```python
from contextlib import ExitStack

import numpy as np
import concourse.bass as bass
from concourse import mybir

ALU = mybir.AluOpType
ACT = mybir.ActivationFunctionType
F32 = mybir.dt.float32
F32R = mybir.dt.float32r
BF16 = mybir.dt.bfloat16
I32 = mybir.dt.int32
U32 = mybir.dt.uint32
AX_X = mybir.AxisListType.X

P = 128
S = 2
D = 1024
KT = D // P
DEPTH = 2
H = 4
WH = H * P
GATES = 4 * H
D_IN = 8 * WH + GATES
QM, KM, VM, OM, GT, QR, KR, VR, GR = (0, WH, 2 * WH, 3 * WH, 4 * WH, 4 * WH + GATES, 5 * WH + GATES,
                                      6 * WH + GATES, 7 * WH + GATES)
F = 2816
FT = F // P
NE = 8
EPS = 1e-6
GRID_W = 64
SCALE = float(P) ** -0.5
BLK = 512
HALF = 1024
RAW = 8
HLS = 3
HLS_MOE = 6
UNITS_FFN = 33
HALVES_FFN = 66
BIG = 1.0e30
MAX_JOBS = 16
PACE_DENSE = 2, [11, 19, 27, 35, 41, 47]
PACE_JOB = 4, [13, 21, 29, 37, 45, 51]
GATE_END = [3, 11, 19, 27, 35, 41]
UP_END = [7, 15, 23, 31, 39, 43]
PT_AFTER, GATHER_AFTER = 48, 55
EARLY = {(1, 0): 2, (1, 1): 2, (2, 0): 1}
PRE = 5
Y_AT, SCATTER_AFTER = 3, (8, 12)

C_ID, C_TRIF, C_TRIB, C_RELP, C_RELM, C_ONES, C_IOTA = (P * n for n in range(7))
C_COS = 7 * P
C_SIN = C_COS + 64
C_POS = C_SIN + 64
C_UNIT = C_POS + 4
C_ALL = C_UNIT + 4 * H - 1


def shape_constants():
    i = np.arange(P, dtype=np.float64)
    row, col = i[:, None], i[None, :]
    t = np.zeros((P, C_ALL), np.float32)
    t[:, C_ID:C_ID + P] = row == col
    t[:, C_TRIF:C_TRIF + P] = row <= col
    t[:, C_TRIB:C_TRIB + P] = row >= col
    t[:, C_RELP:C_RELP + P] = np.maximum(col - row, 0)
    t[:, C_RELM:C_RELM + P] = np.maximum(row - col, 0)
    t[:, C_ONES:C_ONES + P] = 1
    t[:, C_IOTA:C_IOTA + P] = col
    half = P // 4
    freqs = (np.float32(10000.0) ** (-np.arange(half, dtype=np.float32) / np.float32(half))).astype(np.float32)
    for a, pos in enumerate((np.arange(P) // GRID_W, np.arange(P) % GRID_W)):
        ang = (pos.astype(np.float32)[:, None] * freqs).astype(np.float64)
        t[:, C_COS + a * half:C_COS + (a + 1) * half] = np.cos(ang)
        t[:, C_SIN + a * half:C_SIN + (a + 1) * half] = np.sin(ang)
    t[:, C_POS + 0] = i + 1
    t[:, C_POS + 1] = P - i
    t[:, C_POS + 2] = P - 1 - i
    t[:, C_POS + 3] = i
    t[:, C_UNIT + 2 * H - 1] = 1
    return t


class Stages:

    def __init__(self, sem, first, layer, last):
        self.sem = sem
        self.value = {(n, None): k + 1 for k, n in enumerate(first)}
        for l in range(DEPTH):
            base = len(self.value)
            self.value |= {(n, l): base + k + 1 for k, n in enumerate(layer(l))}
        base = len(self.value)
        self.value |= {(n, None): base + k + 1 for k, n in enumerate(last)}
        self.at = 0

    def done(self, ins, name, l=None):
        self.at += 1
        assert self.value[(name, l)] == self.at, (name, l, self.at)
        ins.then_inc(self.sem, 1)

    def wait(self, eng, name, l=None):
        eng.wait_ge(self.sem, self.value[(name, l)])


def last_user(slots, n):
    return next(m for m in range(n - 1, n - 1 - len(slots), -1) if slots[m % len(slots)] == slots[n])


ADA_BATCHES = [4, 5, 3, 4, 3, 3, 2]
ADA_AT = [sum(ADA_BATCHES[:n]) for n in range(len(ADA_BATCHES) + 1)]
ADA_W = S * max(ADA_BATCHES)
ADA_FILL = {("first", 0): 32,
            ("mb0", 0): 2, ("pqk0", 0): 5, ("num0", 0): 3, ("cst", 0): 4, ("qkr0", 0): 2, ("pr0", 0): 2,
            ("o0", 0): 2, ("rst", 0): 2, ("mb1", 0): 2, ("pqk1", 0): 5, ("num1", 0): 1, ("qkr1", 0): 2,
            ("pr1", 0): 2, ("o1", 0): 6,
            ("gb1", 0): 2, ("yt", 0): 10, ("x1", 0): 12,
            ("xt2", 0): 4, ("gb2", 0): 4, ("ffn12", 0): 8, ("x2", 0): 16,
            ("xt1", 1): 8,
            ("pqk0", 1): 2, ("num0", 1): 1, ("cst", 1): 2, ("pr0", 1): 1, ("rst", 1): 1, ("mb1", 1): 1,
            ("pqk1", 1): 2, ("qkr1", 1): 1, ("pr1", 1): 1, ("o1", 1): 4,
            ("yt", 1): 12, ("x1", 1): 12,
            ("xt2", 1): 4, ("nat", 1): 8, ("rank", 1): 4}
ADA_BEFORE_OUT = ["mb0", "pqk0", "num0", "cst", "qkr0", "pr0", "o0", "rst", "mb1", "pqk1", "num1", "qkr1",
                  "pr1", "o1", "gb1", "yt"]


def static_units():
    left = [("ada", l, b, h, []) for l in range(DEPTH) for b in range(6 * D // BLK) for h in range(2)]
    units = []

    def ada(l, *steps):
        tiles = sum(ADA_FILL.get((step, l), 0) for step in steps)
        assert tiles % 4 == 0
        units.extend(left.pop(0) for _ in range(tiles // 4))

    ada(0, "first")
    for l in range(DEPTH):
        ada(l, "xt1")
        units += [("gates", l, 0, 0, [KT * GATES])]
        units += [("in", l, b, h, [HALF, HALF]) for b in range(8) for h in range(2)]
        ada(l, *ADA_BEFORE_OUT)
        units += [("out", l, b, h, [HALF, HALF]) for b in range(D // BLK) for h in range(2)]
        ada(l, "x1", "xt2", "gb2", "nat", "rank")
        if l == 0:
            for u in range(UNITS_FFN):
                units += [("ffn", l, u, 0, [HALF, HALF])]
                ada(l, f"ffn{u}")
            ada(l, "x2")
    assert not left
    return units


RAW_MOE_SLOT = [(len(static_units()) + k) % RAW for n in (8, 7, 6, 6, 6) for k in range(n)]

def bass_hybrid_backbone(nc, a, o):
    ctx = ExitStack()
    with ctx:
        base = 16512

        def at(name, offset, shape, dt=F32):
            return nc.alloc_sbuf_tensor_at(name, shape, dt, offset=base + offset)

        def sem(name):
            return ctx.enter_context(nc.semaphore(name))

        raw = [at(f"raw{n}", 8192 * n, [P, 2 * HALF]) for n in range(RAW)]
        top = 8192 * RAW
        hi = [at(f"hi{n}", top + 4096 * n, [P, HALF], F32R) for n in range(HLS)]
        top += 4096 * HLS
        lo = [at(f"lo{n}", top + 4096 * n, [P, HALF], F32R) for n in range(HLS)]
        top += 4096 * HLS
        region = top
        p = at("p", region, [P, S, D_IN])
        r = region + 4 * S * D_IN
        ET = at("ET", r, [P, 2, H, P])
        ST = at("ST", r + 4096, [P, 2, H, P])
        upd = at("upd", r + 4096, [P, 2, BLK])
        QT = at("QT", r + 8192, [P, H, P])
        KTt = at("KTt", r + 10240, [P, H, P])
        VW = at("VW", r + 12288, [P, 2, H, P])
        rope1 = at("rope1", r + 12288, [P, 2 * H, 2, 32])
        rope2 = at("rope2", r + 14336, [P, 2 * H, 2, 32])
        AR = at("AR", r + 12288, [2 * H, 2, P])
        CM = at("CM", r + 16384, [P, 2, H, P])
        SM = at("SM", r + 20480, [P, 2, H, P])
        DS = at("DS", r + 24576, [P, H, P])
        TR = at("TR", r + 26624, [P, H, P])
        STC = at("STC", r + 28672, [P, 2, H, P])
        region_size = 4 * S * D_IN + 32768
        rowsA = at("rowsA", region, [96, P])
        rowsB = at("rowsB", region + 512, [80, P])
        hTh_d = at("hTh_d", region, [P, FT, S, P], F32R)
        hTl_d = at("hTl_d", region + 4 * FT * S * P, [P, FT, S, P], F32R)
        silu_d = at("silu_d", region + 8 * FT * S * P, [P, S, BLK])
        act_d = at("act_d", region + 8 * FT * S * P + 4096, [P, S, BLK])
        m = region
        hTh_m = at("hTh_m", m, [P, FT, 1, P], F32R)
        hTl_m = at("hTl_m", m + 4 * FT * P, [P, FT, 1, P], F32R)
        m += 8 * FT * P
        nath = at("nath", m, [P, S, D], F32R)
        natl = at("natl", m + 8192, [P, S, D], F32R)
        m += 16384
        yh = at("yh", m, [P, D], F32R)
        yl = at("yl", m + 4096, [P, D], F32R)
        silu_m = at("silu_m", m + 8192, [P, 1, BLK])
        act_m = at("act_m", m + 10240, [P, 1, BLK])
        m += 12288
        P1 = at("P1", m, [P, S, P])
        P2 = at("P2", m + 1024, [P, S, P])
        Pr = at("Pr", m + 2048, [P, S, P], F32R)
        PT = at("PT", m + 3072, [P, S, P], F32R)
        m += 4096
        hi3, lo3 = at("hi3", m, [P, HALF], F32R), at("lo3", m + 4096, [P, HALF], F32R)
        jt = at("jt", m + 8192, [1, MAX_JOBS, NE])
        jtf = at("jtf", m + 8704, [1, MAX_JOBS + 1])
        assert m + 8192 + 1024 <= region + region_size
        gfin = at("gfin", region, [P, D])
        yfin = at("yfin", region + 4096, [P, S, D])
        top = region + region_size
        x = at("x", top, [P, S, D])
        top += 8192
        XTh = [at("XTh0", top, [P, KT, P], F32R), at("XTh1", top + 8192, [P, KT, P], F32R)]
        XTl = [at("XTl0", top + 4096, [P, KT, P], F32R), at("XTl1", top + 12288, [P, KT, P], F32R)]
        ysq = [at("ysq0", top + 4096, [P, 2 * H, P]), at("ysq1", top + 12288, [P, 2 * H, P])]
        hi4, lo4 = at("hi4", top + 8192, [P, HALF], F32R), at("lo4", top + 12288, [P, HALF], F32R)
        top += 16384
        N1 = at("N1", top, [P, S, D])
        N2 = at("N2", top + 8192, [P, S, KT, P])
        hi5, lo5 = at("hi5", top + 8192, [P, HALF], F32R), at("lo5", top + 12288, [P, HALF], F32R)
        top += 16384
        hi += [hi3, hi4, hi5]
        lo += [lo3, lo4, lo5]
        assert len(hi) == HLS_MOE and HALVES_FFN % HLS_MOE == 0 and len(RAW_MOE_SLOT) == UNITS_FFN
        small_at = [top]

        def small(name, shape, dt=F32):
            n = int(np.prod(shape[1:])) * (2 if dt == BF16 else 4)
            t = at(name, small_at[0], shape, dt)
            small_at[0] += -(-n // 32) * 32
            return t

        cst = small("cst", [P, C_ALL])
        identb = small("identb", [P, P], BF16)
        negm = small("negm", [P, 2, P], BF16)
        modc = [small(f"modc{l}", [P, 48, S]) for l in range(DEPTH)]
        colsA = small("colsA", [P, 96])
        colsB = small("colsB", [P, 80])
        csil = small("csil", [P, 16])
        cond = small("cond", [P, KT, 2 * ADA_W - S])
        adarow = small("adarow", [ADA_W, BLK])
        scol = small("scol", [P, KT, S])
        bg = small("bg", [P, DEPTH, GATES])
        retl = small("retl", [P, DEPTH, 2 * H])
        rlg = small("rlg", [P, DEPTH, 2 * H])
        rtmp = small("rtmp", [P, DEPTH, 2 * H])
        dqk = small("dqk", [P, DEPTH, 4, H])
        m0b = small("m0b", [P, DEPTH, 2, H])
        m0r = small("m0r", [2 * H, DEPTH, 2])
        wr = small("wr", [P, KT, NE])
        gt = small("gt", [P, S, GATES])
        nab = small("nab", [P, S, 2 * H])
        lp = small("lp", [P, S, 2 * H])
        FL = small("FL", [P, 2, S, H])
        Bc = small("Bc", [P, 2, S, H])
        Ac = small("Ac", [P, 2, S, H])
        Mc = small("Mc", [P, 2, S, H])
        yy = N2
        mrow = small("mrow", [P, 2, S, H])
        em = small("em", [P, 2, S, H])
        wi = small("wi", [P, 2, H])
        dm = small("dm", [P, 2, H])
        MR = small("MR", [2 * H, 2, P])
        nMR = small("nMR", [2 * H, 2, P])
        den = small("den", [P, 2, H])
        dent = small("dent", [P, 2, H])
        rden = small("rden", [P, 2, S, H])
        wrd = small("wrd", [P, 2, H])
        wn = small("wn", [P, H, 2 * H + 1])
        n0 = small("n0", [P, DEPTH, H, 2 * H + 1])
        rows = small("rows", [GATES, 2, P])
        nrow = small("nrow", [2 * H, P])
        ss = small("ss", [P, S, 8])
        ln_v = small("ln_v", [P, S, 8])
        rs = small("rs", [P, S, 8])
        rs2 = small("rs2", [P, S, 8])
        lg = small("lg", [P, S, NE])
        mx = small("mx", [P, S, 8])
        mi = small("mi", [P, S, 8], U32)
        mif = small("mif", [P, S, 2])
        M1 = small("M1", [P, S, NE])
        M2 = small("M2", [P, S, NE])
        MK = small("MK", [P, S, NE])
        nb = small("nb", [P, NE])
        st_i = small("st_i", [P, NE])
        slots = small("slots", [P, S, NE])
        stmp = small("stmp", [P, S, NE])
        keys = small("keys", [P, 2, S])
        wts = small("wts", [P, 2, S])
        jti = small("jti", [1, MAX_JOBS + 1], I32)
        gs = small("gs", [P, 1])
        assert base + small_at[0] <= 229368, base + small_at[0]

        ident = cst[:, C_ID:C_ID + P]
        trif = cst[:, C_TRIF:C_TRIF + P]
        trib = cst[:, C_TRIB:C_TRIB + P]
        ones = cst[:, C_ONES:C_ONES + P]
        iota = cst[:, C_IOTA:C_IOTA + P]

        pb = ctx.enter_context(nc.psum_tensor("pb", [P, 8, BLK], F32))

        def bank(n):
            return pb[:, n, :]

        def tiles(n):
            return pb[:, n, :].rearrange("p (t c) -> p t c", c=P)

        raw_ld = [sem(f"raw_ld{n}") for n in range(RAW)]
        moe_ld = [sem(f"moe_ld{n}") for n in range(RAW)]
        hi_done, lo_done, w_used = sem("hi_done"), sem("lo_done"), sem("w_used")
        cond_ld, m0r_ld = sem("cond_ld"), sem("m0r_ld")
        small_ld, state_ld, gfin_ld = sem("small_ld"), sem("state_ld"), sem("gfin_ld")
        ada_sum, ada_rows, ada_turned, ada_cols = (sem(f"ada_{n}") for n in ("sum", "rows", "turned", "cols"))
        in_evA, in_evD = sem("in_evA"), sem("in_evD")
        ffn_silu, ffn_prod = sem("ffn_silu"), sem("ffn_prod")
        ffn_tr, ffn_hTh, ffn_hTl = (sem(n) for n in ("ffn_tr", "ffn_hTh", "ffn_hTl"))
        job_silu, job_prod = sem("job_silu"), sem("job_prod")
        job_tr, job_hTh, job_hTl = (sem(n) for n in ("job_tr", "job_hTh", "job_hTl"))
        sel_ready, ptr_mm, pt_ready = sem("sel_ready"), sem("ptr_mm"), sem("pt_ready")
        sel_step, key_step = sem("sel_step"), sem("key_step")
        gath_mm, xh_ready, xl_ready = sem("gath_mm"), sem("xh_ready"), sem("xl_ready")
        yh_ready, yl_ready = sem("yh_ready"), sem("yl_ready")
        scat_mm = [[sem(f"scat_mm{s}{c}") for c in range(2)] for s in range(S)]
        acc_done = [[sem(f"acc_done{s}{c}") for c in range(2)] for s in range(S)]
        dve_chain, act_chain = sem("dve_chain"), sem("act_chain")
        st_out, m_out, n_out, y_out = sem("st_out"), sem("m_out"), sem("n_out"), sem("y_out")

        pe_st = Stages(sem("pe_stage"), ["cols"], lambda l: [
            "xt1a", "xt1", "gate_t", "bcum", "arow", "mcol",
            "qk0", "mb0", "pqk0", "den0", "num0", "cst", "qkr0", "pr0", "o0", "nst", "rst",
            "qk1", "mb1", "pqk1", "den1", "num1", "cq1", "qkr1", "pr1", "o1", "gb1a", "gb1", "yt", "xt2a", "xt2",
            *(["gb2a", "gb2"] if l == 0 else ["router", "nat", "rank", "gb2a", "gb2"])], [])
        act_st = Stages(sem("act_stage"), ["csil", "rlp", "rdec"], lambda l: [
            "sq1", "rs1", "xn1", "h1", "xh1a", "xh1", "gate_r", "gate_e", "dse", "em", "wi",
            "kt0", "et0", "den0", "stc", "ktr0", "rstc",
            "kt1", "et1", "den1", "ktr1", "sig", "hrs", "gb1a", "gb1", "yha", "yh", "sq2", "rs2", "xn2", "h2",
            *(["xh2a", "xh2", "gb2a", "gb2"] if l == 0 else ["nath", "we"])], ["sqf", "rsf"])
        dve_st = Stages(sem("dve_stage"), ["prep", "cond", "n0", "rnab", "rarg"], lambda l: [
            "v1", "rf1", "xn1", "mod1", "h1a", "xl1a", "xl1", "gates", "fl", "ba", "mr", "mc", "rope",
            "qt0", "st0", "vw", "y0", "qtr0", "str0", "vwr", "yr0", "nr",
            "qt1", "st1", "ya1", "qtr1", "y1", "str1", "yr1", "hv", "yn", "yl", "x1a", "x1",
            "v2", "rf2", "xn2", "mod2", "h2a",
            *(["xl2a", "xl2", "x2a", "x2"] if l == 0 else ["natl", "top", "masks", "route", "x2a", "x2"])],
            ["vf", "yfa", "yf"])

        units = static_units()
        n_static_halves = sum(len(u[-1]) for u in units)
        halves = []
        for n, u in enumerate(units):
            for k, size in enumerate(u[-1]):
                halves.append((n, k * HALF, size))
        halves_before = [sum(len(u[-1]) for u in units[:n]) for n in range(len(units) + 1)]

        def through(kind, l, b):
            return halves_before[1 + max(n for n, u in enumerate(units) if u[:3] == (kind, l, b))]

        ffn_first = halves_before[min(n for n, u in enumerate(units) if u[0] == "ffn")]

        def ffn_source(gate, up, down, u):
            if u < 22:
                j, part = (u // 4, u % 4) if u < 20 else (5, 2 * (u - 20))
                w, k0 = (gate, up)[part // 2], 4 * (part % 2)
                if j < 5:
                    return w.rearrange("(k p) n -> p k n", p=P)[:, k0:k0 + 4, j * BLK:(j + 1) * BLK]
                return w.rearrange("(k p) n -> p k n", p=P)[:, :, 5 * BLK:F]
            t = 2 * (u - 22)
            return down.rearrange("(t p) n -> p t n", p=P)[:, t:t + 2, :]

        def source(unit):
            kind, l, b, h, _ = unit
            if kind == "ada":
                return a["w_ada"][l].rearrange("(k p) n -> p k n", p=P)[:, 4 * h:4 * h + 4, b * BLK:(b + 1) * BLK]
            if kind == "gates":
                return a["w_in"][l].rearrange("(k p) n -> p k n", p=P)[:, :, GT:GT + GATES]
            if kind == "in":
                c = b * BLK + (GATES if b >= 4 else 0)
                return a["w_in"][l].rearrange("(k p) n -> p k n", p=P)[:, 4 * h:4 * h + 4, c:c + BLK]
            if kind == "out":
                return a["w_out"][l].rearrange("(k p) n -> p k n", p=P)[:, 4 * h:4 * h + 4, b * BLK:(b + 1) * BLK]
            return ffn_source(a["ffn_w_gate"][0], a["ffn_w_up"][0], a["ffn_w_down"][0], b)

        def unit_view(slot, size, cols):
            return slot[:, 0:size].rearrange("p (k n) -> p k n", n=cols)

        block = ctx.enter_context(nc.Block())

        @block.sync
        def _(sp):
            loads = [
                (cst[:, :], a["consts"]),
                (rowsA[:, :], a["b_ada"].rearrange("l (r p) -> (l r) p", p=P)),
                (rowsB[0:8, :], a["c_ctx"].rearrange("(r p) -> r p", p=P)),
                (rowsB[8:16, :], a["c"].rearrange("b (r p) -> (b r) p", p=P)),
                (rowsB[16:32, :], a["norm1_g"].rearrange("l (r p) -> (l r) p", p=P)),
                (rowsB[32:48, :], a["norm2_g"].rearrange("l (r p) -> (l r) p", p=P)),
                (rowsB[48:56, :], a["mlstm_norm_g"].rearrange("l (r p) -> (l r) p", p=P)),
                (rowsB[56:64, :], a["ret_norm_g"].rearrange("l (r p) -> (l r) p", p=P)),
                (rowsB[64:80, :], a["state_mlstm_n"].rearrange("b l d h p -> (b l d h) p")),
            ]
            for dst, src in loads:
                sp.dma_start(dst, src).then_inc(cond_ld, 16)

            def wait_used(n):
                if units[n][0] == "ada":
                    sp.wait_ge(ada_sum, sum(u[0] == "ada" for u in units[:n + 1]))
                else:
                    sp.wait_ge(lo_done, halves_before[n + 1])

            for n, unit in enumerate(units):
                if n >= RAW:
                    wait_used(n - RAW)
                kind, l, b, h, sizes = unit
                cols = {"gates": GATES, "ffn": (BLK if b < 20 else F - 5 * BLK) if b < 22 else D}.get(kind, BLK)
                sp.dma_start(unit_view(raw[n % RAW], sum(sizes) or 2 * HALF, cols), source(unit))\
                    .then_inc(raw_ld[n % RAW], 16)
                if kind == "gates":
                    if l > 0:
                        pe_st.wait(sp, "o1", l - 1)
                        dve_st.wait(sp, "x2", l - 1)
                    sp.dma_start(CM[:, :, :, :], a["state_mlstm_C"][0, l].rearrange("d h p e -> p d h e"))\
                        .then_inc(state_ld, 16)
                    sp.dma_start(SM[:, :, :, :], a["state_ret_S"][0, l].rearrange("d h p e -> p d h e"))\
                        .then_inc(state_ld, 16)

            def job(u, e):
                src = ffn_source(*(a[f"moe_w_{w}"][0][e] if isinstance(e, int) else
                                   a[f"moe_w_{w}"][0][bass.ds(e, 1)].rearrange("o r n -> (o r) n")
                                   for w in ("gate", "up", "down")), u)
                cols = (BLK if u < 20 else F - 5 * BLK) if u < 22 else D
                slot = RAW_MOE_SLOT[u]
                sp.dma_start(unit_view(raw[slot], 2 * HALF, cols), src).then_inc(moe_ld[slot], 16)

            for u in range(UNITS_FFN):
                if u < RAW:
                    wait_used(max(n for n in range(len(units)) if n % RAW == RAW_MOE_SLOT[u]))
                else:
                    sp.wait_ge(lo_done, n_static_halves + 2 * (last_user(RAW_MOE_SLOT, u) + 1))
                job(u, 0)
            dve_st.wait(sp, "route", 1)
            jobs = sp.value_load(jti[0:1, MAX_JOBS:MAX_JOBS + 1], min_val=NE, max_val=NE + 3)
            with sp.Fori(1, jobs) as i:
                e = sp.value_load(jti[0:1, bass.ds(i, 1)], min_val=0, max_val=NE - 1)
                for u in range(UNITS_FFN):
                    sp.wait_ge(lo_done, i * HALVES_FFN + (n_static_halves + 2 * (last_user(RAW_MOE_SLOT, u) + 1)))
                    job(u, e)
            pe_st.wait(sp, "gb2", 1)
            sp.dma_start(gfin[:, :], a["norm_f_g"].rearrange("(o n) -> o n", o=1).to_broadcast([P, D]))\
                .then_inc(gfin_ld, 16)
            dve_st.wait(sp, "yfa")
            sp.dma_start(o["y_prompt"][0], yfin[:, 0, :]).then_inc(y_out, 16)
            dve_st.wait(sp, "yf")
            sp.dma_start(o["y_sample"][0], yfin[:, 1, :]).then_inc(y_out, 16)
            sp.wait_ge(y_out, 32)
            sp.wait_ge(st_out, 16 * 8)
            sp.wait_ge(m_out, 16 * 4)
            sp.wait_ge(n_out, 16 * 2)

        @block.gpsimd
        def _(pool):
            dve_st.wait(pool, "prep")
            for l in range(DEPTH):
                for d in range(2):
                    pool.dma_start(m0r[H:2 * H, l, d:d + 1],
                                   a["state_mlstm_m"][0, l, d].rearrange("(h o) -> h o", o=1)).then_inc(m0r_ld, 16)
            for l in range(DEPTH):
                dve_st.wait(pool, "mc", l)
                pool.dma_start(o["new_m"][0, l, 0:1, :], mrow[P - 1:P, 0, 0, :]).then_inc(m_out, 16)
                pool.dma_start(o["new_m"][0, l, 1:2, :], mrow[0:1, 1, 0, :]).then_inc(m_out, 16)
                act_st.wait(pool, "stc", l)
                for d in range(2):
                    pool.dma_start(o["new_C"][0, l, d].rearrange("h p e -> p h e"), STC[:, d, :, :])\
                        .then_inc(st_out, 16)
                dve_st.wait(pool, "nr", l)
                pool.dma_start(o["new_n"][0, l].rearrange("d h p -> (d h) p"), nrow[:, :]).then_inc(n_out, 16)
                act_st.wait(pool, "rstc", l)
                for d in range(2):
                    pool.dma_start(o["new_S"][0, l, d].rearrange("h p e -> p h e"), STC[:, d, :, :])\
                        .then_inc(st_out, 16)

        @block.scalar
        def _(act):
            chain = [0]
            pos = [0]

            def link(ins):
                chain[0] += 1
                ins.then_inc(act_chain, 1)
                act.wait_ge(act_chain, chain[0])

            def copy(out, in_, scale=1.0):
                return nc.scalar.activation(out, in_, ACT.Copy, scale=scale)

            def split(n=1):
                for _ in range(n):
                    q = pos[0]
                    u, off, size = halves[q]
                    if off == 0:
                        act.wait_ge(raw_ld[u % RAW], 16 * (u // RAW + 1))
                    if q >= HLS:
                        act.wait_ge(w_used, q - HLS + 1)
                    copy(hi[q % HLS][:, 0:size], raw[u % RAW][:, off:off + size]).then_inc(hi_done, 1)
                    pos[0] += 1

            def ln_exp_table():
                nc.scalar.preload_act_table_set("natural_log_exp_and_others")

            def rsqrt(src, n, name, l=None):
                link(nc.scalar.activation(ln_v[:, :, 0:n], src, ACT.Ln))
                act_st.done(nc.scalar.activation(rs[:, :, 0:n], ln_v[:, :, 0:n], ACT.Exp, scale=-0.5), name, l)

            def norm_sums(name, step, l=None, l_step=None):
                ln_exp_table()
                for s in range(S):
                    if step:
                        dve_st.wait(act, step + "a" * (1 - s), l_step)
                    ins = nc.scalar.activation(N1[:, s, :], x[:, s, :], ACT.Square, accum_out=ss[:, s, 0:1])
                act_st.done(ins, name, l)

            def ada_rows_out(batch):
                act.wait_ge(ada_sum, 2 * ADA_AT[batch + 1])
                if batch:
                    act.wait_ge(ada_turned, batch)
                copy(adarow[:, :], bank(7)[0:ADA_W, :]).then_inc(ada_rows, 1)

            def norm(k, l):
                dve_st.wait(act, f"v{k}", l)
                rsqrt(ss[:, :, 0:1], 1, f"rs{k}", l)
                dve_st.wait(act, f"rf{k}", l)
                act_st.done(copy(N1[:, 1, :], x[:, 1, :], rs[:, 1, 0:1]), f"xn{k}", l)
                split(EARLY.get((k, l), 0))
                ada_rows_out(3 * l + (0 if k == 1 else 2))
                dve_st.wait(act, f"mod{k}", l)
                pe_st.wait(act, f"xt{k}", l)
                shift = 0 if k == 1 else 24
                for t in range(KT):
                    ins = nc.scalar.activation(N2[:, 1, t, :], tiles(2 + t // 4)[:, t % 4, :], ACT.Identity,
                                               scale=scol[:, t, 1:2], bias=modc[l][:, shift + t, 1:2])
                act_st.done(ins, f"h{k}", l)
                if (k, l) != (2, 1):
                    for s, step in enumerate((f"xh{k}a", f"xh{k}")):
                        if s == 0:
                            dve_st.wait(act, f"h{k}a", l)
                        else:
                            act_st.wait(act, f"h{k}", l)
                        act_st.done(copy(XTh[s][:, :, :], N2[:, s, :, :]), step, l)

            def gate_rows(name, l):
                for s, step in enumerate((name + "a", name)):
                    pe_st.wait(act, step, l)
                    for k in range(2):
                        ins = copy(N1[:, s, k * BLK:(k + 1) * BLK], bank(4 + k))
                    act_st.done(ins, step, l)

            def ffn_act(split_half, pace, ns, i, first, silu, hTh, sems):
                silu_sem, prod, tr, hTh_sem = sems
                lag, t_after = pace

                def do_silu(j):
                    w = BLK if j < 5 else F - 5 * BLK
                    act.wait_ge(w_used, i * HALVES_FFN + (first + GATE_END[j] + 1))
                    for s in range(ns):
                        if not (isinstance(i, int) and j == 0):
                            act.wait_ge(prod, i * (6 * ns) + ns * j)
                        nc.scalar.activation(silu[:, s, 0:w], bank(2 * s)[:, 0:w], ACT.Silu)\
                            .then_inc(silu_sem, 1)

                def do_hT(j):
                    nt = 4 if j < 5 else 2
                    for s in range(ns):
                        act.wait_ge(tr, i * (6 * ns) + (ns * j + s + 1))
                        copy(hTh[:, 4 * j:4 * j + nt, s, :], tiles(4 + s)[:, 0:nt, :]).then_inc(hTh_sem, 1)

                for h in range(HALVES_FFN):
                    split_half(h)
                    for j in range(6):
                        if h == GATE_END[j] + lag:
                            do_silu(j)
                    for j in range(6):
                        if h == t_after[j] + lag:
                            do_hT(j)

            loads = [
                (x[:, 0, :], a["x_prompt"][0]),
                (x[:, 1, :], a["x_sample"][0]),
                (bg[:, :, :], a["b_gates"].rearrange("(o l) g -> o l g", o=1).to_broadcast([P, DEPTH, GATES])),
                (retl[:, :, :], a["ret_decay_logit"].rearrange("(o l) d h -> o l (d h)", o=1)
                    .to_broadcast([P, DEPTH, 2 * H])),
                (m0b[:, :, :, :], a["state_mlstm_m"].to_broadcast([P, DEPTH, 2, H])),
                (wr[:, :, :], a["moe_w_router"][0].rearrange("(k p) e -> p k e", p=P)),
            ]
            for dst, src in loads:
                act.dma_start(dst, src).then_inc(small_ld, 16)
            pe_st.wait(act, "cols")
            act_st.done(nc.scalar.activation(csil[:, :], bank(5)[:, 0:16], ACT.Silu), "csil")
            dve_st.wait(act, "rnab")
            link(nc.scalar.activation(rtmp[:, :, :], rtmp[:, :, :], ACT.Exp))
            act_st.done(nc.scalar.activation(rtmp[:, :, :], rtmp[:, :, :], ACT.Ln, bias=1.0), "rlp")
            dve_st.wait(act, "rarg")
            act_st.done(nc.scalar.activation(dqk[:, :, :, :], dqk[:, :, :, :], ACT.Exp), "rdec")

            for l in range(DEPTH):
                if l == 0:
                    act.wait_ge(small_ld, 16 * 6)
                norm_sums("sq1", "x2" if l else None, l, l - 1)
                norm(1, l)
                split(3 - EARLY[1, l])
                act.wait_ge(w_used, through("gates", l, 0))
                act_st.done(copy(rows[:, :, :], tiles(4)[0:GATES, 0:S, :]), "gate_r", l)
                ln_exp_table()
                split(2)
                dve_st.wait(act, "gates", l)
                link(nc.scalar.activation(nab[:, :, :], nab[:, :, :], ACT.Exp))
                act_st.done(nc.scalar.activation(lp[:, :, :], nab[:, :, :], ACT.Ln, bias=1.0), "gate_e", l)

                def block_out(b):
                    act.wait_ge(w_used, through("in", l, b))
                    c = b * BLK + (GATES if b >= 4 else 0)
                    copy(p[:, 0, c:c + BLK], bank(b % 2 * 2)).then_inc(in_evA, 1)

                for b in range(8):
                    if b:
                        split(2)
                        block_out(b - 1)
                        split(2)
                    if b == 1:
                        for h in range(H):
                            nc.scalar.activation(DS[:, h, :], cst[:, C_RELP:C_RELP + P], ACT.Exp,
                                                 scale=rlg[:, l, h:h + 1])
                            ins = nc.scalar.activation(TR[:, h, :], cst[:, C_RELM:C_RELM + P], ACT.Exp,
                                                       scale=rlg[:, l, H + h:H + h + 1])
                        act_st.done(ins, "dse", l)
                block_out(7)
                dve_st.wait(act, "mc", l)
                act_st.done(nc.scalar.activation(em[:, :, :, :], mrow[:, :, :, :], ACT.Exp, scale=-1.0), "em", l)
                act_st.done(nc.scalar.activation(wi[:, :, :], dm[:, :, :], ACT.Exp), "wi", l)
                for s in range(S):
                    pe_st.wait(act, f"qk{s}", l)
                    act_st.done(copy(KTt[:, :, :], tiles(3)), f"kt{s}", l)
                    pe_st.wait(act, f"mb{s}", l)
                    if s:
                        dve_st.wait(act, "vw", l)
                    for d in range(2):
                        for h in range(H):
                            ins = nc.scalar.activation(ET[:, d, h, :], tiles(d)[:, h, :], ACT.Exp,
                                                       bias=Ac[:, d, s, h:h + 1])
                    act_st.done(ins, f"et{s}", l)
                    pe_st.wait(act, f"den{s}", l)
                    act_st.done(copy(rows[0:2 * H, 0:s + 1, :], tiles(4)[0:2 * H, 0:s + 1, :]), f"den{s}", l)
                    if s == 0:
                        pe_st.wait(act, "cst", l)
                        if l:
                            act.wait_ge(st_out, 16 * 4 * l)
                        for d in range(2):
                            ins = copy(STC[:, d, :, :], tiles(d))
                        act_st.done(ins, "stc", l)
                    pe_st.wait(act, f"qkr{s}", l)
                    act_st.done(copy(KTt[:, :, :], tiles(3)), f"ktr{s}", l)
                    if s == 0:
                        pe_st.wait(act, "rst", l)
                        act.wait_ge(st_out, 16 * (4 * l + 2))
                        for d in range(2):
                            ins = copy(STC[:, d, :, :], tiles(d))
                        act_st.done(ins, "rstc", l)
                act.wait_ge(in_evD, 8 * l + 8)
                act.wait_ge(in_evA, 8 * l + 8)
                nc.scalar.activation(p[:, :, OM:OM + WH], p[:, :, OM:OM + WH], ACT.Sigmoid)
                act_st.done(nc.scalar.activation(p[:, :, GR:GR + WH], p[:, :, GR:GR + WH], ACT.Silu), "sig", l)
                ln_exp_table()
                ada_rows_out(3 * l + 1)
                dve_st.wait(act, "hv", l)
                rsqrt(ss[:, :, :], 8, "hrs", l)
                gate_rows("gb1", l)
                split(3)
                pe_st.wait(act, "yt", l)
                for s, step in enumerate(("yha", "yh")):
                    for t in range(KT):
                        g = 48 + 4 * l + t if t < H else 56 + 4 * l + t - H
                        ins = copy(XTh[s][:, t, :], tiles(2 * s + t // 4)[:, t % 4, :], colsB[:, g:g + 1])
                    act_st.done(ins, step, l)
                split(5)
                norm_sums("sq2", "x1", l, l)
                norm(2, l)
                if l == 0:
                    gate_rows("gb2", l)
                    ffn_act(lambda h: split(h >= EARLY[2, 0]), PACE_DENSE, S, 0, ffn_first, silu_d, hTh_d,
                            (ffn_silu, ffn_prod, ffn_tr, ffn_hTh))

            def split_job(i, h):
                u = h // 2
                if h % 2 == 0:
                    slot = RAW_MOE_SLOT[u]
                    act.wait_ge(moe_ld[slot], i * (16 * RAW_MOE_SLOT.count(slot))
                                + 16 * RAW_MOE_SLOT[:u + 1].count(slot))
                old = 0 if isinstance(i, int) and h < HLS_MOE else h - HLS_MOE + 1
                act.wait_ge(w_used, i * HALVES_FFN + (n_static_halves + old))
                copy(hi[h % HLS_MOE][:, :],
                     raw[RAW_MOE_SLOT[u]][:, h % 2 * HALF:(h % 2 + 1) * HALF]).then_inc(hi_done, 1)

            act.wait_ge(st_out, 16 * 8)
            for h in range(PRE):
                split_job(0, h)
            pe_st.wait(act, "nat", 1)
            for s in range(S):
                for k in range(2):
                    ins = copy(nath[:, s, k * BLK:(k + 1) * BLK], bank(2 * s + k))
            act_st.done(ins, "nath", 1)
            dve_st.wait(act, "top", 1)
            act_st.done(nc.scalar.activation(wts[:, 1, :], wts[:, 0, :], ACT.Exp), "we", 1)

            def gather_hi(n):
                for k in range(2):
                    act.wait_ge(gath_mm, n * 2 + (k + 1))
                    copy(XTh[0][:, 4 * k:4 * k + 4, :], tiles(6 + k)).then_inc(xh_ready, 1)

            ada_rows_out(len(ADA_BATCHES) - 1)

            def y_hi(n):
                act.wait_ge(w_used, n * HALVES_FFN + n_static_halves)
                act.wait_ge(pt_ready, n)
                for c in range(2):
                    copy(yh[:, c * BLK:(c + 1) * BLK], bank(2 + c), gs[:, 0:1]).then_inc(yh_ready, 1)

            def job(i, first):
                def half(h):
                    if h >= first:
                        split_job(i, h)
                    if h == Y_AT and not isinstance(i, int):
                        y_hi(i)
                    if h == GATHER_AFTER + PACE_JOB[0]:
                        gather_hi(i + 1)

                ffn_act(half, PACE_JOB, 1, i, n_static_halves, silu_m, hTh_m,
                        (job_silu, job_prod, job_tr, job_hTh))

            gather_hi(0)
            job(0, PRE)
            jobs = act.value_load(jti[0:1, MAX_JOBS:MAX_JOBS + 1], min_val=NE, max_val=NE + 3)
            with act.Fori(1, jobs) as i:
                job(i, 0)
            y_hi(jobs)

            norm_sums("sqf", "x2", None, 1)
            dve_st.wait(act, "vf")
            rsqrt(ss[:, :, 0:1], 1, "rsf")

        @block.vector
        def _(dve):
            chain = [0]
            pos = [0]
            v = nc.vector

            def link(ins):
                chain[0] += 1
                ins.then_inc(dve_chain, 1)
                dve.wait_ge(dve_chain, chain[0])

            def split(n=1):
                for _ in range(n):
                    q = pos[0]
                    u, off, size = halves[q]
                    dve.wait_ge(hi_done, q + 1)
                    v.tensor_tensor(lo[q % HLS][:, 0:size], raw[u % RAW][:, off:off + size],
                                    hi[q % HLS][:, 0:size].bitcast(F32), ALU.subtract).then_inc(lo_done, 1)
                    pos[0] += 1

            def refine(n, name=None, l=None):
                r_, t_, v_ = rs[:, :, 0:n], rs2[:, :, 0:n], ss[:, :, 0:n]
                link(v.tensor_tensor(t_, r_, r_, ALU.mult))
                link(v.tensor_tensor(t_, t_, v_, ALU.mult))
                link(v.tensor_scalar(t_, t_, -0.5, 1.5, ALU.mult, ALU.add))
                ins = v.tensor_tensor(r_, r_, t_, ALU.mult)
                if name:
                    dve_st.done(ins, name, l)
                    dve_st.wait(dve, name, l)
                else:
                    link(ins)

            def negative_abs(out, z):
                return v.scalar_tensor_tensor(out=out, in0=z, scalar=-1.0, in1=z, op0=ALU.mult, op1=ALU.min)

            def log_sigmoid(out, z, softplus):
                return v.scalar_tensor_tensor(out=out, in0=z, scalar=0.0, in1=softplus, op0=ALU.min,
                                              op1=ALU.subtract)

            def mean(n, width, name, l=None):
                dve_st.done(v.tensor_scalar(ss[:, :, 0:n], ss[:, :, 0:n], 1.0 / width, EPS, ALU.mult, ALU.add),
                            name, l)

            def modulation(batch):
                dve.wait_ge(ada_turned, batch + 1)
                nb = ADA_BATCHES[batch]
                l, b = divmod(ADA_AT[batch], 6 * D // BLK)
                bias = colsA[:, 48 * l + 4 * b:48 * l + 4 * (b + nb)]
                v.tensor_tensor(
                    modc[l][:, 4 * b:4 * (b + nb), :].rearrange("p (b t) s -> p b t s", t=4),
                    bank(7)[:, 0:4 * ADA_W].rearrange("p (t b s) -> p b t s", t=4, s=S)[:, 0:nb, :, :],
                    bias.rearrange("p (b t o) -> p b t o", t=4, o=1).to_broadcast([P, nb, 4, S]), ALU.add)\
                    .then_inc(ada_cols, 1)

            def norm(k, l):
                act_st.wait(dve, f"sq{k}", l)
                mean(1, D, f"v{k}", l)
                act_st.wait(dve, f"rs{k}", l)
                refine(1, f"rf{k}", l)
                dve_st.done(v.tensor_scalar(N1[:, 0, :], x[:, 0, :], rs[:, 0, 0:1], None, ALU.mult), f"xn{k}", l)
                split(EARLY.get((k, l), 0))
                batch = 3 * l + (0 if k == 1 else 2)
                modulation(batch)
                dve.wait_ge(ada_cols, batch + 1)
                g0 = (16 if k == 1 else 32) + 8 * l
                comp = 1 if k == 1 else 4
                dve_st.done(v.scalar_tensor_tensor(
                    out=scol[:, :, :], in0=modc[l][:, 8 * comp:8 * comp + 8, :], scalar=1.0,
                    in1=colsB[:, g0:g0 + 8].rearrange("p (t o) -> p t o", o=1).to_broadcast([P, KT, S]),
                    op0=ALU.add, op1=ALU.mult), f"mod{k}", l)
                dve_st.wait(dve, f"mod{k}", l)
                pe_st.wait(dve, f"xt{k}a", l)
                shift = 0 if k == 1 else 24
                for t in range(KT):
                    ins = v.tensor_scalar(N2[:, 0, t, :], tiles(t // 4)[:, t % 4, :],
                                          scol[:, t, 0:1], modc[l][:, shift + t, 0:1], ALU.mult, ALU.add)
                dve_st.done(ins, f"h{k}a", l)
                if (k, l) != (2, 1):
                    for s, step in enumerate((f"xh{k}a", f"xh{k}")):
                        act_st.wait(dve, step, l)
                        dve_st.done(v.tensor_tensor(XTl[s][:, :, :], N2[:, s, :, :], XTh[s][:, :, :].bitcast(F32),
                                                    ALU.subtract), f"xl{k}" + "a" * (1 - s), l)

            def residual(banks, summed, name, l):
                for n, (s, c, bk) in enumerate(banks):
                    cols = slice(c * BLK, (c + 1) * BLK)
                    dve.wait_ge(w_used, summed(s, c))
                    link(v.tensor_tensor(upd[:, n % 2, :], bank(bk), N1[:, s, cols], ALU.mult))
                    ins = v.tensor_tensor(x[:, s, cols], x[:, s, cols], upd[:, n % 2, :], ALU.add)
                    if n + 1 == 2 + (name == "x1"):
                        dve_st.done(ins, name + "a", l)
                dve_st.done(ins, name, l)

            def ffn_dve(split_half, pace, ns, i, first, silu, act_t, hTh, hTl, sems):
                silu_sem, prod, tr, hTh_sem, hTl_sem = sems
                lag, t_after = pace

                def do_prod(j):
                    w = BLK if j < 5 else F - 5 * BLK
                    for s in range(ns):
                        dve.wait_ge(silu_sem, i * (6 * ns) + (ns * j + s + 1))
                        dve.wait_ge(w_used, i * HALVES_FFN + (first + UP_END[j] + 1))
                        if not (isinstance(i, int) and j == 0):
                            dve.wait_ge(tr, i * (6 * ns) + ns * j)
                        v.tensor_tensor(act_t[:, s, 0:w], bank(2 * s + 1)[:, 0:w], silu[:, s, 0:w], ALU.mult)\
                            .then_inc(prod, 1)

                def do_hT(j):
                    nt = 4 if j < 5 else 2
                    for s in range(ns):
                        dve.wait_ge(hTh_sem, i * (6 * ns) + (ns * j + s + 1))
                        v.tensor_tensor(hTl[:, 4 * j:4 * j + nt, s, :], tiles(4 + s)[:, 0:nt, :],
                                        hTh[:, 4 * j:4 * j + nt, s, :].bitcast(F32), ALU.subtract)\
                            .then_inc(hTl_sem, 1)

                for h in range(HALVES_FFN):
                    split_half(h)
                    for j in range(6):
                        if h == UP_END[j] + lag:
                            do_prod(j)
                    for j in range(6):
                        if h == t_after[j] + lag:
                            do_hT(j)

            dve.wait_ge(cond_ld, 16 * 9)
            v.tensor_copy(identb[:, :], ident)
            v.tensor_scalar(negm[:, 0, :], trif, 1.0, BIG, ALU.subtract, ALU.mult)
            v.tensor_scalar(negm[:, 1, :], trib, 1.0, BIG, ALU.subtract, ALU.mult)
            dve_st.done(v.memset(m0r[:, :, :], 0.0), "prep")
            pe_st.wait(dve, "cols")
            v.tensor_copy(colsA[:, :], bank(4)[:, 0:96])
            act_st.wait(dve, "csil")
            v.tensor_copy(colsB[:, :], bank(5)[:, 0:80])
            v.memset(wn[:, :, :], 0.0)
            v.memset(n0[:, :, :, :], 0.0)
            link(v.memset(cond[:, :, :], 0.0))
            dve_st.done(v.tensor_copy(cond[:, :, ADA_W - S:ADA_W], csil[:, :].rearrange("p (s k) -> p k s", s=S)),
                        "cond")
            for l in range(DEPTH):
                for d in range(2):
                    ins = v.tensor_copy(n0[:, l, :, H * d], colsB[:, 64 + 8 * l + 4 * d:68 + 8 * l + 4 * d])
            dve_st.done(ins, "n0")
            dve.wait_ge(small_ld, 16 * 6)
            dve_st.done(negative_abs(rtmp[:, :, :], retl[:, :, :]), "rnab")
            act_st.wait(dve, "rlp")
            link(log_sigmoid(rlg[:, :, :], retl[:, :, :], rtmp[:, :, :]))
            for d in range(4):
                ins = v.tensor_scalar(dqk[:, :, d, :], rlg[:, :, d % 2 * H:(d % 2 + 1) * H],
                                      cst[:, C_POS + d:C_POS + d + 1], None, ALU.mult)
            dve_st.done(ins, "rarg")

            for l in range(DEPTH):
                norm(1, l)

                split(5 - EARLY[1, l])
                pe_st.wait(dve, "gate_t", l)
                link(v.tensor_tensor(gt[:, :, :], bank(4)[:, 0:S * GATES].rearrange("p (s g) -> p s g", s=S),
                                     bg[:, l:l + 1, :].to_broadcast([P, S, GATES]), ALU.add))
                dve_st.done(negative_abs(nab[:, :, :], gt[:, :, 2 * H:4 * H]), "gates", l)

                def by_direction(t):
                    return t.rearrange("p s (d h) -> p d s h", d=2)

                def block_out(b):
                    dve.wait_ge(w_used, through("in", l, b))
                    c = b * BLK + (GATES if b >= 4 else 0)
                    v.tensor_copy(p[:, 1, c:c + BLK], bank(b % 2 * 2 + 1)).then_inc(in_evD, 1)

                for b in range(8):
                    if b:
                        split(2)
                        block_out(b - 1)
                        split(2)
                    if b == 0:
                        act_st.wait(dve, "gate_e", l)
                        for d in range(2):
                            ins = log_sigmoid(FL[:, d, :, :], gt[:, :, (2 + d) * H:(3 + d) * H],
                                              lp[:, :, d * H:(d + 1) * H])
                        dve_st.done(ins, "fl", l)
                    if b == 2:
                        pe_st.wait(dve, "bcum", l)
                        link(v.tensor_copy(Bc[:, :, :, :],
                                           bank(5)[:, 0:16].rearrange("p (d s h) -> p d s h", d=2, s=S)))
                        for d in range(2):
                            ins = v.tensor_tensor(Ac[:, d, :, :], gt[:, :, d * H:(d + 1) * H], Bc[:, d, :, :],
                                                  ALU.subtract)
                        dve_st.done(ins, "ba", l)
                    if b == 3:
                        act_st.wait(dve, "dse", l)
                        for t, c0 in ((DS, C_TRIF), (TR, C_TRIB)):
                            mask = cst[:, c0:c0 + P].rearrange("p (o c) -> p o c", o=1).to_broadcast([P, H, P])
                            ins = v.tensor_tensor(t[:, :, :], t[:, :, :], mask, ALU.mult)
                        link(ins)
                        link(v.tensor_tensor(DS[:, :, :], DS[:, :, :], TR[:, :, :], ALU.add))
                    if b == 4:
                        pe_st.wait(dve, "arow", l)
                        dve.wait_ge(m0r_ld, 16 * 4)
                        link(v.tensor_copy(AR[:, :, :],
                                           bank(5)[0:2 * H, 0:2 * P].rearrange("p (d c) -> p d c", d=2)))
                        v.tensor_tensor_scan(MR[:, 0, :], AR[:, 0, :], AR[:, 0, :], m0r[:, l, 0:1],
                                             ALU.max, ALU.max)
                        link(v.tensor_tensor_scan(MR[:, 1, ::-1], AR[:, 1, ::-1], AR[:, 1, ::-1],
                                                  m0r[:, l, 1:2], ALU.max, ALU.max))
                        dve_st.done(v.tensor_scalar(nMR[:, :, :], MR[:, :, :], -1.0, None, ALU.mult), "mr", l)
                    if b == 6:
                        pe_st.wait(dve, "mcol", l)
                        if l:
                            dve.wait_ge(m_out, 32 * l)
                        link(v.tensor_copy(Mc[:, :, :, :],
                                           bank(5)[:, 0:16].rearrange("p (d s h) -> p d s h", d=2, s=S)))
                        v.tensor_tensor(dm[:, :, :], m0b[:, l, :, :], Mc[:, :, 1, :], ALU.subtract)
                        dve_st.done(v.tensor_tensor(mrow[:, :, :, :], Bc[:, :, :, :], Mc[:, :, :, :], ALU.add),
                                    "mc", l)
                block_out(7)
                dve.wait_ge(in_evD, 8 * l + 8)
                dve.wait_ge(in_evA, 8 * l + 8)

                qk = p[:, 1, QR:QR + 2 * WH].rearrange("p (h a f c) -> p h a f c", a=2, f=2, c=32)
                x1, x2 = qk[:, :, :, 0, :], qk[:, :, :, 1, :]

                def table(c0):
                    t = cst[:, c0:c0 + 64].rearrange("p (o a c) -> p o a c", o=1, a=2)
                    return t.to_broadcast([P, 2 * H, 2, 32])

                v.tensor_tensor(rope1[:, :, :, :], x2, table(C_SIN), ALU.mult)
                link(v.tensor_tensor(rope2[:, :, :, :], x1, table(C_SIN), ALU.mult))
                v.tensor_tensor(x1, x1, table(C_COS), ALU.mult)
                link(v.tensor_tensor(x2, x2, table(C_COS), ALU.mult))
                v.tensor_tensor(x1, x1, rope1[:, :, :, :], ALU.subtract)
                dve_st.done(v.tensor_tensor(x2, x2, rope2[:, :, :, :], ALU.add), "rope", l)
                dve_st.wait(dve, "rope", l)
                def squares(s, h0, h1):
                    y = yy[:, s, h0:h1, :]
                    sq = ysq[s][:, h0:h1, :]
                    link(v.tensor_tensor(sq, y, y, ALU.mult))
                    link(v.tensor_reduce(ss[:, s, h0:h1], sq, AX_X, ALU.add))

                for s in range(S):
                    pe_st.wait(dve, f"qk{s}", l)
                    dve_st.done(v.tensor_copy(QT[:, :, :], tiles(2)), f"qt{s}", l)
                    act_st.wait(dve, f"et{s}", l)
                    pe_st.wait(dve, f"pqk{s}", l)
                    for d in range(2):
                        ins = v.scalar_tensor_tensor(out=ST[:, d, :, :], in0=tiles(4), scalar=SCALE,
                                                     in1=ET[:, d, :, :], op0=ALU.mult, op1=ALU.mult)
                    dve_st.done(ins, f"st{s}", l)
                    if s == 0:
                        for d, end in ((0, P - 1), (1, 0)):
                            v.tensor_scalar(wn[:, :, H * d], ET[:, d, :, end], SCALE, None, ALU.mult)
                            for h in range(H):
                                ins = v.tensor_scalar(VW[:, d, h, :], p[:, 0, VM + h * P:VM + (h + 1) * P],
                                                      ET[:, d, h, end:end + 1], SCALE, ALU.mult, ALU.mult)
                        dve_st.done(ins, "vw", l)
                    pe_st.wait(dve, f"num{s}", l)
                    act_st.wait(dve, "wi", l)

                    def small8(c0):
                        return bank(4)[:, c0:c0 + 8].rearrange("p (d h) -> p d h", d=2)

                    if s == 0:
                        link(v.tensor_copy(dent[:, :, :], small8(0)))
                    else:
                        link(v.tensor_tensor(dent[:, :, :], small8(8), wi[:, :, :], ALU.mult))
                        link(v.tensor_tensor(dent[:, :, :], small8(0), dent[:, :, :], ALU.add))
                    link(v.scalar_tensor_tensor(out=den[:, :, :], in0=dent[:, :, :], scalar=-1.0,
                                                in1=dent[:, :, :], op0=ALU.mult, op1=ALU.max))
                    link(v.tensor_tensor(den[:, :, :], den[:, :, :], em[:, :, s, :], ALU.max))
                    link(v.reciprocal(rden[:, :, s, :], den[:, :, :]))
                    terms = [(5, lambda h: rden[:, 0, s, h:h + 1]), (6, lambda h: rden[:, 1, s, h:h + 1])]
                    if s == 1:
                        link(v.tensor_tensor(wrd[:, :, :], wi[:, :, :], rden[:, :, 1, :], ALU.mult))

                    def sum_terms(terms, h0, first):
                        for n, (bk, scalar) in enumerate(terms):
                            for h in range(H):
                                y = yy[:, s, h0 + h, :]
                                if n == 0 and first:
                                    ins = v.tensor_scalar(y, tiles(bk)[:, h, :], scalar(h), None, ALU.mult)
                                else:
                                    ins = v.scalar_tensor_tensor(out=y, in0=tiles(bk)[:, h, :], scalar=scalar(h),
                                                                 in1=y, op0=ALU.mult, op1=ALU.add)
                            if n + 1 < len(terms):
                                link(ins)
                        return ins

                    dve_st.done(sum_terms(terms, 0, True), "ya1" if s else "y0", l)
                    pe_st.wait(dve, f"qkr{s}", l)
                    dve_st.done(v.tensor_copy(QT[:, :, :], tiles(2)), f"qtr{s}", l)
                    if s:
                        dve_st.wait(dve, "ya1", l)
                        pe_st.wait(dve, "cq1", l)
                        dve_st.done(sum_terms([(0, lambda h: wrd[:, 0, h:h + 1]), (1, lambda h: wrd[:, 1, h:h + 1])],
                                              0, False), "y1", l)
                    pe_st.wait(dve, f"pr{s}", l)
                    dve_st.done(v.scalar_tensor_tensor(out=ST[:, 0, :, :], in0=tiles(4), scalar=SCALE,
                                                       in1=DS[:, :, :], op0=ALU.mult, op1=ALU.mult),
                                f"str{s}", l)
                    if s:
                        dve_st.wait(dve, "y1", l)
                        squares(1, 0, H)
                    else:
                        pe_st.wait(dve, "cst", l)
                        act_st.wait(dve, "rdec")
                        for d in range(2):
                            for h in range(H):
                                ins = v.tensor_scalar(VW[:, d, h, :], p[:, 0, VR + h * P:VR + (h + 1) * P],
                                                      dqk[:, l, 2 + d, h:h + 1], SCALE, ALU.mult, ALU.mult)
                        dve_st.done(ins, "vwr", l)
                    pe_st.wait(dve, f"o{s}", l)
                    ins = v.tensor_copy(yy[:, s, H:2 * H, :], tiles(5))
                    if s == 1:
                        link(ins)
                        ins = sum_terms([(6, lambda h: dqk[:, l, 0, h:h + 1]), (2, lambda h: dqk[:, l, 1, h:h + 1])],
                                        H, False)
                    dve_st.done(ins, f"yr{s}", l)
                    dve_st.wait(dve, f"yr{s}", l)
                    if s == 0:
                        pe_st.wait(dve, "nst", l)
                        if l:
                            dve.wait_ge(n_out, 16 * l)
                        dve_st.done(v.tensor_copy(nrow[:, :], bank(4)[0:2 * H, 0:P]), "nr", l)
                        squares(0, 0, 2 * H)
                    else:
                        squares(1, H, 2 * H)

                mean(8, P, "hv", l)
                modulation(3 * l + 1)
                act_st.wait(dve, "hrs", l)
                act_st.wait(dve, "sig", l)
                refine(8)
                for s in range(S):
                    for h in range(2 * H):
                        c = OM + h * P if h < H else GR + (h - H) * P
                        ins = v.scalar_tensor_tensor(out=yy[:, s, h, :], in0=yy[:, s, h, :],
                                                     scalar=rs[:, s, h:h + 1], in1=p[:, s, c:c + P],
                                                     op0=ALU.mult, op1=ALU.mult)
                dve_st.done(ins, "yn", l)
                split(3)
                pe_st.wait(dve, "yt", l)
                for s, step in enumerate(("yha", "yh")):
                    act_st.wait(dve, step, l)
                    for t in range(KT):
                        g = 48 + 4 * l + t if t < H else 56 + 4 * l + t - H
                        ins = v.scalar_tensor_tensor(out=XTl[s][:, t, :], in0=tiles(2 * s + t // 4)[:, t % 4, :],
                                                     scalar=colsB[:, g:g + 1],
                                                     in1=XTh[s][:, t, :].bitcast(F32), op0=ALU.mult,
                                                     op1=ALU.subtract)
                dve_st.done(ins, "yl", l)
                split(5)
                act_st.wait(dve, "gb1", l)
                residual([(s, c, 2 * c + s) for c in range(2) for s in range(S)], 
                         lambda s, c: through("out", l, c), "x1", l)
                norm(2, l)
                if l == 0:
                    ffn_dve(lambda h: split(h >= EARLY[2, 0]), PACE_DENSE, S, 0, ffn_first, silu_d, act_d, hTh_d, hTl_d,
                            (ffn_silu, ffn_prod, ffn_tr, ffn_hTh, ffn_hTl))
                    act_st.wait(dve, "gb2", l)
                    residual([(s, c, 2 * s + c) for s in range(S) for c in range(2)], 
                             lambda s, c: ffn_first + HALVES_FFN, "x2", l)

            pe_st.wait(dve, "xt2", 1)
            v.memset(N1[:, :, :], 0.0)
            def split_job(i, h):
                dve.wait_ge(hi_done, i * HALVES_FFN + (n_static_halves + h + 1))
                q = h % HLS_MOE
                v.tensor_tensor(lo[q][:, :], raw[RAW_MOE_SLOT[h // 2]][:, h % 2 * HALF:(h % 2 + 1) * HALF],
                                hi[q][:, :].bitcast(F32), ALU.subtract).then_inc(lo_done, 1)

            for h in range(PRE):
                split_job(0, h)
            act_st.wait(dve, "nath", 1)
            for s in range(S):
                for k in range(2):
                    c = slice(k * BLK, (k + 1) * BLK)
                    ins = v.tensor_tensor(natl[:, s, c], bank(2 * s + k), nath[:, s, c].bitcast(F32), ALU.subtract)
            dve_st.done(ins, "natl", 1)
            pe_st.wait(dve, "router", 1)
            link(v.tensor_copy(lg[:, :, :], bank(4)[:, 0:S * NE].rearrange("p (s e) -> p s e", s=S)))
            for s in range(S):
                link(v.max(mx[:, s, :], lg[:, s, :]))
                link(v.max_index(mi[:, s, :], mx[:, s, :], lg[:, s, :]))
            v.tensor_copy(mif[:, :, :], mi[:, :, 0:2])
            ins = v.tensor_tensor(wts[:, 0, :], mx[:, :, 1], mx[:, :, 0], ALU.subtract)
            dve_st.done(ins, "top", 1)
            dve_st.wait(dve, "top", 1)
            for s in range(S):
                for t, k in ((M1, 0), (M2, 1)):
                    ins = v.tensor_scalar(t[:, s, :], cst[:, C_IOTA:C_IOTA + NE], mif[:, s, k:k + 1], None,
                                          ALU.is_equal)
            link(ins)
            dve_st.done(v.tensor_tensor(MK[:, :, :], M1[:, :, :], M2[:, :, :], ALU.add), "masks", 1)
            act_st.wait(dve, "we", 1)
            link(v.tensor_scalar(wts[:, 0, :], wts[:, 1, :], 1.0, None, ALU.add))
            link(v.reciprocal(wts[:, 0, :], wts[:, 0, :]))
            link(v.tensor_tensor(wts[:, 1, :], wts[:, 1, :], wts[:, 0, :], ALU.mult))
            dve.wait_ge(st_out, 16 * 8)
            pe_st.wait(dve, "rank", 1)
            link(v.tensor_scalar(nb[:, :], bank(5)[:, 16:24], float(P), 1.0, ALU.is_gt, ALU.add))
            link(v.tensor_tensor_scan(st_i[:, :], cst[:, C_ONES:C_ONES + NE], nb[:, :], 0.0, ALU.mult, ALU.add))
            link(v.tensor_copy(jtf[:, MAX_JOBS:MAX_JOBS + 1], st_i[0:1, NE - 1:NE]))
            link(v.tensor_tensor(st_i[:, :], st_i[:, :], nb[:, :], ALU.subtract))
            link(v.tensor_scalar(nb[:, :], st_i[:, :], float(P), -1.0, ALU.mult, ALU.add))
            for s in range(S):
                ins = v.tensor_tensor(slots[:, s, :], bank(5)[:, 8 * s:8 * s + 8], nb[:, :], ALU.add)
            link(ins)
            for k, t in enumerate((M1, M2)):
                link(v.tensor_tensor(stmp[:, :, :], t[:, :, :], slots[:, :, :], ALU.mult))
                link(v.tensor_reduce(keys[:, k, :], stmp[:, :, :], AX_X, ALU.add))
            starts = st_i[0:1, :].rearrange("p (o e) -> p o e", o=1).to_broadcast([1, MAX_JOBS, NE])
            number = cst[0:1, C_IOTA:C_IOTA + MAX_JOBS].rearrange("p (j o) -> p j o", o=1)
            link(v.tensor_tensor(jt[:, :, :], starts, number.to_broadcast([1, MAX_JOBS, NE]), ALU.is_le))
            link(v.tensor_reduce(jtf[:, 0:MAX_JOBS], jt[:, :, :], AX_X, ALU.add))
            link(v.tensor_scalar(jtf[:, 0:MAX_JOBS], jtf[:, 0:MAX_JOBS], 1.0, None, ALU.subtract))
            dve_st.done(v.tensor_copy(jti[:, :], jtf[:, :]), "route", 1)
            modulation(len(ADA_BATCHES) - 1)

            def select():
                for s in range(S):
                    v.tensor_scalar(P1[:, s, :], iota, keys[:, 0, s:s + 1], None, ALU.is_equal)
                    ins = v.tensor_scalar(P2[:, s, :], iota, keys[:, 1, s:s + 1], None, ALU.is_equal)
                ins.then_inc(sel_step, 1)

            def select_sum():
                v.tensor_tensor(Pr[:, :, :], P1[:, :, :], P2[:, :, :], ALU.add).then_inc(sel_ready, 1)
                v.tensor_scalar(keys[:, :, :], keys[:, :, :], float(P), None, ALU.subtract)\
                    .then_inc(key_step, 1)

            def gather_lo(n):
                for k in range(2):
                    dve.wait_ge(xh_ready, n * 2 + (k + 1))
                    v.tensor_tensor(XTl[0][:, 4 * k:4 * k + 4, :], tiles(6 + k),
                                    XTh[0][:, 4 * k:4 * k + 4, :].bitcast(F32), ALU.subtract)\
                        .then_inc(xl_ready, 1)

            def y_lo(n):
                dve.wait_ge(yh_ready, n * 2)
                for c in range(2):
                    cols = slice(c * BLK, (c + 1) * BLK)
                    v.scalar_tensor_tensor(out=yl[:, cols], in0=bank(2 + c), scalar=gs[:, 0:1],
                                           in1=yh[:, cols].bitcast(F32), op0=ALU.mult, op1=ALU.subtract)\
                        .then_inc(yl_ready, 1)

            def accumulate(n, s):
                for c in range(2):
                    dve.wait_ge(scat_mm[s][c], n)
                    v.tensor_tensor(N1[:, s, c * BLK:(c + 1) * BLK], bank(6 + c),
                                    N1[:, s, c * BLK:(c + 1) * BLK], ALU.add).then_inc(acc_done[s][c], 1)

            def job(i, first):
                def half(h):
                    if h >= first:
                        split_job(i, h)
                    if h == Y_AT + 1 and not isinstance(i, int):
                        y_lo(i)
                    for part in range(2):
                        if h == SCATTER_AFTER[part] + PACE_JOB[0] and not isinstance(i, int):
                            accumulate(i, part)
                    if h == PT_AFTER + PACE_JOB[0]:
                        dve.wait_ge(ptr_mm, i + 1)
                        v.tensor_copy(PT[:, :, :], bank(5)[:, 0:S * P].rearrange("p (s t) -> p s t", s=S))
                        v.tensor_copy(gs[:, :], bank(5)[:, S * P:S * P + 1]).then_inc(pt_ready, 1)
                        dve.wait_ge(key_step, i + 1)
                        select()
                        dve.wait_ge(sel_step, i + 2)
                        select_sum()
                    if h == GATHER_AFTER + PACE_JOB[0]:
                        gather_lo(i + 1)

                ffn_dve(half, PACE_JOB, 1, i, n_static_halves, silu_m, act_m, hTh_m, hTl_m,
                        (job_silu, job_prod, job_tr, job_hTh, job_hTl))

            select()
            dve.wait_ge(sel_step, 1)
            select_sum()
            gather_lo(0)
            job(0, PRE)
            jobs = dve.value_load(jti[0:1, MAX_JOBS:MAX_JOBS + 1], min_val=NE, max_val=NE + 3)
            with dve.Fori(1, jobs) as i:
                job(i, 0)
            y_lo(jobs)
            accumulate(jobs, 0)
            accumulate(jobs, 1)

            for s, step in enumerate(("x2a", "x2")):
                pe_st.wait(dve, "gb2" + "a" * (1 - s), 1)
                for c in range(2):
                    cols = slice(c * BLK, (c + 1) * BLK)
                    dve.wait_ge(acc_done[s][c], jobs)
                    ins = v.tensor_tensor(N1[:, s, cols], N1[:, s, cols], bank(4 * s + c), ALU.mult)
                link(ins)
                dve_st.done(v.tensor_tensor(x[:, s, :], x[:, s, :], N1[:, s, :], ALU.add), step, 1)
            act_st.wait(dve, "sqf")
            mean(1, D, "vf")
            act_st.wait(dve, "rsf")
            refine(1)
            dve.wait_ge(gfin_ld, 16)
            for s, step in enumerate(("yfa", "yf")):
                dve_st.done(v.scalar_tensor_tensor(out=yfin[:, s, :], in0=x[:, s, :], scalar=rs[:, s, 0:1],
                                                   in1=gfin[:, :], op0=ALU.mult, op1=ALU.mult), step)

        @block.tensor
        def _(pe):
            mm = nc.tensor.matmul
            pos = [0]

            def take():
                q = pos[0]
                pe.wait_ge(lo_done, q + 1)
                pos[0] += 1
                return q % HLS

            def product(out, xh, xl, q, cols, start, stop):
                mm(out, xh, hi[q][:, cols], start=start, stop=False)
                mm(out, xh, lo[q][:, cols], start=False, stop=False)
                return mm(out, xl, hi[q][:, cols], start=False, stop=stop)

            def turn(out, in_, n=P):
                return nc.tensor.transpose(out, in_, cst[0:n, C_ID:C_ID + n])

            def gate_tile(out, l, comp, s, t):
                return mm(out, modc[l][:, 8 * comp + t, s:s + 1].to_broadcast([P, P]), ident, start=True, stop=True)

            def gate_rows(name, l, comp):
                for s, step in enumerate((name + "a", name)):
                    if s:
                        act_st.wait(pe, name + "a", l)
                    for t in range(KT):
                        ins = gate_tile(tiles(4 + t // 4)[:, t % 4, :], l, comp, s, t)
                    pe_st.done(ins, step, l)

            def norm_turns(k, l):
                for s, stages in enumerate((dve_st, act_st)):
                    stages.wait(pe, f"xn{k}", l)
                    for t in range(KT):
                        ins = turn(tiles(2 * s + t // 4)[:, t % 4, :], N1[:, s, t * P:(t + 1) * P])
                    pe_st.done(ins, f"xt{k}" + "a" * (1 - s), l)

            def ffn_pe(take_half, pace, ns, i, xt, act_t, hTh, hTl, down_banks, sems, extra):
                silu_sem, prod, tr, hTl_sem = sems
                t_after = pace[1]

                def turns(j):
                    nt = 4 if j < 5 else 2
                    for s in range(ns):
                        pe.wait_ge(prod, i * (6 * ns) + (ns * j + s + 1))
                        if not (isinstance(i, int) and j == 0):
                            pe.wait_ge(hTl_sem, i * (6 * ns) + ns * j)
                        for t in range(nt):
                            ins = turn(tiles(4 + s)[:, t, :], act_t[:, s, t * P:(t + 1) * P])
                        ins.then_inc(tr, 1)

                for h in range(HALVES_FFN):
                    if h < 44:
                        j = h // 8 if h < 40 else 5
                        r, per, w = (h % 8, 4, BLK) if h < 40 else (h - 40, 2, F - 5 * BLK)
                        is_up, part = r // per, r % per
                        kts = KT // per
                        if part == 0 and not (isinstance(i, int) and j == 0):
                            pe.wait_ge(prod if is_up else silu_sem, i * (6 * ns) + ns * j)
                        q = take_half(h)
                        for s in range(ns):
                            out = bank(2 * s + is_up)[:, 0:w]
                            for k in range(kts):
                                kt = part * kts + k
                                ins = product(out, xt[s][0][:, kt, :], xt[s][1][:, kt, :], q,
                                              slice(k * w, (k + 1) * w), kt == 0, kt == KT - 1)
                        release(ins)
                    else:
                        t = h - 44
                        if t == 0:
                            extra("down")
                        if t % 4 == 0:
                            pe.wait_ge(hTl_sem, i * (6 * ns) + ns * (t // 4 + 1))
                        q = take_half(h)
                        for s in range(ns):
                            for c in range(2):
                                ins = product(bank(down_banks[2 * s + c]), hTh[:, t, s, :], hTl[:, t, s, :], q,
                                              slice(c * BLK, (c + 1) * BLK), t == 0, t == FT - 1)
                        release(ins)
                    for j in range(6):
                        if h == t_after[j]:
                            turns(j)
                    extra(h)

            def release(ins):
                ins.then_inc(w_used, 1)

            pe.wait_ge(cond_ld, 16 * 9)
            turn(bank(4)[:, 0:96], rowsA[:, :], 96)
            pe_st.done(turn(bank(5)[:, 0:80], rowsB[:, :], 80), "cols")
            dve_st.wait(pe, "cond")
            ada_at = [0]
            ada_unit = [n for n, u in enumerate(units) if u[0] == "ada"]

            def fill(step, l):
                for _ in range(ADA_FILL.get((step, l), 0)):
                    k, kt = divmod(ada_at[0], KT)
                    batch = max(m for m, first in enumerate(ADA_AT) if first <= k)
                    j = k - ADA_AT[batch]
                    u = ada_unit[2 * k + kt // 4]
                    if batch and j == kt == 0:
                        pe.wait_ge(ada_cols, batch)
                    if kt % 4 == 0:
                        pe.wait_ge(raw_ld[u % RAW], 16 * (u // RAW + 1))
                    c0 = ADA_W - S - S * j
                    ins = mm(bank(7)[0:ADA_W, :], cond[:, kt, c0:c0 + ADA_W],
                             raw[u % RAW][:, kt % 4 * BLK:(kt % 4 + 1) * BLK],
                             start=(j == kt == 0), stop=(j == ADA_BATCHES[batch] - 1 and kt == KT - 1))
                    if kt % 4 == 3:
                        ins.then_inc(ada_sum, 1)
                    ada_at[0] += 1

            def ada_turns(batch):
                pe.wait_ge(ada_rows, batch + 1)
                for t in range(4):
                    ins = turn(bank(7)[:, t * ADA_W:(t + 1) * ADA_W], adarow[:, t * P:(t + 1) * P], ADA_W)
                ins.then_inc(ada_turned, 1)

            fill("first", 0)
            for l in range(DEPTH):
                if l:
                    dve_st.wait(pe, "x2", l - 1)
                norm_turns(1, l)
                ada_turns(3 * l)
                fill("xt1", l)
                q = take()
                for s, step in enumerate(("xl1a", "xl1")):
                    dve_st.wait(pe, step, l)
                    for kt in range(KT):
                        cols = slice(kt * GATES, (kt + 1) * GATES)
                        out = tiles(4)[0:GATES, s, :]
                        mm(out, hi[q][:, cols], XTh[s][:, kt, :], start=(kt == 0), stop=False)
                        mm(out, lo[q][:, cols], XTh[s][:, kt, :], start=False, stop=False)
                        ins = mm(out, hi[q][:, cols], XTl[s][:, kt, :], start=False, stop=(kt == KT - 1))
                release(ins)
                for b in range(8):
                    n = 8 * l + b
                    if n >= 2:
                        pe.wait_ge(in_evA, n - 1)
                        pe.wait_ge(in_evD, n - 1)
                    for k in range(4):
                        q = take()
                        for s in range(S):
                            for t in range(2):
                                kt = 2 * k + t
                                ins = product(bank(b % 2 * 2 + s), XTh[s][:, kt, :], XTl[s][:, kt, :], q,
                                              slice(t * BLK, (t + 1) * BLK), kt == 0, kt == KT - 1)
                        release(ins)
                        if b == 0 and k == 1:
                            act_st.wait(pe, "gate_r", l)
                            for s in range(S):
                                ins = turn(bank(4)[:, s * GATES:(s + 1) * GATES], rows[:, s, :], GATES)
                            pe_st.done(ins, "gate_t", l)
                    if b == 1:
                        dve_st.wait(pe, "fl", l)
                        for d, tri in enumerate((trif, trib)):
                            ins = mm(bank(5)[:, 8 * d:8 * d + 8], tri, FL[:, d, :, :], start=True, stop=True)
                        pe_st.done(ins, "bcum", l)
                    if b == 3:
                        dve_st.wait(pe, "ba", l)
                        for d in range(2):
                            ins = turn(bank(5)[0:2 * H, d * P:(d + 1) * P],
                                       Ac[:, d, :, :].rearrange("p s h -> p (s h)"))
                        pe_st.done(ins, "arow", l)
                    if b == 5:
                        dve_st.wait(pe, "mr", l)
                        for d in range(2):
                            ins = turn(bank(5)[:, 8 * d:8 * d + 8], MR[:, d, :], 2 * H)
                        pe_st.done(ins, "mcol", l)

                pe.wait_ge(in_evA, 8 * l + 8)
                pe.wait_ge(in_evD, 8 * l + 8)
                pe.wait_ge(state_ld, 32 * (l + 1))

                def head(s, c0, h):
                    return p[:, s, c0 + h * P:c0 + (h + 1) * P]

                def turn_qk(s, qc, kc, name):
                    for bk, c0 in ((2, qc), (3, kc)):
                        for h in range(H):
                            ins = turn(tiles(bk)[:, h, :], head(s, c0, h))
                    pe_st.done(ins, name, l)
                    fill(name, l)

                def scores(name):
                    for h in range(H):
                        ins = mm(tiles(4)[:, h, :], KTt[:, h, :], QT[:, h, :], start=True, stop=True)
                    pe_st.done(ins, name, l)
                    fill(name, l)

                for s in range(S):
                    if s:
                        dve_st.wait(pe, "qtr0", l)
                    turn_qk(s, QM, KM, f"qk{s}")
                    dve_st.wait(pe, "mc", l)
                    if s:
                        act_st.wait(pe, "rstc", l)
                    for d in range(2):
                        mm(bank(d), identb[:, :],
                           negm[:, d:d + 1, :].to_broadcast([P, H, P]), start=True, stop=True)
                        for h in range(H):
                            r = s * H + h
                            ins = mm(tiles(d)[:, h, :], cst[0:2 * H, C_ID + r:C_ID + r + 1].to_broadcast([2 * H, P]),
                                     nMR[:, d, :], start=False, stop=True, skip_group_check=True)
                    pe_st.done(ins, f"mb{s}", l)
                    fill(f"mb{s}", l)
                    act_st.wait(pe, f"kt{s}", l)
                    dve_st.wait(pe, f"qt{s}", l)
                    if s:
                        dve_st.wait(pe, "nr", l)
                    scores(f"pqk{s}")
                    dve_st.wait(pe, f"st{s}", l)
                    for d in range(2):
                        for h in range(H):
                            c0 = C_UNIT + 2 * H - 1 - (H * d + h)
                            ins = mm(tiles(4)[0:2 * H, 0, :], cst[:, c0:c0 + 2 * H], ST[:, d, h, :],
                                     start=(d == h == 0), stop=(d == 1 and h == H - 1))
                    if s == 1:
                        n0_l = n0[:, l, :, :].rearrange("p h c -> p (h c)")
                        for h in range(H):
                            ins = mm(tiles(4)[0:2 * H, 1, :], n0_l[:, 8 * h:8 * h + 2 * H], QT[:, h, :],
                                     start=(h == 0), stop=(h == H - 1))
                    pe_st.done(ins, f"den{s}", l)
                    for d in range(2):
                        for h in range(H):
                            mm(tiles(5 + d)[:, h, :], ST[:, d, h, :], head(s, VM, h), start=True, stop=True)
                    act_st.wait(pe, f"den{s}", l)
                    for k in range(s + 1):
                        ins = turn(bank(4)[:, 2 * H * k:2 * H * (k + 1)], rows[0:2 * H, k, :], 2 * H)
                    pe_st.done(ins, f"num{s}", l)
                    fill(f"num{s}", l)
                    if s == 0:
                        dve_st.wait(pe, "vw", l)
                        act_st.wait(pe, "et0", l)
                        for d in range(2):
                            for h in range(H):
                                ins = mm(tiles(d)[:, h, :], head(0, KM, h), VW[:, d, h, :], start=True, stop=True)
                        pe_st.done(ins, "cst", l)
                        fill("cst", l)
                    else:
                        act_st.wait(pe, "et1", l)
                        for d in range(2):
                            for h in range(H):
                                ins = mm(tiles(d)[:, h, :], QT[:, h, :], CM[:, d, h, :], start=True, stop=True)
                        pe_st.done(ins, "cq1", l)
                        dve_st.wait(pe, "rope", l)
                    turn_qk(s, QR, KR, f"qkr{s}")
                    act_st.wait(pe, f"ktr{s}", l)
                    dve_st.wait(pe, f"qtr{s}", l)
                    scores(f"pr{s}")
                    dve_st.wait(pe, f"str{s}", l)
                    for h in range(H):
                        ins = mm(tiles(5)[:, h, :], ST[:, 0, h, :], head(s, VR, h), start=True, stop=True)
                    if s == 1:
                        for d, bk in ((0, 6), (1, 2)):
                            for h in range(H):
                                ins = mm(tiles(bk)[:, h, :], QT[:, h, :], SM[:, d, h, :], start=True, stop=True)
                    pe_st.done(ins, f"o{s}", l)
                    fill(f"o{s}", l)
                    if s == 0:
                        wn_h = wn[:, :, :].rearrange("p h c -> p (h c)")
                        for h in range(H):
                            ins = mm(bank(4)[0:2 * H, 0:P], wn_h[:, 8 * h:8 * h + 2 * H], head(0, KM, h),
                                     start=(h == 0), stop=(h == H - 1))
                        pe_st.done(ins, "nst", l)
                        act_st.wait(pe, "stc", l)
                        dve_st.wait(pe, "vwr", l)
                        for d in range(2):
                            for h in range(H):
                                ins = mm(tiles(d)[:, h, :], head(0, KR, h), VW[:, d, h, :], start=True, stop=True)
                        pe_st.done(ins, "rst", l)
                        fill("rst", l)

                ada_turns(3 * l + 1)
                dve_st.wait(pe, "yr1", l)
                pe.wait_ge(ada_cols, 3 * l + 2)
                gate_rows("gb1", l, 2)
                fill("gb1", l)
                dve_st.wait(pe, "yn", l)
                for s in range(S):
                    for t in range(KT):
                        ins = turn(tiles(2 * s + t // 4)[:, t % 4, :], yy[:, s, t, :])
                pe_st.done(ins, "yt", l)
                fill("yt", l)
                dve_st.wait(pe, "yl", l)
                for b in range(2):
                    for k in range(4):
                        q = take()
                        for s in range(S):
                            for t in range(2):
                                kt = 2 * k + t
                                ins = product(bank(2 * b + s), XTh[s][:, kt, :], XTl[s][:, kt, :], q,
                                              slice(t * BLK, (t + 1) * BLK), kt == 0, kt == KT - 1)
                        release(ins)
                fill("x1", l)
                norm_turns(2, l)
                ada_turns(3 * l + 2)
                fill("xt2", l)
                if l == 0:
                    pe.wait_ge(ada_cols, 3 * l + 3)
                    gate_rows("gb2", l, 5)
                    fill("gb2", l)
                    dve_st.wait(pe, "xl2", l)
                    act_st.wait(pe, "gb2", l)

                    def dense_extra(h):
                        if h == "down":
                            pe.wait_ge(ffn_prod, 12)
                        elif h % 2:
                            fill(f"ffn{h // 2}", l)

                    ffn_pe(lambda h: take(), PACE_DENSE, S, 0, list(zip(XTh, XTl)), act_d, hTh_d, hTl_d, (0, 1, 2, 3),
                           (ffn_silu, ffn_prod, ffn_tr, ffn_hTl), dense_extra)
                    fill("x2", l)

            dve_st.wait(pe, "h2a", 1)
            act_st.wait(pe, "h2", 1)
            for s in range(S):
                for kt in range(KT):
                    ins = mm(bank(4)[:, NE * s:NE * s + NE], N2[:, s, kt, :], wr[:, kt, :],
                             start=(kt == 0), stop=(kt == KT - 1))
            pe_st.done(ins, "router", 1)
            for s in range(S):
                for t in range(KT):
                    ins = turn(tiles(2 * s + t // 4)[:, t % 4, :], N2[:, s, t, :])
            pe_st.done(ins, "nat", 1)
            fill("nat", 1)
            dve_st.wait(pe, "masks", 1)
            mm(bank(5)[:, 0:8], trif, MK[:, 0, :], start=True, stop=True)
            mm(bank(5)[:, 8:16], trif, MK[:, 1, :], start=True, stop=False)
            mm(bank(5)[:, 8:16], ones, MK[:, 0, :], start=False, stop=True)
            mm(bank(5)[:, 16:24], ones, MK[:, 0, :], start=True, stop=False)
            pe_st.done(mm(bank(5)[:, 16:24], ones, MK[:, 1, :], start=False, stop=True), "rank", 1)
            fill("rank", 1)
            ada_turns(len(ADA_BATCHES) - 1)

            def gather(n):
                pe.wait_ge(sel_ready, n + 1)
                for t in range(KT):
                    out = tiles(6 + t // 4)[:, t % 4, :]
                    for s in range(S):
                        mm(out, nath[:, s, t * P:(t + 1) * P], Pr[:, s, :], start=(s == 0), stop=False)
                        ins = mm(out, natl[:, s, t * P:(t + 1) * P], Pr[:, s, :], start=False, stop=(s == S - 1))
                    if t % 4 == 3:
                        ins.then_inc(gath_mm, 1)

            def scatter(n, s):
                pe.wait_ge(yl_ready, n * 2)
                for c in range(2):
                    if s:
                        pe.wait_ge(acc_done[0][c], n)
                    cols = slice(c * BLK, (c + 1) * BLK)
                    mm(bank(6 + c), PT[:, s, :], yh[:, cols], start=True, stop=False)
                    mm(bank(6 + c), PT[:, s, :], yl[:, cols], start=False, stop=True)\
                        .then_inc(scat_mm[s][c], 1)

            dve_st.wait(pe, "natl", 1)
            gather(0)
            def job(i):
                def take_job(h):
                    if h in (0, 2):
                        pe.wait_ge(xl_ready, i * 2 + (h // 2 + 1))
                    pe.wait_ge(lo_done, i * HALVES_FFN + (n_static_halves + h + 1))
                    return h % HLS_MOE

                def job_extra(h):
                    for part in range(2):
                        if h == SCATTER_AFTER[part] and not isinstance(i, int):
                            scatter(i, part)
                    if h == PT_AFTER:
                        pe.wait_ge(sel_ready, i + 1)
                        for s in range(S):
                            out = bank(5)[:, s * P:(s + 1) * P]
                            mm(out, P1[:, s, :], ident, start=True, stop=False)
                            mm(out, P2[:, s, :], ident, start=False, stop=True)
                        out = bank(5)[:, S * P:S * P + 1]
                        for n, (sel, k, s) in enumerate(((P1, 0, 0), (P1, 0, 1), (P2, 1, 0), (P2, 1, 1))):
                            ins = mm(out, sel[:, s, :], wts[:, k, s:s + 1], start=(n == 0), stop=(n == 3))
                        ins.then_inc(ptr_mm, 1)
                    if h == GATHER_AFTER:
                        if not isinstance(i, int):
                            for c in range(2):
                                pe.wait_ge(acc_done[1][c], i)
                        gather(i + 1)

                ffn_pe(take_job, PACE_JOB, 1, i, [(XTh[0], XTl[0])], act_m, hTh_m, hTl_m, (2, 3),
                       (job_silu, job_prod, job_tr, job_hTl), job_extra)

            job(0)
            jobs = pe.value_load(jti[0:1, MAX_JOBS:MAX_JOBS + 1], min_val=NE, max_val=NE + 3)
            with pe.Fori(1, jobs) as i:
                job(i)
            pe.wait_ge(job_prod, jobs * 6)
            pe.wait_ge(job_hTl, jobs * 6)
            pe.wait_ge(pt_ready, jobs)
            for s, step in enumerate(("gb2a", "gb2")):
                for t in range(KT):
                    ins = gate_tile(tiles(4 * s + t // 4)[:, t % 4, :], 1, 5, s, t)
                pe_st.done(ins, step, 1)
            scatter(jobs, 0)
            scatter(jobs, 1)


_INS = ["x_prompt", "x_sample", "state_mlstm_C", "state_mlstm_n", "state_mlstm_m", "state_ret_S", "c", "c_ctx",
        "norm1_g", "norm2_g", "norm_f_g", "w_ada", "b_ada", "w_in", "b_gates", "ret_decay_logit",
        "mlstm_norm_g", "ret_norm_g", "w_out", "ffn_w_gate", "ffn_w_up", "ffn_w_down",
        "moe_w_router", "moe_w_gate", "moe_w_up", "moe_w_down"]
_OUTS = {"y_prompt": (1, P, D), "y_sample": (1, P, D), "new_C": (1, DEPTH, 2, H, P, P),
         "new_n": (1, DEPTH, 2, H, P), "new_m": (1, DEPTH, 2, H), "new_S": (1, DEPTH, 2, H, P, P)}


def kernel(**inputs):
    import concourse.bacc as bacc
    from concourse.bass_utils import run_bass_kernel_spmd

    nc = bacc.Bacc("TRN2", target_bir_lowering=False, num_devices=1)
    arrays = {name: np.ascontiguousarray(inputs[name]) for name in _INS}
    arrays["consts"] = shape_constants()
    a = {n: nc.dram_tensor(n, v.shape, mybir.dt.from_np(v.dtype), kind="ExternalInput").ap()
         for n, v in arrays.items()}
    o = {n: nc.dram_tensor(n, shape, F32, kind="ExternalOutput").ap() for n, shape in _OUTS.items()}
    bass_hybrid_backbone(nc, a, o)
    got = run_bass_kernel_spmd(nc, [arrays], core_ids=[0]).results[0]
    return tuple(got[n] for n in _OUTS)
```
